# Optimizing a Trainium2 kernel written in Bass

```python
import math
import jax, jax.numpy as jnp
from jax import lax
import numpy as np

D_MODEL = 1024
BATCH = 1
SEQ = 256
DEPTH = 1

PLE_DIM = 256
HEAD_DIM = 64
D_MIX = D_MODEL
SB_HEADS = D_MIX // 2 // HEAD_DIM
RET_HEADS = D_MIX // 2 // HEAD_DIM
SB_WIDTH = SB_HEADS * HEAD_DIM
RET_WIDTH = RET_HEADS * HEAD_DIM
D_IN = 3 * SB_WIDTH + 4 * RET_WIDTH
Q_BLOCK = 128
RET_CHUNK = 128
ROPE_BASE = 10000.0
N_EXPERTS = 32
TOP_K = 4
D_EXPERT = D_MODEL
SWIGLU_LIMIT = 7.0
SWIGLU_ALPHA = 1.702
MOE_BLOCK = 128
EPS = 1e-6


def _rmsnorm(x, g):
    xf = x.astype(jnp.float32)
    y = xf * lax.rsqrt(jnp.mean(xf * xf, axis=-1, keepdims=True) + EPS)
    return (y * g.astype(jnp.float32)).astype(x.dtype)

def _heads(t, n_heads):
    b, s, _ = t.shape
    return t.reshape(b, s, n_heads, HEAD_DIM).transpose(0, 2, 1, 3)

def _rope(t, positions):
    half = HEAD_DIM // 2
    inv_freq = ROPE_BASE ** (-jnp.arange(half, dtype=jnp.float32) / half)
    ang = positions.astype(jnp.float32)[:, None, :, None] * inv_freq
    cos, sin = jnp.cos(ang), jnp.sin(ang)
    tf = t.astype(jnp.float32)
    t1, t2 = tf[..., :half], tf[..., half:]
    return jnp.concatenate([t1 * cos - t2 * sin, t2 * cos + t1 * sin], axis=-1).astype(t.dtype)

def _stick_breaking(q, k, v):
    b, h, s, d = q.shape
    nqb = s // Q_BLOCK
    scale = 1.0 / math.sqrt(d)
    qs = q.reshape(b, h, nqb, Q_BLOCK, d).transpose(2, 0, 1, 3, 4)
    t0s = jnp.arange(nqb, dtype=jnp.int32) * Q_BLOCK
    kpos = jnp.arange(s, dtype=jnp.int32)

    def block(args):
        qb, t0 = args
        z = jnp.einsum('bhqd,bhkd->bhqk', qb, k).astype(jnp.float32) * scale
        qpos = t0 + jnp.arange(Q_BLOCK, dtype=jnp.int32)
        mask = kpos[None, :] < qpos[:, None]
        lneg = jnp.where(mask, jax.nn.log_sigmoid(-z), 0.0)
        tail = lax.cumsum(lneg, axis=3, reverse=True) - lneg
        w = jnp.where(mask, jnp.exp(jax.nn.log_sigmoid(z) + tail), 0.0)
        return jnp.einsum('bhqk,bhkd->bhqd', w.astype(v.dtype), v)

    out = lax.map(block, (qs, t0s))
    return out.transpose(1, 2, 0, 3, 4).reshape(b, h, s, d)

def _retention(q, k, v):
    b, h, s, d = q.shape
    n = s // RET_CHUNK
    c = RET_CHUNK
    log_g = jnp.log(1.0 - 2.0 ** (-5.0 - jnp.arange(h, dtype=jnp.float32)))
    idx = jnp.arange(c, dtype=jnp.float32)
    diff = idx[:, None] - idx[None, :]
    dmat = jnp.where(diff >= 0, jnp.exp(log_g[:, None, None] * jnp.maximum(diff, 0.0)), 0.0)
    k_dec = jnp.exp(log_g[:, None] * (c - 1 - idx)[None, :])
    q_dec = jnp.exp(log_g[:, None] * (idx + 1.0)[None, :])
    g_chunk = jnp.exp(log_g * c)
    qc = q.reshape(b, h, n, c, d)
    kc = k.reshape(b, h, n, c, d)
    vc = v.reshape(b, h, n, c, d)
    dt = q.dtype
    scores = jnp.einsum('bhnid,bhnjd->bhnij', qc, kc) * dmat[None, :, None].astype(dt)
    inner = jnp.einsum('bhnij,bhnjd->bhnid', scores, vc)
    kv = jnp.einsum('bhnjd,bhnje->bhnde', kc * k_dec[None, :, None, :, None].astype(dt), vc)

    def step(state, kv_n):
        return g_chunk[:, None, None].astype(state.dtype) * state + kv_n, state

    init = jnp.zeros((b, h, d, d), dtype=kv.dtype)
    _, prev = lax.scan(step, init, jnp.moveaxis(kv, 2, 0))
    prev = jnp.moveaxis(prev, 0, 2)
    cross = jnp.einsum('bhnid,bhnde->bhnie', qc, prev) * q_dec[None, :, None, :, None].astype(dt)
    return (inner + cross).reshape(b, h, s, d)

def _group_norm(y, gain, bias):
    yf = y.astype(jnp.float32)
    mu = jnp.mean(yf, axis=-1, keepdims=True)
    var = jnp.mean((yf - mu) ** 2, axis=-1, keepdims=True)
    yn = (yf - mu) * lax.rsqrt(var + EPS)
    b, h, s, d = y.shape
    yn = yn.transpose(0, 2, 1, 3).reshape(b, s, h * d)
    return (yn * gain.astype(jnp.float32) + bias.astype(jnp.float32)).astype(y.dtype)

def _moe(xt, w_router, b_router, w_up_gate, b_up_gate, w_down, b_down):
    t, d = xt.shape
    logits = (xt @ w_router + b_router).astype(jnp.float32)
    top_vals, top_idx = lax.top_k(logits, TOP_K)
    gates = jax.nn.softmax(top_vals, axis=-1)
    a = t * TOP_K
    flat_e = top_idx.reshape(a).astype(jnp.int32)
    flat_tok = jnp.arange(a, dtype=jnp.int32) // TOP_K
    flat_gate = gates.reshape(a)
    order = jnp.argsort(flat_e)
    sorted_e = flat_e[order]
    counts = jnp.zeros((N_EXPERTS,), jnp.int32).at[flat_e].add(1)
    padded = ((counts + MOE_BLOCK - 1) // MOE_BLOCK) * MOE_BLOCK
    pad_end = jnp.cumsum(padded)
    pad_start = pad_end - padded
    start = jnp.cumsum(counts) - counts
    rank = jnp.arange(a, dtype=jnp.int32) - start[sorted_e]
    dest = pad_start[sorted_e] + rank
    n_slots = a + N_EXPERTS * MOE_BLOCK
    n_blocks = n_slots // MOE_BLOCK
    slot_tok = jnp.zeros((n_slots,), jnp.int32).at[dest].set(flat_tok[order])
    slot_gate = jnp.zeros((n_slots,), jnp.float32).at[dest].set(flat_gate[order])
    block_e = jnp.clip(jnp.searchsorted(pad_end, jnp.arange(n_blocks, dtype=jnp.int32) * MOE_BLOCK, side='right'), 0, N_EXPERTS - 1)
    xs = xt[slot_tok].reshape(n_blocks, MOE_BLOCK, d)

    def expert_block(args):
        xb, e = args
        hgu = xb @ w_up_gate[e] + b_up_gate[e]
        x_glu = jnp.minimum(hgu[:, :D_EXPERT], SWIGLU_LIMIT)
        x_lin = jnp.clip(hgu[:, D_EXPERT:], -SWIGLU_LIMIT, SWIGLU_LIMIT)
        hact = x_glu * jax.nn.sigmoid(SWIGLU_ALPHA * x_glu) * (x_lin + 1.0)
        return hact @ w_down[e] + b_down[e]

    ys = lax.map(expert_block, (xs, block_e)).reshape(n_slots, d)
    return jnp.zeros((t, d), xt.dtype).at[slot_tok].add(ys * slot_gate[:, None].astype(xt.dtype))

def first_inputs(seed: int = 0) -> dict:
    key = jax.random.key(seed)
    ks = jax.random.split(key, 24)
    nrm = lambda k, shape, s: jax.random.normal(k, shape, jnp.float32) * s
    L = DEPTH
    return {
        "x": nrm(ks[0], (BATCH, SEQ, D_MODEL), 1.0),
        "p": nrm(ks[1], (DEPTH, BATCH, SEQ, PLE_DIM), 1.0),
        "positions": jnp.broadcast_to(jnp.arange(SEQ, dtype=jnp.int32), (BATCH, SEQ)),
        "g_mix_norm": 1.0 + nrm(ks[2], (L, D_MODEL), 0.02),
        "w_in": nrm(ks[3], (L, D_MODEL, D_IN), D_MODEL ** -0.5),
        "sb_q_gain": 1.0 + nrm(ks[4], (L, HEAD_DIM), 0.02),
        "sb_k_gain": 1.0 + nrm(ks[5], (L, HEAD_DIM), 0.02),
        "ret_q_gain": 1.0 + nrm(ks[6], (L, HEAD_DIM), 0.02),
        "ret_k_gain": 1.0 + nrm(ks[7], (L, HEAD_DIM), 0.02),
        "ret_gn_gain": 1.0 + nrm(ks[8], (L, RET_WIDTH), 0.02),
        "ret_gn_bias": nrm(ks[9], (L, RET_WIDTH), 0.02),
        "w_out": nrm(ks[10], (L, D_MIX, D_MODEL), D_MIX ** -0.5),
        "g_ffn_norm": 1.0 + nrm(ks[11], (L, D_MODEL), 0.02),
        "w_router": nrm(ks[12], (L, D_MODEL, N_EXPERTS), D_MODEL ** -0.5),
        "b_router": nrm(ks[13], (L, N_EXPERTS), 0.01),
        "w_up_gate": nrm(ks[14], (L, N_EXPERTS, D_MODEL, 2 * D_EXPERT), D_MODEL ** -0.5),
        "b_up_gate": nrm(ks[15], (L, N_EXPERTS, 2 * D_EXPERT), 0.02),
        "w_down": nrm(ks[16], (L, N_EXPERTS, D_EXPERT, D_MODEL), D_EXPERT ** -0.5),
        "b_down": nrm(ks[17], (L, N_EXPERTS, D_MODEL), 0.02),
        "g_ple_norm": 1.0 + nrm(ks[18], (L, D_MODEL), 0.02),
        "w_ple_gate": nrm(ks[19], (L, D_MODEL, D_MODEL), D_MODEL ** -0.5),
        "w_ple_proj": nrm(ks[20], (L, PLE_DIM, D_MODEL), PLE_DIM ** -0.5),
    }

def first_block(x, p, positions, g_mix_norm, w_in, sb_q_gain, sb_k_gain, ret_q_gain, ret_k_gain,
              ret_gn_gain, ret_gn_bias, w_out, g_ffn_norm, w_router, b_router, w_up_gate, b_up_gate,
              w_down, b_down, g_ple_norm, w_ple_gate, w_ple_proj):
    b, s, d = x.shape
    for i in range(DEPTH):
        xn = _rmsnorm(x, g_mix_norm[i])
        proj = xn @ w_in[i]
        o = 0
        sb_q = proj[..., o:o + SB_WIDTH]; o += SB_WIDTH
        sb_k = proj[..., o:o + SB_WIDTH]; o += SB_WIDTH
        sb_v = proj[..., o:o + SB_WIDTH]; o += SB_WIDTH
        r_q = proj[..., o:o + RET_WIDTH]; o += RET_WIDTH
        r_k = proj[..., o:o + RET_WIDTH]; o += RET_WIDTH
        r_v = proj[..., o:o + RET_WIDTH]; o += RET_WIDTH
        r_g = proj[..., o:o + RET_WIDTH]
        q_a = _rmsnorm(_heads(sb_q, SB_HEADS), sb_q_gain[i])
        k_a = _rmsnorm(_heads(sb_k, SB_HEADS), sb_k_gain[i])
        y_a = _stick_breaking(q_a, k_a, _heads(sb_v, SB_HEADS))
        y_a = y_a.transpose(0, 2, 1, 3).reshape(b, s, SB_WIDTH)
        q_b = _rope(_rmsnorm(_heads(r_q, RET_HEADS), ret_q_gain[i]), positions)
        k_b = _rope(_rmsnorm(_heads(r_k, RET_HEADS), ret_k_gain[i]), positions) * (HEAD_DIM ** -0.5)
        y_b = _retention(q_b, k_b, _heads(r_v, RET_HEADS))
        y_b = _group_norm(y_b, ret_gn_gain[i], ret_gn_bias[i]) * jax.nn.silu(r_g)
        x = x + jnp.concatenate([y_a, y_b], axis=-1) @ w_out[i]
        hn = _rmsnorm(x, g_ffn_norm[i]).reshape(b * s, d)
        x = x + _moe(hn, w_router[i], b_router[i], w_up_gate[i], b_up_gate[i], w_down[i], b_down[i]).reshape(b, s, d)
        gate = jax.nn.sigmoid(_rmsnorm(x, g_ple_norm[i]) @ w_ple_gate[i])
        x = x + (p[i] @ w_ple_proj[i]) * gate
    return x


DEPTH_2 = 2

CHUNK = 64
N_MIXERS = 2
N_LAYERS_A = (DEPTH_2 + 1) // 2
N_LAYERS_B = DEPTH_2 // 2
SGU_BLOCK = 128
SGU_WIDTH = 2 * D_MODEL
SGU_GROUPS = 16
SGU_GROUP_DIM = SGU_WIDTH // SGU_GROUPS
RWKV_HEAD_DIM = 64
RWKV_HEADS = D_MODEL // RWKV_HEAD_DIM
DECAY_LORA = 64
AAA_LORA = 64
MV_LORA = 32
GATE_LORA = 128
FFN_HIDDEN = 4 * D_MODEL
RMS_EPS = 1e-6
LN_EPS = 1e-5
GN_EPS = 64e-5


def _rmsnorm_2(x, g):
    xf = x.astype(jnp.float32)
    y = xf * lax.rsqrt(jnp.mean(xf * xf, axis=-1, keepdims=True) + RMS_EPS)
    return (y * g.astype(jnp.float32)).astype(x.dtype)

def _layernorm(x, g, b, eps):
    xf = x.astype(jnp.float32)
    mu = jnp.mean(xf, axis=-1, keepdims=True)
    var = jnp.mean(jnp.square(xf - mu), axis=-1, keepdims=True)
    y = (xf - mu) * lax.rsqrt(var + eps)
    return (y * g.astype(jnp.float32) + b.astype(jnp.float32)).astype(x.dtype)

def _sgu_mask():
    chunk_id = jnp.arange(SGU_BLOCK) // CHUNK
    return chunk_id[None, :] <= chunk_id[:, None]

def _spatial_gating_mixer(h, w_in, b_in, ln_g, ln_b, w_s, b_s, w_out):
    bsz, seq, _ = h.shape
    z = jax.nn.gelu(h @ w_in + b_in, approximate=False)
    u, v = jnp.split(z, 2, axis=-1)
    v = _layernorm(v, ln_g, ln_b, LN_EPS)
    v = v.reshape(bsz, seq // SGU_BLOCK, SGU_BLOCK, SGU_GROUPS, SGU_GROUP_DIM)
    w_s = w_s * _sgu_mask()[None].astype(w_s.dtype)
    s = jnp.einsum('gij,bnjgc->bnigc', w_s, v) + b_s.T[None, None, :, :, None]
    y = u * s.reshape(bsz, seq, SGU_WIDTH)
    return y @ w_out

def _wkv7_scan(r, w, k, v, kk, kka):
    bsz, _, nh, n = r.shape
    xs = tuple(jnp.moveaxis(t, 1, 0) for t in (r, w, k, v, kk, kka))

    def step(S, inp):
        r_t, w_t, k_t, v_t, kk_t, kka_t = inp
        sa = jnp.einsum('bhvk,bhk->bhv', S, -kk_t)
        S = (S * w_t[:, :, None, :] + sa[..., None] * kka_t[:, :, None, :]
             + v_t[..., None] * k_t[:, :, None, :])
        y = jnp.einsum('bhvk,bhk->bhv', S, r_t)
        return S, y

    S0 = jnp.zeros((bsz, nh, n, n), jnp.float32)
    _, y = lax.scan(step, S0, xs)
    return jnp.moveaxis(y, 0, 1)

def _rwkv7_mixer(h, mu, w_rkv, w0, w_la, w_lb, a0, a_la, a_lb, g_la, g_lb,
                 k_k, k_a, r_k, ln_g, ln_b, w_o, v_first, v_mix):
    bsz, seq, d = h.shape
    f32 = jnp.float32

    def heads(t):
        return t.reshape(bsz, seq, RWKV_HEADS, RWKV_HEAD_DIM)

    xx = jnp.pad(h, ((0, 0), (1, 0), (0, 0)))[:, :-1] - h
    xs = h[None] + xx[None] * mu[:, None, None, :]
    rkv = jnp.einsum('pbtd,pde->pbte', xs[:3], w_rkv)
    r, k, v = rkv[0], rkv[1], rkv[2]
    xv, xw, xa, xg = xs[2], xs[3], xs[4], xs[5]
    log_w = -jax.nn.softplus(-(w0 + jnp.tanh(xw @ w_la) @ w_lb)) - 0.5
    decay = jnp.exp(-jnp.exp(log_w.astype(f32)))
    if v_mix is None:
        v_first = v
    else:
        v0, v_la, v_lb = v_mix
        v = v + (v_first - v) * jax.nn.sigmoid(v0 + (xv @ v_la) @ v_lb)
    a = jax.nn.sigmoid(a0 + (xa @ a_la) @ a_lb)
    g = jax.nn.sigmoid(xg @ g_la) @ g_lb
    kk = heads(k * k_k).astype(f32)
    kk = kk / jnp.maximum(jnp.sqrt(jnp.sum(kk * kk, axis=-1, keepdims=True)), 1e-12)
    k = k * (1.0 + (a - 1.0) * k_a)
    r_h, k_h, v_h = heads(r).astype(f32), heads(k).astype(f32), heads(v).astype(f32)
    y = _wkv7_scan(r_h, heads(decay), k_h, v_h, kk, kk * heads(a).astype(f32))
    mu_y = jnp.mean(y, axis=-1, keepdims=True)
    var_y = jnp.mean(jnp.square(y - mu_y), axis=-1, keepdims=True)
    y = ((y - mu_y) * lax.rsqrt(var_y + GN_EPS)).reshape(bsz, seq, d)
    y = y * ln_g.astype(f32) + ln_b.astype(f32)
    bonus = jnp.sum(r_h * k_h * r_k.astype(f32), axis=-1, keepdims=True) * v_h
    y = (y + bonus.reshape(bsz, seq, d)) * g.astype(f32)
    return y.astype(h.dtype) @ w_o, v_first

def _squared_relu_mlp(h, w1, w2):
    return jnp.square(jax.nn.relu(h @ w1)) @ w2

def second_inputs(seed: int = 0) -> dict:
    key = jax.random.key(seed)
    ks = jax.random.split(key, 32)
    f32 = jnp.float32
    D, E, G, H, N = D_MODEL, SGU_WIDTH, SGU_GROUPS, RWKV_HEADS, RWKV_HEAD_DIM
    nA, nB = N_LAYERS_A, N_LAYERS_B

    def nrm(k, shape, scale):
        return jax.random.normal(k, shape, f32) * scale

    return {
        "x": nrm(ks[0], (BATCH, SEQ, D), 1.0),
        "norm_mix_g": 1.0 + nrm(ks[1], (DEPTH_2, D), 0.05),
        "norm_ffn_g": 1.0 + nrm(ks[2], (DEPTH_2, D), 0.05),
        "final_norm_g": 1.0 + nrm(ks[3], (D,), 0.05),
        "ffn_w1": nrm(ks[4], (DEPTH_2, D, FFN_HIDDEN), D ** -0.5),
        "ffn_w2": nrm(ks[5], (DEPTH_2, FFN_HIDDEN, D), 0.5 * FFN_HIDDEN ** -0.5),
        "sgu_w_in": nrm(ks[6], (nA, D, 2 * E), D ** -0.5),
        "sgu_b_in": nrm(ks[7], (nA, 2 * E), 0.02),
        "sgu_ln_g": 1.0 + nrm(ks[8], (nA, E), 0.05),
        "sgu_ln_b": nrm(ks[9], (nA, E), 0.02),
        "sgu_w_s": nrm(ks[10], (nA, G, SGU_BLOCK, SGU_BLOCK), SGU_BLOCK ** -0.5),
        "sgu_b_s": 1.0 + nrm(ks[11], (nA, G, SGU_BLOCK), 0.1),
        "sgu_w_out": nrm(ks[12], (nA, E, D), 0.5 * E ** -0.5),
        "rwkv_mu": jax.random.uniform(ks[13], (nB, 6, D), f32),
        "rwkv_w_rkv": nrm(ks[14], (nB, 3, D, D), D ** -0.5),
        "rwkv_w0": jax.random.uniform(ks[15], (nB, D), f32, -6.0, 0.5),
        "rwkv_w_lora_a": nrm(ks[16], (nB, D, DECAY_LORA), D ** -0.5),
        "rwkv_w_lora_b": nrm(ks[17], (nB, DECAY_LORA, D), 0.3 * DECAY_LORA ** -0.5),
        "rwkv_a0": nrm(ks[18], (nB, D), 0.1),
        "rwkv_a_lora_a": nrm(ks[19], (nB, D, AAA_LORA), D ** -0.5),
        "rwkv_a_lora_b": nrm(ks[20], (nB, AAA_LORA, D), 0.3 * AAA_LORA ** -0.5),
        "rwkv_v0": 0.5 + nrm(ks[21], (nB - 1, D), 0.1),
        "rwkv_v_lora_a": nrm(ks[22], (nB - 1, D, MV_LORA), D ** -0.5),
        "rwkv_v_lora_b": nrm(ks[23], (nB - 1, MV_LORA, D), 0.3 * MV_LORA ** -0.5),
        "rwkv_g_lora_a": nrm(ks[24], (nB, D, GATE_LORA), D ** -0.5),
        "rwkv_g_lora_b": nrm(ks[25], (nB, GATE_LORA, D), GATE_LORA ** -0.5),
        "rwkv_k_k": 0.85 + nrm(ks[26], (nB, D), 0.05),
        "rwkv_k_a": 1.0 + nrm(ks[27], (nB, D), 0.05),
        "rwkv_r_k": nrm(ks[28], (nB, H, N), 0.1),
        "rwkv_ln_g": 1.0 + nrm(ks[29], (nB, D), 0.05),
        "rwkv_ln_b": nrm(ks[30], (nB, D), 0.02),
        "rwkv_w_o": nrm(ks[31], (nB, D, D), 0.5 * D ** -0.5),
    }

def second_block(x, norm_mix_g, norm_ffn_g, final_norm_g, ffn_w1, ffn_w2,
              sgu_w_in, sgu_b_in, sgu_ln_g, sgu_ln_b, sgu_w_s, sgu_b_s, sgu_w_out,
              rwkv_mu, rwkv_w_rkv, rwkv_w0, rwkv_w_lora_a, rwkv_w_lora_b,
              rwkv_a0, rwkv_a_lora_a, rwkv_a_lora_b,
              rwkv_v0, rwkv_v_lora_a, rwkv_v_lora_b,
              rwkv_g_lora_a, rwkv_g_lora_b, rwkv_k_k, rwkv_k_a, rwkv_r_k,
              rwkv_ln_g, rwkv_ln_b, rwkv_w_o):
    v_first = None
    for i in range(DEPTH_2):
        h = _rmsnorm_2(x, norm_mix_g[i])
        j = i // N_MIXERS
        if i % N_MIXERS == 0:
            y = _spatial_gating_mixer(h, sgu_w_in[j], sgu_b_in[j], sgu_ln_g[j], sgu_ln_b[j],
                                      sgu_w_s[j], sgu_b_s[j], sgu_w_out[j])
        else:
            v_mix = None if j == 0 else (rwkv_v0[j - 1], rwkv_v_lora_a[j - 1], rwkv_v_lora_b[j - 1])
            y, v_first = _rwkv7_mixer(h, rwkv_mu[j], rwkv_w_rkv[j], rwkv_w0[j],
                                      rwkv_w_lora_a[j], rwkv_w_lora_b[j],
                                      rwkv_a0[j], rwkv_a_lora_a[j], rwkv_a_lora_b[j],
                                      rwkv_g_lora_a[j], rwkv_g_lora_b[j],
                                      rwkv_k_k[j], rwkv_k_a[j], rwkv_r_k[j],
                                      rwkv_ln_g[j], rwkv_ln_b[j], rwkv_w_o[j],
                                      v_first, v_mix)
        x = x + y
        x = x + _squared_relu_mlp(_rmsnorm_2(x, norm_ffn_g[i]), ffn_w1[i], ffn_w2[i])
    return _rmsnorm_2(x, final_norm_g)


def setup_inputs(seed=0):
    out = dict(first_inputs(seed))
    for name, value in second_inputs(seed + 1).items():
        if name != "x":
            out[name + "_2"] = value
    return out


def reference(
    x, p, positions, g_mix_norm, w_in, sb_q_gain, sb_k_gain, ret_q_gain, ret_k_gain,
    ret_gn_gain, ret_gn_bias, w_out, g_ffn_norm, w_router, b_router, w_up_gate, b_up_gate,
    w_down, b_down, g_ple_norm, w_ple_gate, w_ple_proj, norm_mix_g_2, norm_ffn_g_2,
    final_norm_g_2, ffn_w1_2, ffn_w2_2, sgu_w_in_2, sgu_b_in_2, sgu_ln_g_2, sgu_ln_b_2,
    sgu_w_s_2, sgu_b_s_2, sgu_w_out_2, rwkv_mu_2, rwkv_w_rkv_2, rwkv_w0_2, rwkv_w_lora_a_2,
    rwkv_w_lora_b_2, rwkv_a0_2, rwkv_a_lora_a_2, rwkv_a_lora_b_2, rwkv_v0_2, rwkv_v_lora_a_2,
    rwkv_v_lora_b_2, rwkv_g_lora_a_2, rwkv_g_lora_b_2, rwkv_k_k_2, rwkv_k_a_2, rwkv_r_k_2,
    rwkv_ln_g_2, rwkv_ln_b_2, rwkv_w_o_2,
):
    x = first_block(
        x, p, positions, g_mix_norm, w_in, sb_q_gain, sb_k_gain, ret_q_gain, ret_k_gain,
        ret_gn_gain, ret_gn_bias, w_out, g_ffn_norm, w_router, b_router, w_up_gate, b_up_gate,
        w_down, b_down, g_ple_norm, w_ple_gate, w_ple_proj,
    )
    return second_block(
        x, norm_mix_g_2, norm_ffn_g_2, final_norm_g_2, ffn_w1_2, ffn_w2_2, sgu_w_in_2,
        sgu_b_in_2, sgu_ln_g_2, sgu_ln_b_2, sgu_w_s_2, sgu_b_s_2, sgu_w_out_2, rwkv_mu_2,
        rwkv_w_rkv_2, rwkv_w0_2, rwkv_w_lora_a_2, rwkv_w_lora_b_2, rwkv_a0_2, rwkv_a_lora_a_2,
        rwkv_a_lora_b_2, rwkv_v0_2, rwkv_v_lora_a_2, rwkv_v_lora_b_2, rwkv_g_lora_a_2,
        rwkv_g_lora_b_2, rwkv_k_k_2, rwkv_k_a_2, rwkv_r_k_2, rwkv_ln_g_2, rwkv_ln_b_2,
        rwkv_w_o_2,
    )


_drawn_inputs = setup_inputs


def setup_inputs(seed=0):
    import zlib

    import numpy as np

    out = dict(_drawn_inputs(seed))
    spreads = {}
    factors = {'sb_q_gain': 3.634,
     'sb_k_gain': 2.885,
     'b_up_gate': 5.627,
     'b_down': 6.476,
     'g_ple_norm': 8.0,
     'sgu_b_in_2': 6.988,
     'sgu_ln_g_2': 5.258,
     'sgu_ln_b_2': 8.0,
     'rwkv_w_lora_a_2': 8.0,
     'rwkv_w_lora_b_2': 8.0,
     'rwkv_a0_2': 7.311,
     'rwkv_k_k_2': 29.043,
     'rwkv_k_a_2': 5.419,
     'rwkv_ln_g_2': 6.317,
     'rwkv_ln_b_2': 28.106}
    for name, (base, spread) in spreads.items():
        noise = np.random.default_rng([zlib.crc32(name.encode()), seed]).standard_normal(out[name].shape)
        drawn = base * np.exp(spread * noise) if base else spread * noise
        out[name] = __import__('jax').numpy.asarray(drawn.astype(out[name].dtype))
    for name, factor in factors.items():
        out[name] = (out[name] * factor).astype(out[name].dtype)
    return out
```

```python
from contextlib import ExitStack

import numpy as np

import concourse.bass as bass
from concourse import mybir

F32 = mybir.dt.float32
F32R = mybir.dt.float32r
BF16 = mybir.dt.bfloat16
I32 = mybir.dt.int32
U32 = mybir.dt.uint32
ALU = mybir.AluOpType
ACT = mybir.ActivationFunctionType
AX = mybir.AxisListType

P = 128
T = 256
TC = T // P
D = 1024
KC = D // P
BANK = 512
HD = 64
HEADS = 8
PAIRS = HEADS // 2
HW = HEADS * HD
PLE = 256
EXPERTS = 32
TOPK = 4
CAP = 64
MAX_EXTRA = T * TOPK // (CAP + 1) + 1
BLOCKS = T // CAP
LIMIT = 7.0
ALPHA = 1.702
EPS = 1e-6
SGU = 2048
GROUPS = 16
FF = 4096
RH = 16
CH = 32
GN_EPS = 64e-5
LN_EPS = 1e-5
MIX_R, MIX_K, MIX_V, MIX_W, MIX_A, MIX_G = range(6)

COLS = {}
for _name, _n in (("g_mix", 8), ("g_ffn", 8), ("g_ple", 8), ("n_mix0", 8), ("n_mix1", 8), ("n_ffn0", 8),
                  ("n_ffn1", 8), ("b_u", 16), ("mu", 48), ("w0", 8), ("a0", 8), ("k_k", 8), ("k_a", 8),
                  ("r_k", 8)):
    COLS[_name] = sum(_n for _, _n in COLS.values()), _n
NCOLS = sum(_n for _, _n in COLS.values())
ROWS = {}
for _name, _n in (("sb_q", HD), ("sb_k", HD), ("ret_q", HD), ("ret_k", HD), ("gn_g", HW), ("gn_b", HW),
                  ("b_router", EXPERTS), ("inv_freq", HD // 2), ("b_v", SGU), ("ln_g", SGU), ("ln_b", SGU),
                  ("b_s", SGU), ("final", D), ("rln_g", D), ("rln_b", D)):
    ROWS[_name] = sum(_n for _, _n in ROWS.values()), _n
NROWS = sum(_n for _, _n in ROWS.values())


class Chain:

    def __init__(self, sem):
        self.sem, self.n = sem, 0

    def __call__(self, eng, ins):
        self.n += 1
        ins.then_inc(self.sem, 1)
        eng.wait_ge(self.sem, self.n)


class Core:

    def __init__(self, nc, dram, out, ctx):
        self.nc, self.dram, self.out, self.ctx = nc, dram, out, ctx
        self.stage_semaphores = []
        self.stage = 1
        self.x = ctx.enter_context(nc.sbuf_tensor("x", [P, TC, D], F32))
        self.xT = ctx.enter_context(nc.sbuf_tensor("xT", [P, KC, T], F32))
        self.ident = ctx.enter_context(nc.sbuf_tensor("ident", [P, P], F32))
        self.cols = ctx.enter_context(nc.sbuf_tensor("cols", [P, NCOLS], F32))
        self.stat = ctx.enter_context(nc.sbuf_tensor("stat", [P, 8], F32))
        self.banks = ctx.enter_context(nc.psum_tensor("banks", [P, 8, BANK], F32))
        self.dve_chain = Chain(ctx.enter_context(nc.semaphore("dve_chain")))
        self.act_chain = Chain(ctx.enter_context(nc.semaphore("act_chain")))
        self.root = ctx.enter_context(nc.sbuf_tensor("root", [P, 2, RH], F32))

    def dve_rstd(self, dve, ins, var, work=None):
        v, chain, n = self.nc.vector, self.dve_chain, var.shape[1]
        y, t = work or (self.root[:, 0, 0:n], self.root[:, 1, 0:n])
        chain(dve, ins)
        chain(dve, v.tensor_scalar(t.bitcast(I32), var.bitcast(I32), 1, None, ALU.logical_shift_right))
        chain(dve, v.tensor_scalar(y.bitcast(I32), t.bitcast(I32), -1.0, float(0x5F3759DF), ALU.mult, ALU.add))
        for step in range(3):
            chain(dve, v.scalar_tensor_tensor(t, y, -0.5, y, ALU.mult, ALU.mult))
            chain(dve, v.tensor_tensor(t, t, var, ALU.mult))
            chain(dve, v.scalar_tensor_tensor(y if step < 2 else var, t, 1.5, y, ALU.add, ALU.mult))

    def open_ring(self, es, slots):
        self.ring = es.enter_context(self.nc.sbuf_tensor(f"ring_{self.stage}", [P, slots * 4096], F32))

    def semaphore(self, name):
        self.stage_semaphores.append(self.nc.alloc_semaphore(f"{name}_{self.stage}"))
        return self.stage_semaphores[-1]

    def end_stage(self):
        self.nc.clear_and_free_semaphores(self.stage_semaphores)
        self.nc.all_engine_barrier()
        self.stage_semaphores = []
        self.stage += 1

    def col(self, name, c=0, n=1):
        at = COLS[name][0] + c
        return self.cols[:, at:at + n]

    def row(self, name):
        at, n = ROWS[name]
        return self.dram["rows"][0:1, at:at + n]


def rows_to_all(row):
    return row.to_broadcast([P, row.shape[1]])


class Norm:

    def __init__(self, core, es, tag, gain, xn, first_bank=0):
        self.core, self.gain, self.xn, self.b0 = core, gain, xn, first_bank
        self.rows_done = core.semaphore(f"{tag}_rows_done")
        self.turned = core.semaphore(f"{tag}_turned")
        self.by_act = core.semaphore(f"{tag}_by_act")
        self.by_dve = core.semaphore(f"{tag}_by_dve")

    def dve_rows(self, dve, tc):
        c, nc, chain = self.core, self.core.nc, self.core.dve_chain
        xn, x, s = self.xn, c.x, c.stat
        chain(dve, nc.vector.tensor_tensor_reduce(xn[:, tc, :], x[:, tc, :], x[:, tc, :], 1.0, 0.0,
                                                  ALU.mult, ALU.add, s[:, tc:tc + 1]))
        c.dve_rstd(dve, nc.vector.tensor_scalar(s[:, tc:tc + 1], s[:, tc:tc + 1], 1.0 / D, EPS, ALU.mult, ALU.add), s[:, tc:tc + 1])
        nc.vector.tensor_scalar(xn[:, tc, :], x[:, tc, :], s[:, tc:tc + 1], None, ALU.mult).then_inc(
            self.rows_done, 1)

    def pe_turn(self, pe):
        c = self.core
        pe.wait_ge(self.rows_done, TC)
        for k in range(KC):
            for tc in range(TC):
                at = (k % 2) * T + tc * P
                ins = c.nc.tensor.transpose(c.banks[:, self.b0 + k // 2, at:at + P],
                                            self.xn[:, tc, k * P:(k + 1) * P], c.ident[:, :])
            if k % 2:
                ins.then_inc(self.turned, 1)

    def _bank(self, b):
        return self.core.banks[:, self.b0 + b, :]

    def act_take(self, act):
        c = self.core
        for b in (0, 2):
            act.wait_ge(self.turned, b + 1)
            for k in (2 * b, 2 * b + 1):
                c.nc.scalar.activation(c.xT[:, k, :], self._bank(b)[:, (k % 2) * T:(k % 2 + 1) * T], ACT.Copy,
                                       scale=c.col(self.gain, k)).then_inc(self.by_act, 1)

    def dve_take(self, dve):
        c = self.core
        for b in (1, 3):
            dve.wait_ge(self.turned, b + 1)
            for k in (2 * b, 2 * b + 1):
                c.nc.vector.tensor_scalar(c.xT[:, k, :], self._bank(b)[:, (k % 2) * T:(k % 2 + 1) * T],
                                          c.col(self.gain, k), None, ALU.mult).then_inc(self.by_dve, 1)

    def wait(self, eng):
        eng.wait_ge(self.by_act, 4)
        eng.wait_ge(self.by_dve, 4)


def matmuls(nc, out, lhs, rhs, start=True, stop=True):
    n = len(lhs)
    for i in range(n):
        ins = nc.tensor.matmul(out, lhs[i], rhs[i], start=start and i == 0, stop=stop and i == n - 1)
    return ins


def mixer_stage(c):
    nc, d = c.nc, c.dram
    SEGS = 7
    SB_Q, SB_K, SB_V, R_Q, R_K, R_V, R_G = range(SEGS)
    NORMED = {SB_Q: 0, SB_K: 1, R_Q: 2, R_K: 3}
    VALUES = {SB_V: 0, R_V: 1}
    GAINS = ("sb_q", "sb_k", "ret_q", "ret_k")
    w_in = d["w_in"].rearrange("(k p) n -> p k n", p=P)
    w_out = d["w_out"].rearrange("(k p) n -> p k n", p=P)
    with ExitStack() as es:
        def sb(name, shape, dt=F32):
            return es.enter_context(nc.sbuf_tensor(name, shape, dt))

        def sem(name):
            return c.semaphore(name)

        c.open_ring(es, 7)
        xn = sb("m_xn", [P, TC, D])
        qk = sb("qk", [P, 4, TC, HW])
        val = sb("val", [P, 2, TC, HW])
        silu_g = sb("silu_g", [P, TC, HW])
        squares = sb("squares", [P, 2, HW])
        ssum = sb("ssum", [P, HEADS])
        gains = sb("gains", [P, 4, HD])
        gn_g = sb("gn_g", [P, HW])
        gn_b = sb("gn_b", [P, HW])
        pos_i = sb("pos_i", [P, TC], I32)
        pos = sb("pos", [P, TC])
        inv_freq = sb("inv_freq", [P, HD // 2])
        angle = sb("angle", [P, 2, TC, HD // 2])
        turns = sb("turns", [P, 2, TC, HD // 2])
        sincos = sb("sincos", [P, 2, TC, HD // 2])
        rope = sb("rope", [P, 4, HW // 2])
        x_in, small_in, rope_in = sem("x_in"), sem("small_in"), sem("rope_in")
        w_seg = [sem(f"w_seg{s}") for s in range(SEGS)]
        norm = Norm(c, es, "mix_norm", "g_mix", xn)
        projected = sem("projected")
        squared = sem("squared")
        squares_read = sem("squares_read")
        bank_dve, bank_act = sem("bank_dve"), sem("bank_act")
        angles_done, sines_done = sem("angles_done"), sem("sines_done")

        def bank_of(seg, tc):
            return (seg * TC + tc) % 8

        def bank_free(pe, n):
            if n >= 8:
                seg, tc = divmod(n - 8, TC)
                mine = NORMED if seg in NORMED else {s: 0 for s in range(SEGS) if s not in NORMED}
                before = sum(s < seg for s in mine)
                pe.wait_ge(bank_dve if seg in NORMED else bank_act, before * TC + tc + 1)

        with nc.Block() as block:
            @block.sync
            def _(sp):
                sp.dma_start(c.x[:, :, :], d["x"].rearrange("(c p) n -> p c n", p=P)).then_inc(x_in, 16)
                sp.dma_start(c.ident[:, :], d["ident"]).then_inc(x_in, 16)
                sp.dma_start(c.cols[:, :], d["cols"]).then_inc(x_in, 16)
                for s in range(SEGS):
                    sp.dma_start(c.ring[:, s * 4096:(s + 1) * 4096].rearrange("p (k n) -> p k n", k=KC),
                                 w_in[:, :, s * HW:(s + 1) * HW]).then_inc(w_seg[s], 16)
                    if s == 0:
                        sp.dma_start(pos_i[:, :], d["positions"]).then_inc(rope_in, 16)
                        sp.dma_start(inv_freq[:, :], rows_to_all(c.row("inv_freq"))).then_inc(rope_in, 16)
                        for i, g in enumerate(GAINS):
                            sp.dma_start(gains[:, i, :], rows_to_all(c.row(g))).then_inc(small_in, 16)
                        sp.dma_start(gn_g[:, :], rows_to_all(c.row("gn_g"))).then_inc(small_in, 16)
                        sp.dma_start(gn_b[:, :], rows_to_all(c.row("gn_b"))).then_inc(small_in, 16)

            @block.tensor
            def _(pe):
                pe.wait_ge(x_in, 48)
                norm.pe_turn(pe)
                norm.wait(pe)
                for s in range(SEGS):
                    pe.wait_ge(w_seg[s], 16)
                    w = c.ring[:, s * 4096:(s + 1) * 4096].rearrange("p (k n) -> p k n", k=KC)
                    for tc in range(TC):
                        bank_free(pe, s * TC + tc)
                        matmuls(nc, c.banks[:, bank_of(s, tc), :],
                                [c.xT[:, k, tc * P:(tc + 1) * P] for k in range(KC)],
                                [w[:, k, :] for k in range(KC)]).then_inc(projected, 1)

            @block.scalar
            def _(act):
                act.wait_ge(x_in, 48)
                norm.act_take(act)
                n_sq = 0
                for s in range(SEGS):
                    for tc in range(TC):
                        bank = c.banks[:, bank_of(s, tc), :]
                        act.wait_ge(projected, s * TC + tc + 1)
                        if s in NORMED:
                            if n_sq >= 2:
                                act.wait_ge(squares_read, n_sq - 1)
                            nc.scalar.activation(squares[:, n_sq % 2, :], bank, ACT.Square).then_inc(squared, 1)
                            n_sq += 1
                        elif s in VALUES:
                            nc.scalar.activation(val[:, VALUES[s], tc, :], bank, ACT.Copy).then_inc(bank_act, 1)
                        else:
                            nc.scalar.activation(silu_g[:, tc, :], bank, ACT.Silu).then_inc(bank_act, 1)
                act.wait_ge(angles_done, 1)
                nc.scalar.activation(sincos[:, :, :, :], angle[:, :, :, :], ACT.Sin).then_inc(sines_done, 1)

            @block.vector
            def _(dve):
                chain = c.dve_chain
                dve.wait_ge(x_in, 48)
                for tc in range(TC):
                    norm.dve_rows(dve, tc)
                norm.dve_take(dve)
                dve.wait_ge(rope_in, 32)
                chain(dve, nc.vector.tensor_copy(pos[:, :], pos_i[:, :]))
                MAGIC = 12582912.0
                two_pi = 2 * np.pi
                c1 = 6.28125
                c2 = float(np.float32(two_pi - c1) - np.float32(two_pi - c1) % np.float32(2.0 ** -20))
                c3 = two_pi - c1 - c2
                for tc in range(TC):
                    chain(dve, nc.vector.tensor_scalar(turns[:, 0, tc, :], inv_freq[:, :], pos[:, tc:tc + 1], None,
                                                       ALU.mult))
                for f in range(2):
                    chain(dve, nc.vector.tensor_scalar(angle[:, f, :, :], turns[:, 0, :, :], 1 / two_pi,
                                                       0.25 * f, ALU.mult, ALU.add))
                    chain(dve, nc.vector.tensor_scalar(angle[:, f, :, :], angle[:, f, :, :], MAGIC, None, ALU.add))
                    chain(dve, nc.vector.tensor_scalar(angle[:, f, :, :], angle[:, f, :, :], -MAGIC, None, ALU.add))
                    for i, part in enumerate((c1, c2, c3)):
                        src = turns[:, 0, :, :] if i == 0 else turns[:, 1, :, :]
                        chain(dve, nc.vector.scalar_tensor_tensor(turns[:, 1, :, :], angle[:, f, :, :], -part, src,
                                                                  ALU.mult, ALU.add))
                    chain(dve, nc.vector.tensor_scalar(angle[:, f, :, :], turns[:, 1, :, :], f * np.pi / 2, 3.1415925,
                                                       ALU.add, ALU.min))
                    chain(dve, nc.vector.tensor_scalar(angle[:, f, :, :], angle[:, f, :, :], -3.1415925, None,
                                                       ALU.max))
                dve.nop().then_inc(angles_done, 1)
                dve.wait_ge(small_in, 96)
                n_sq = 0
                for s in range(SEGS):
                    if s not in NORMED:
                        continue
                    at = NORMED[s]
                    for tc in range(TC):
                        bank = c.banks[:, bank_of(s, tc), :]
                        out = qk[:, at, tc, :].rearrange("p (h d) -> p h d", h=HEADS)
                        dve.wait_ge(squared, n_sq + 1)
                        nc.vector.tensor_reduce(ssum[:, :], squares[:, n_sq % 2, :].rearrange(
                            "p (h d) -> p h d", h=HEADS), AX.X, ALU.add).then_inc(squares_read, 1)
                        dve.wait_ge(squares_read, n_sq + 1)
                        c.dve_rstd(dve, nc.vector.tensor_scalar(ssum[:, :], ssum[:, :], 1.0 / HD, EPS, ALU.mult, ALU.add), ssum[:, :])
                        nc.vector.tensor_tensor(out, bank.rearrange("p (h d) -> p h d", h=HEADS),
                                                ssum[:, :].unsqueeze(2).to_broadcast([P, HEADS, HD]),
                                                ALU.mult).then_inc(bank_dve, 1)
                        dve.wait_ge(bank_dve, n_sq + 1)
                        chain(dve, nc.vector.tensor_tensor(out, out, gains[:, at, :].unsqueeze(1).to_broadcast(
                            [P, HEADS, HD]), ALU.mult))
                        n_sq += 1
                dve.wait_ge(sines_done, 1)
                for at in (2, 3):
                    for tc in range(TC):
                        v = qk[:, at, tc, :].rearrange("p (h f d) -> p h f d", h=HEADS, f=2)
                        tmp = [rope[:, i, :].rearrange("p (h d) -> p h d", h=HEADS) for i in range(4)]
                        sin, cos = (sincos[:, f, tc, :].unsqueeze(1).to_broadcast([P, HEADS, HD // 2])
                                    for f in range(2))
                        nc.vector.tensor_tensor(tmp[0], v[:, :, 0, :], cos, ALU.mult)
                        nc.vector.tensor_tensor(tmp[1], v[:, :, 1, :], sin, ALU.mult)
                        nc.vector.tensor_tensor(tmp[2], v[:, :, 1, :], cos, ALU.mult)
                        chain(dve, nc.vector.tensor_tensor(tmp[3], v[:, :, 0, :], sin, ALU.mult))
                        nc.vector.tensor_tensor(v[:, :, 0, :], tmp[0], tmp[1], ALU.subtract)
                        chain(dve, nc.vector.tensor_tensor(v[:, :, 1, :], tmp[2], tmp[3], ALU.add))

        DIAG = 2 * P + P
        qkT = c.ring[:, 8192:12288].rearrange("p (a b t) -> p a b t", a=4, b=PAIRS)
        decay = c.ring[:, 12288:15360].rearrange("p (h n) -> p h n", h=HEADS)
        sufsum = sb("sufsum", [P, P])
        allneg = sb("allneg", [P, P])
        soft = sb("soft", [P, 2, DIAG])
        weight = sb("weight", [P, 2, DIAG])
        scored = sb("scored", [P, 2, DIAG])
        yT = c.ring[:, 16384:18432].rearrange("p (k t) -> p k t", k=KC)
        yb = sb("yb", [P, TC, HW])
        tmp = sb("gn_tmp", [P, HW])
        mean = sb("gn_mean", [P, 2, HEADS])
        const_in, allneg_done = sem("const_in"), sem("allneg_done")
        w_out_in = sem("w_out_in")
        turned, took_act, took_dve = sem("h_turned"), sem("h_took_act"), sem("h_took_dve")
        z_done, soft_done, soft_masked = sem("z_done"), sem("soft_done"), sem("soft_masked")
        ln_done = sem("ln_done")
        arg_done, exp_done, w_masked = sem("arg_done"), sem("exp_done"), sem("w_masked")
        y_done, y_taken = sem("y_done"), sem("y_taken")
        s_done, s_decayed, r_done = sem("s_done"), sem("s_decayed"), sem("r_done")
        yb_done, yb_turned, yb_taken = sem("yb_done"), sem("yb_turned"), sem("yb_taken")
        mixed = sem("mixed")
        Z, A, Y, S, R = (0, 1), (2, 3), 4, 5, (6, 7)

        def half(h):
            return slice(HD * (h % 2), HD * (h % 2) + HD)

        def scores(out, kT, qT, h, start, stop):
            s, p = half(h), h // 2
            nc.tensor.matmul(out[:, 0:T], kT[s, p, 0:P], qT[s, p, :], start=start, stop=stop,
                             skip_group_check=True)
            return nc.tensor.matmul(out[:, T:DIAG], kT[s, p, P:T], qT[s, p, P:T], start=False, stop=stop,
                                    skip_group_check=True)

        with nc.Block() as block:
            @block.sync
            def _(sp):
                sp.dma_start(sufsum[:, :], d["sufsum"]).then_inc(const_in, 16)
                sp.dma_start(decay, d["decay"].rearrange("p (h n) -> p h n", h=HEADS)).then_inc(
                    const_in, 16)
                sp.dma_start(c.ring[:, 0:KC * D].rearrange("p (k n) -> p k n", k=KC), w_out).then_inc(w_out_in, 16)

            @block.tensor
            def _(pe):
                for g in range(8):
                    for i in range(2):
                        at, p = divmod(2 * g + i, PAIRS)
                        for tc in range(TC):
                            ins = nc.tensor.transpose(
                                c.banks[:, g, i * T + tc * P:i * T + (tc + 1) * P],
                                qk[:, at, tc, p * P:(p + 1) * P], c.ident[:, :])
                    ins.then_inc(turned, 1)
                pe.wait_ge(took_act, 4)
                pe.wait_ge(took_dve, 4)
                pe.wait_ge(const_in, 32)
                pe.wait_ge(allneg_done, 1)
                qT, kT, rqT, rkT = (qkT[:, i, :, :] for i in range(4))

                def first(h):
                    if h >= 2:
                        pe.wait_ge(soft_done, h - 1)
                    scores(c.banks[:, Z[h % 2], :], kT, qT, h, True, True).then_inc(z_done, 1)

                def retention_scores(h):
                    if h:
                        pe.wait_ge(s_decayed, h)
                    scores(c.banks[:, S, :], rkT, rqT, h, True, True).then_inc(s_done, 1)

                def second(h):
                    pe.wait_ge(soft_masked, h + 1)
                    if h >= 2:
                        pe.wait_ge(exp_done, h - 1)
                    out, sp = c.banks[:, A[h % 2], :], soft[:, h % 2, :]
                    scores(out, kT, qT, h, True, False)
                    nc.tensor.matmul(out[:, P:T], allneg[:, :], sp[:, T:DIAG], start=False, stop=False,
                                     skip_group_check=True)
                    nc.tensor.matmul(out[:, 0:T], sufsum[:, :], sp[:, 0:T], start=False, stop=True,
                                     skip_group_check=True)
                    nc.tensor.matmul(out[:, T:DIAG], sufsum[:, :], sp[:, T:DIAG], start=False, stop=True,
                                     skip_group_check=True).then_inc(arg_done, 1)

                def values(h):
                    pe.wait_ge(w_masked, h + 1)
                    if h % 2 == 0 and h:
                        pe.wait_ge(y_taken, h // 2)
                    out, w, v = c.banks[half(h), Y, :], weight[:, h % 2, :], val[:, 0, :, h * HD:(h + 1) * HD]
                    nc.tensor.matmul(out[:, P:T], v[:, 1, :], w[:, T:DIAG], start=True, stop=False,
                                     skip_group_check=True)
                    nc.tensor.matmul(out[:, 0:T], v[:, 0, :], w[:, 0:T], start=False, stop=True,
                                     skip_group_check=True).then_inc(y_done, 1)

                def retention_values(h):
                    pe.wait_ge(s_decayed, h + 1)
                    s, v, at = scored[:, h % 2, :], val[:, 1, :, h * HD:(h + 1) * HD], slice(h * HD, (h + 1) * HD)
                    nc.tensor.matmul(c.banks[:, R[0], at], s[:, 0:P], v[:, 0, :], start=True, stop=True)
                    nc.tensor.matmul(c.banks[:, R[1], at], s[:, P:T], v[:, 0, :], start=True, stop=False)
                    nc.tensor.matmul(c.banks[:, R[1], at], s[:, T:DIAG], v[:, 1, :], start=False,
                                     stop=True).then_inc(r_done, 1)

                first(0)
                for h in range(HEADS):
                    retention_scores(h)
                    if h + 1 < HEADS:
                        first(h + 1)
                    second(h)
                    retention_values(h)
                    if h:
                        values(h - 1)
                values(HEADS - 1)
                pe.wait_ge(yb_done, TC)
                for p in range(PAIRS):
                    for tc in range(TC):
                        ins = nc.tensor.transpose(c.banks[:, p // 2, (p % 2) * T + tc * P:(p % 2) * T + (tc + 1) * P],
                                                  yb[:, tc, p * P:(p + 1) * P], c.ident[:, :])
                    if p % 2:
                        ins.then_inc(yb_turned, 1)
                pe.wait_ge(y_taken, PAIRS)
                pe.wait_ge(yb_taken, PAIRS)
                pe.wait_ge(w_out_in, 16)
                w = c.ring[:, 0:KC * D].rearrange("p (k n) -> p k n", k=KC)
                for tc in range(TC):
                    for n in range(2):
                        matmuls(nc, c.banks[:, 2 + 2 * tc + n, :],
                                [yT[:, k, tc * P:(tc + 1) * P] for k in range(KC)],
                                [w[:, k, n * BANK:(n + 1) * BANK] for k in range(KC)]).then_inc(mixed, 1)

            SCALED = (0, 3)

            @block.scalar
            def _(act):
                for g in range(0, 8, 2):
                    act.wait_ge(turned, g + 1)
                    at, p = divmod(2 * g, PAIRS)
                    nc.scalar.activation(qkT[:, at, p:p + 2, :].rearrange("p a b -> p (a b)"), c.banks[:, g, :],
                                         ACT.Copy, scale=HD ** -0.5 if at in SCALED else 1.0).then_inc(took_act, 1)

                def log_part(h):
                    chain = c.act_chain
                    out = soft[:, h % 2, :]
                    act.wait_ge(z_done, h + 1)
                    if h >= 2:
                        act.wait_ge(arg_done, h - 1)
                    chain(act, nc.scalar.activation(out, c.banks[:, Z[h % 2], 0:DIAG], ACT.Abs))
                    chain(act, nc.scalar.activation(out, out, ACT.Exp, scale=-1.0))
                    nc.scalar.activation(out, out, ACT.Ln, bias=1.0).then_inc(ln_done, 1)

                def exponent(h):
                    act.wait_ge(arg_done, h + 1)
                    if h >= 2:
                        act.wait_ge(y_done, h - 1)
                    nc.scalar.activation(weight[:, h % 2, :], c.banks[:, A[h % 2], 0:DIAG], ACT.Exp).then_inc(
                        exp_done, 1)

                def take(p):
                    act.wait_ge(y_done, 2 * p + 2)
                    nc.scalar.activation(yT[:, p, :], c.banks[:, Y, 0:T], ACT.Copy).then_inc(y_taken, 1)

                log_part(0)
                for h in range(HEADS):
                    if h + 1 < HEADS:
                        log_part(h + 1)
                    exponent(h)
                    if h % 2 == 0 and h:
                        take(h // 2 - 1)
                take(PAIRS - 1)
                for b in range(2):
                    act.wait_ge(yb_turned, b + 1)
                    nc.scalar.activation(yT[:, PAIRS + 2 * b:PAIRS + 2 * b + 2, :].rearrange("p a b -> p (a b)"),
                                         c.banks[:, b, :], ACT.Copy).then_inc(yb_taken, 2)

            @block.gpsimd
            def _(pool):
                nc.gpsimd.memset(allneg[:, :], -1.0).then_inc(allneg_done, 1)
                for h in range(HEADS):
                    for src, ready, done in ((soft, soft_done, soft_masked), (weight, exp_done, w_masked)):
                        pool.wait_ge(ready, h + 1)
                        v = src[:, h % 2, 0:P]
                        nc.gpsimd.affine_select(out=v, in_=v, compare_op=ALU.is_gt, fill=0.0, base=0,
                                                pattern=[[1, P]], channel_multiplier=-1)
                        v = src[:, h % 2, T:DIAG]
                        nc.gpsimd.affine_select(out=v, in_=v, compare_op=ALU.is_gt, fill=0.0, base=0,
                                                pattern=[[1, P]], channel_multiplier=-1).then_inc(done, 1)

            @block.vector
            def _(dve):
                chain = c.dve_chain
                for g in range(1, 8, 2):
                    dve.wait_ge(turned, g + 1)
                    at, p = divmod(2 * g, PAIRS)
                    nc.vector.tensor_scalar(qkT[:, at, p:p + 2, :].rearrange("p a b -> p (a b)"), c.banks[:, g, :],
                                            HD ** -0.5 if at in SCALED else 1.0, None, ALU.mult).then_inc(took_dve, 1)
                dve.wait_ge(const_in, 32)

                def softplus(h):
                    dve.wait_ge(ln_done, h + 1)
                    nc.vector.scalar_tensor_tensor(soft[:, h % 2, :], c.banks[:, Z[h % 2], 0:DIAG], 0.0,
                                                   soft[:, h % 2, :], ALU.max, ALU.add).then_inc(soft_done, 1)

                softplus(0)
                for h in range(HEADS):
                    dve.wait_ge(s_done, h + 1)
                    if h >= 2:
                        dve.wait_ge(r_done, h - 1)
                    nc.vector.tensor_tensor(scored[:, h % 2, :], c.banks[:, S, 0:DIAG], decay[:, h, :],
                                            ALU.mult).then_inc(s_decayed, 1)
                    if h + 1 < HEADS:
                        softplus(h + 1)
                dve.wait_ge(r_done, HEADS)
                for tc in range(TC):
                    y3 = yb[:, tc, :].rearrange("p (h d) -> p h d", h=HEADS)
                    r3 = c.banks[:, R[tc], :].rearrange("p (h d) -> p h d", h=HEADS)
                    t3 = tmp[:, :].rearrange("p (h d) -> p h d", h=HEADS)
                    mu, var = mean[:, 0, :], mean[:, 1, :]
                    chain(dve, nc.vector.tensor_reduce(mu, r3, AX.X, ALU.add))
                    chain(dve, nc.vector.tensor_scalar(mu, mu, 1.0 / HD, None, ALU.mult))
                    chain(dve, nc.vector.tensor_tensor(y3, r3, mu.unsqueeze(2).to_broadcast([P, HEADS, HD]),
                                                       ALU.subtract))
                    chain(dve, nc.vector.tensor_tensor(t3, y3, y3, ALU.mult))
                    chain(dve, nc.vector.tensor_reduce(var, t3, AX.X, ALU.add))
                    c.dve_rstd(dve, nc.vector.tensor_scalar(var, var, 1.0 / HD, EPS, ALU.mult, ALU.add), var)
                    chain(dve, nc.vector.tensor_tensor(y3, y3, var.unsqueeze(2).to_broadcast([P, HEADS, HD]),
                                                       ALU.mult))
                    chain(dve, nc.vector.tensor_tensor(yb[:, tc, :], yb[:, tc, :], gn_g[:, :], ALU.mult))
                    chain(dve, nc.vector.tensor_tensor(yb[:, tc, :], yb[:, tc, :], gn_b[:, :], ALU.add))
                    nc.vector.tensor_tensor(yb[:, tc, :], yb[:, tc, :], silu_g[:, tc, :], ALU.mult).then_inc(
                        yb_done, 1)
                for tc in range(TC):
                    for n in range(2):
                        dve.wait_ge(mixed, 2 * tc + n + 1)
                        v = c.x[:, tc, n * BANK:(n + 1) * BANK]
                        nc.vector.tensor_tensor(v, v, c.banks[:, 2 + 2 * tc + n, :], ALU.add)


def expert_stage(c):
    nc, d = c.nc, c.dram
    E, E3 = EXPERTS, EXPERTS * (BLOCKS - 1)
    w_up, w_down, b_up = d["w_up"], d["w_down"], d["b_up"]
    COUNT, EXPERT_AT, BLOCK_AT, LIST = 0, 64, 128, 192
    with ExitStack() as es:
        def sb(name, shape, dt=F32):
            return es.enter_context(nc.sbuf_tensor(name, shape, dt))

        def sem(name):
            return c.semaphore(name)

        c.open_ring(es, 7)
        xn = sb("e_xn", [P, TC, D])
        parts = sb("parts", [P, 3, TC, D], BF16)
        w_router = sb("w_router_sb", [P, KC, E])
        b_router = sb("b_router_sb", [P, E])
        b_down = sb("b_down_sb", [E, D])
        upto = sb("upto", [P, P])
        ones = sb("ones", [P, P])
        number = sb("number", [P, BLOCKS * 2 * CAP])
        expert_no = sb("expert_no", [P, E])
        extra_col = sb("extra_col", [P, 3])
        work_list = sb("work_list", [1, LIST], I32)
        logits = sb("logits", [P, TC, E])
        top = sb("top", [P, TC, 8])
        top_i = sb("top_i", [P, TC, 8], U32)
        top_f = sb("top_f", [P, TC, 8])
        neg_max = sb("neg_max", [P, TC])
        gate = sb("gate", [P, TC, TOPK])
        gate_sum = sb("gate_sum", [P, TC])
        hit = sb("hit", [P, 2, TOPK, E])
        gates = sb("gates", [P, TC, E])
        chosen = sb("chosen", [P, TC, BLOCKS - 1, E])
        rank = sb("rank", [P, TC, E])
        gatesT = sb("gatesT", [E, T])
        flag = sb("flag", [E3, 1])
        place = sb("place", [E3, 1])
        spot = sb("spot", [E3, MAX_EXTRA])

        norm = Norm(c, es, "ffn_norm", "g_ffn", xn)
        router_in, const_in, list_in = sem("router_in"), sem("r_const_in"), sem("list_in")
        split_act, split_dve = sem("split_act"), sem("split_dve")
        routed, negated, exped = sem("routed"), sem("negated"), sem("exped")
        marked, counted, flagged, placed, spotted, listed = (sem(n) for n in (
            "marked", "counted", "flagged", "placed", "spotted", "listed"))
        gates_turned = sem("gates_turned")
        up_slot = [c.ring[:, k * 2048:(k + 1) * 2048] for k in range(KC)]
        down_slot = [c.ring[:, (KC + j) * 2048:(KC + j + 1) * 2048].rearrange("p (c n) -> p c n", c=2)
                     for j in range(KC // 2)]
        up_in = [sem(f"up_in{k}") for k in range(KC)]
        down_in = [sem(f"down_in{j}") for j in range(KC // 2)]
        bias_in = sem("bias_in")
        bias = sb("bias", [1, 2 * D])

        def load_up(sp, e, k):
            sp.dma_start(up_slot[k], w_up[bass.ds(e * D + k * P, P), :]).then_inc(up_in[k], 16)

        def load_down(sp, e, j):
            rows = w_down[bass.ds(e * D + j * 2 * P, 2 * P), :].rearrange("(c p) n -> p c n", p=P)
            sp.dma_start(down_slot[j], rows).then_inc(down_in[j], 16)

        def load_bias(sp, e):
            sp.dma_start(bias[:, :], b_up[bass.ds(e, 1), :]).then_inc(bias_in, 16)

        with nc.Block() as block:
            @block.sync
            def _(sp):
                sp.dma_start(w_router[:, :, :], d["w_router"].rearrange("(k p) n -> p k n", p=P)).then_inc(
                    router_in, 16)
                sp.dma_start(b_router[:, :], rows_to_all(c.row("b_router"))).then_inc(router_in, 16)
                sp.dma_start(upto[:, :], d["upto"]).then_inc(const_in, 16)
                sp.dma_start(number[:, :], d["number"]).then_inc(const_in, 16)
                sp.dma_start(expert_no[:, :], d["expert_no"]).then_inc(const_in, 16)
                sp.dma_start(extra_col[:, :], d["extra_col"]).then_inc(const_in, 16)
                sp.dma_start(b_down[:, :], d["b_down"]).then_inc(const_in, 16)
                sp.dma_start(work_list[:, :], d["work_list"]).then_inc(list_in, 16)
                load_bias(sp, 0)
                for k in range(KC):
                    load_up(sp, 0, k)
                for j in range(KC // 2):
                    load_down(sp, 0, j)

            LOGIT, RANK, EXTRA, TURN = 4, 5, 6, 7

            @block.tensor
            def _(pe):
                norm.pe_turn(pe)
                norm.wait(pe)
                pe.wait_ge(router_in, 32)
                for tc in range(TC):
                    matmuls(nc, c.banks[:, LOGIT, tc * E:(tc + 1) * E],
                            [c.xT[:, k, tc * P:(tc + 1) * P] for k in range(KC)],
                            [w_router[:, k, :] for k in range(KC)]).then_inc(routed, 1)
                pe.wait_ge(const_in, 80)
                pe.wait_ge(marked, 2)
                for tc in range(TC):
                    out = c.banks[:, RANK, tc * E:(tc + 1) * E]
                    if tc:
                        nc.tensor.matmul(out, ones[:, :], chosen[:, 0, 0, :], start=True, stop=False)
                    nc.tensor.matmul(out, upto[:, :], chosen[:, tc, 0, :], start=not tc, stop=True)
                for tc in range(TC):
                    nc.tensor.matmul(c.banks[0:E3, EXTRA, 0:1], chosen[:, tc, :, :].rearrange("p b e -> p (b e)"),
                                     ones[:, 0:1], start=tc == 0, stop=tc == 1)
                for tc in range(TC):
                    ins = nc.tensor.transpose(c.banks[0:E, TURN, tc * P:(tc + 1) * P], gates[:, tc, :],
                                              c.ident[:, :])
                ins.then_inc(counted, 1)
                pe.wait_ge(flagged, 1)
                nc.tensor.matmul(c.banks[0:E3, EXTRA, 1:2], upto[0:E3, 0:E3], flag[:, :], start=True,
                                 stop=True).then_inc(placed, 1)
                pe.wait_ge(spotted, 1)
                nc.tensor.matmul(c.banks[0:1, EXTRA, 8:8 + MAX_EXTRA], extra_col[0:E3, 1:2], spot[:, :],
                                 start=True, stop=True)
                nc.tensor.matmul(c.banks[0:1, EXTRA, 32:32 + MAX_EXTRA], extra_col[0:E3, 2:3], spot[:, :],
                                 start=True, stop=True)
                nc.tensor.matmul(c.banks[0:1, EXTRA, 64:65], flag[:, :], ones[0:E3, 0:1],
                                 start=True, stop=True).then_inc(placed, 1)

            @block.scalar
            def _(act):
                norm.act_take(act)
                act.wait_ge(norm.rows_done, TC)
                nc.scalar.activation(parts[:, 0, :, :], xn[:, :, :], ACT.Copy).then_inc(split_act, 1)
                for tc in range(TC):
                    act.wait_ge(negated, tc + 1)
                    nc.scalar.activation(gate[:, tc, :], top[:, tc, 0:TOPK], ACT.Exp, bias=neg_max[:, tc:tc + 1],
                                         accum_out=gate_sum[:, tc:tc + 1]).then_inc(exped, 1)

            @block.gpsimd
            def _(pool):
                nc.gpsimd.memset(ones[:, :], 1.0).then_inc(marked, 1)

            @block.vector
            def _(dve):
                chain, v = c.dve_chain, nc.vector
                for tc in range(TC):
                    norm.dve_rows(dve, tc)
                norm.dve_take(dve)
                dve.wait_ge(router_in, 32)
                dve.wait_ge(const_in, 80)
                for tc in range(TC):
                    dve.wait_ge(routed, TC)
                    chain(dve, v.tensor_tensor(logits[:, tc, :], c.banks[:, LOGIT, tc * E:(tc + 1) * E],
                                               b_router[:, :], ALU.add))
                    chain(dve, v.max(top[:, tc, :], logits[:, tc, :]))
                    v.tensor_scalar(neg_max[:, tc:tc + 1], top[:, tc, 0:1], -1.0, None, ALU.mult).then_inc(negated, 1)
                    chain(dve, v.max_index(top_i[:, tc, :], top[:, tc, :], logits[:, tc, :]))
                    chain(dve, v.tensor_copy(top_f[:, tc, :], top_i[:, tc, :]))
                for tc in range(TC):
                    dve.wait_ge(exped, tc + 1)
                    chain(dve, v.reciprocal(gate_sum[:, tc:tc + 1], gate_sum[:, tc:tc + 1]))
                    chain(dve, v.tensor_scalar(gate[:, tc, :], gate[:, tc, :], gate_sum[:, tc:tc + 1], None, ALU.mult))
                    for j in range(TOPK):
                        v.tensor_scalar(hit[:, 0, j, :], expert_no[:, :], top_f[:, tc, j:j + 1], None, ALU.is_equal)
                        last = v.tensor_scalar(hit[:, 1, j, :], expert_no[:, :], top_f[:, tc, j:j + 1],
                                               gate[:, tc, j:j + 1], ALU.is_equal, ALU.mult)
                    chain(dve, last)
                    for i, out in ((0, chosen[:, tc, 0, :]), (1, gates[:, tc, :])):
                        v.tensor_tensor(hit[:, i, 0, :], hit[:, i, 0, :], hit[:, i, 1, :], ALU.add)
                        chain(dve, v.tensor_tensor(hit[:, i, 2, :], hit[:, i, 2, :], hit[:, i, 3, :], ALU.add))
                        chain(dve, v.tensor_tensor(out, hit[:, i, 0, :], hit[:, i, 2, :], ALU.add))
                    for b in range(1, BLOCKS - 1):
                        last = v.tensor_copy(chosen[:, tc, b, :], chosen[:, tc, 0, :])
                    chain(dve, last)
                v.nop().then_inc(marked, 1)
                dve.wait_ge(counted, 1)
                for tc in range(TC):
                    chain(dve, v.tensor_tensor(rank[:, tc, :], c.banks[:, RANK, tc * E:(tc + 1) * E],
                                               chosen[:, tc, 0, :], ALU.mult))
                    v.tensor_scalar(rank[:, tc, :], rank[:, tc, :], -1.0, None, ALU.add)
                v.tensor_copy(gatesT[:, :], c.banks[0:E, TURN, 0:T]).then_inc(gates_turned, 1)
                v.tensor_tensor(flag[:, :], c.banks[0:E3, EXTRA, 0:1], extra_col[0:E3, 0:1], ALU.is_gt).then_inc(
                    flagged, 1)
                dve.wait_ge(flagged, 1)
                dve.wait_ge(placed, 1)
                chain(dve, v.tensor_tensor(place[:, :], c.banks[0:E3, EXTRA, 1:2], flag[:, :], ALU.mult))
                chain(dve, v.tensor_scalar(place[:, :], place[:, :], -1.0, None, ALU.add))
                v.tensor_scalar(spot[:, :], number[0:E3, 0:MAX_EXTRA], place[:, :], None, ALU.is_equal).then_inc(
                    spotted, 1)
                dve.wait_ge(placed, 2)
                dve.wait_ge(list_in, 16)
                v.tensor_copy(work_list[:, EXPERT_AT + E:EXPERT_AT + E + MAX_EXTRA],
                              c.banks[0:1, EXTRA, 8:8 + MAX_EXTRA])
                v.tensor_copy(work_list[:, BLOCK_AT + E:BLOCK_AT + E + MAX_EXTRA],
                              c.banks[0:1, EXTRA, 32:32 + MAX_EXTRA])
                v.tensor_scalar(work_list[:, COUNT:COUNT + 1], c.banks[0:1, EXTRA, 64:65], float(E), None, ALU.add)
                dve.wait_ge(split_act, 1)
                for tc in range(TC):
                    chain(dve, v.tensor_tensor(xn[:, tc, :], xn[:, tc, :], parts[:, 0, tc, :], ALU.subtract))
                    chain(dve, v.tensor_copy(parts[:, 1, tc, :], xn[:, tc, :]))
                    v.tensor_tensor(parts[:, 2, tc, :], xn[:, tc, :], parts[:, 1, tc, :], ALU.subtract)

        xsT = sb("xsT", [P, KC, CAP])
        pick = sb("pick", [P, TC, CAP], BF16)
        spread = sb("spread", [P, TC, 2 * CAP])
        spreadT = sb("spreadT", [2 * CAP, T])
        glu = sb("glu", [P, BANK])
        sig = sb("sig", [P, BANK])
        lin = sb("lin", [P, BANK])
        act_h = sb("act_h", [P, BANK])
        hT = sb("hT", [P, BANK])
        y = sb("e_y", [P, BANK])
        GLU, LIN, DOWN, TURN, SUM = 0, 1, 2, 3, 4
        picked, spread_ready, spread_turned, spreadT_ready = (sem(n) for n in (
            "picked", "spread_ready", "spread_turned", "spreadT_ready"))
        gathered, xs_ready, up_used, up_done, halves_read = (sem(n) for n in (
            "gathered", "xs_ready", "up_used", "up_done", "halves_read"))
        glu_ready, sig_ready, h_ready, h_turned, hT_ready = (sem(n) for n in (
            "glu_ready", "sig_ready", "h_ready", "h_turned", "hT_ready"))
        down_used, down_done, y_ready, bias_used, zeroed, summed = (sem(n) for n in (
            "down_used", "down_done", "e_y_ready", "bias_used", "zeroed", "summed"))

        def listed_at(eng, at, top_value):
            return eng.value_load(work_list[0:1, bass.ds(at, 1)], min_val=0, max_val=top_value)

        def count(eng):
            return eng.value_load(work_list[0:1, 0:1], min_val=E, max_val=E + MAX_EXTRA)

        with nc.Block() as block:
            @block.sync
            def _(sp):
                items = count(sp)
                with sp.Fori(1, items) as i:
                    e = listed_at(sp, i + EXPERT_AT, E - 1)
                    sp.wait_ge(bias_used, i)
                    load_bias(sp, e)
                    for k in range(KC):
                        sp.wait_ge(up_used, i * KC + (k + 1 - KC))
                        load_up(sp, e, k)
                    for j in range(KC // 2):
                        sp.wait_ge(down_used, i * (KC // 2) + (j + 1 - KC // 2))
                        load_down(sp, e, j)

            @block.tensor
            def _(pe):
                def gather(n):
                    pe.wait_ge(picked, n + 1)
                    for k in range(KC):
                        out = c.banks[:, TURN, k * CAP:(k + 1) * CAP]
                        ins = matmuls(nc, out,
                                      [parts[:, a, tc, k * P:(k + 1) * P] for tc in range(TC) for a in range(3)],
                                      [pick[:, tc, :] for tc in range(TC) for a in range(3)])
                    ins.then_inc(gathered, 1)

                def combine(stop):
                    for tc in range(TC):
                        for h in range(2):
                            half = slice(CAP * h, CAP * (h + 1))
                            ins = nc.tensor.matmul(c.banks[:, SUM + 2 * tc + h, :],
                                                   spreadT[half, tc * P:(tc + 1) * P], y[half, :],
                                                   start=False, stop=stop)
                    return ins

                items = count(pe)
                for tc in range(TC):
                    for h in range(2):
                        nc.tensor.matmul(c.banks[:, SUM + 2 * tc + h, :], gatesT[:, tc * P:(tc + 1) * P],
                                         b_down[:, h * BANK:(h + 1) * BANK], start=True, stop=False)
                pe.wait_ge(zeroed, 1)
                pe.nop().then_inc(spread_turned, 1)
                gather(0)
                with pe.Fori(0, items) as i:
                    pe.wait_ge(xs_ready, i + 1)
                    pe.wait_ge(halves_read, i + 1)
                    pe.wait_ge(bias_in, i * 16 + 16)
                    quarters = [(bank, h, bank * D + h * BANK) for bank in (GLU, LIN) for h in range(2)]
                    for bank, h, at in quarters:
                        ins = nc.tensor.matmul(c.banks[CAP * h:CAP * (h + 1), bank, :], ones[0:1, 0:CAP],
                                               bias[:, at:at + BANK], start=True, stop=False)
                    ins.then_inc(bias_used, 1)
                    for k in range(KC):
                        pe.wait_ge(up_in[k], i * 16 + 16)
                        for bank, h, at in quarters:
                            ins = nc.tensor.matmul(c.banks[CAP * h:CAP * (h + 1), bank, :], xsT[:, k, :],
                                                   up_slot[k][:, at:at + BANK], start=False, stop=k == KC - 1)
                        ins.then_inc(up_used, 1)
                    pe.wait_ge(y_ready, i + 1)
                    pe.wait_ge(spreadT_ready, i + 1)
                    combine(False)
                    pe.wait_ge(spread_ready, i + 1)
                    for tc in range(TC):
                        ins = nc.tensor.transpose(c.banks[:, DOWN, tc * P:(tc + 1) * P], spread[:, tc, :],
                                                  c.ident[:, :])
                    ins.then_inc(spread_turned, 1)
                    pe.wait_ge(hT_ready, i + 1)
                    gather(i + 1)
                    pe.wait_ge(h_ready, i + 1)
                    pe.wait_ge(xs_ready, i + 2)
                    for j in range(KC // 2):
                        ins = nc.tensor.transpose(c.banks[:, TURN, j * P:(j + 1) * P],
                                                  act_h[:, j * P:(j + 1) * P], c.ident[:, :])
                    ins.then_inc(h_turned, 1)
                    pe.wait_ge(hT_ready, i + 2)
                    pe.wait_ge(spreadT_ready, i + 2)
                    for k in range(KC):
                        at = (k % 4) * P + (k // 4) * CAP
                        if k % 2 == 0:
                            pe.wait_ge(down_in[k // 2], i * 16 + 16)
                        for h in range(2):
                            ins = nc.tensor.matmul(c.banks[CAP * h:CAP * (h + 1), DOWN, :], hT[:, at:at + CAP],
                                                   down_slot[k // 2][:, k % 2, h * BANK:(h + 1) * BANK],
                                                   start=k == 0, stop=k == KC - 1)
                        if k % 2:
                            ins.then_inc(down_used, 1)
                pe.wait_ge(y_ready, items + 1)
                pe.wait_ge(spreadT_ready, items + 1)
                combine(True).then_inc(summed, 1)

            @block.scalar
            def _(act):
                items = count(act)
                for s in (spreadT_ready, hT_ready, y_ready):
                    act.nop().then_inc(s, 1)
                with act.Fori(0, items) as i:
                    act.wait_ge(glu_ready, i + 1)
                    nc.scalar.activation(sig[:, :], glu[:, :], ACT.Sigmoid, scale=ALPHA).then_inc(sig_ready, 1)
                    act.wait_ge(spread_turned, i + 2)
                    nc.scalar.activation(spreadT[:, :], c.banks[:, DOWN, 0:T], ACT.Copy).then_inc(spreadT_ready, 1)
                    act.wait_ge(h_turned, i + 1)
                    nc.scalar.activation(hT[:, :], c.banks[:, TURN, :], ACT.Copy).then_inc(hT_ready, 1)
                    act.wait_ge(down_used, i * (KC // 2) + KC // 2)
                    nc.scalar.activation(y[:, :], c.banks[:, DOWN, :], ACT.Copy).then_inc(y_ready, 1)

            @block.vector
            def _(dve):
                v = nc.vector

                def pick_item(e, b):
                    for tc in range(TC):
                        ins = v.tensor_scalar(pick[:, tc, :], number[:, bass.ds(b * (2 * CAP), CAP)],
                                              rank[:, tc, bass.ds(e, 1)], None, ALU.is_equal)
                    ins.then_inc(picked, 1)

                def take_gathered():
                    v.tensor_tensor(xsT[:, :, :], c.banks[:, TURN, :].rearrange("p (k s) -> p k s", k=KC),
                                    c.col("g_ffn", 0, KC).unsqueeze(2).to_broadcast([P, KC, CAP]),
                                    ALU.mult).then_inc(xs_ready, 1)

                items = count(dve)
                v.memset(y[:, :], 0.0)
                v.memset(spreadT[:, :], 0.0).then_inc(zeroed, 1)
                v.nop().then_inc(halves_read, 1)
                pick_item(0, 0)
                dve.wait_ge(gathered, 1)
                take_gathered()
                with dve.Fori(0, items) as i:
                    e = listed_at(dve, i + EXPERT_AT, E - 1)
                    b = listed_at(dve, i + BLOCK_AT, BLOCKS - 1)
                    dve.wait_ge(spread_turned, i + 1)
                    for tc in range(TC):
                        ins = v.tensor_scalar(spread[:, tc, :], number[:, bass.ds(b * (2 * CAP), 2 * CAP)],
                                              rank[:, tc, bass.ds(e, 1)], gates[:, tc, bass.ds(e, 1)],
                                              ALU.is_equal, ALU.mult)
                    ins.then_inc(spread_ready, 1)
                    dve.wait_ge(gathered, i + 1)
                    pick_item(listed_at(dve, i + (EXPERT_AT + 1), E - 1), listed_at(dve, i + (BLOCK_AT + 1),
                                                                                   BLOCKS - 1))
                    dve.wait_ge(up_used, i * KC + KC)
                    v.tensor_scalar(glu[:, :], c.banks[:, GLU, :], LIMIT, None, ALU.min).then_inc(glu_ready, 1)
                    v.tensor_scalar(lin[:, :], c.banks[:, LIN, :], LIMIT, -LIMIT, ALU.min, ALU.max).then_inc(
                        halves_read, 1)
                    dve.wait_ge(glu_ready, i + 1)
                    dve.wait_ge(halves_read, i + 2)
                    v.scalar_tensor_tensor(lin[:, :], lin[:, :], 1.0, glu[:, :], ALU.add, ALU.mult)
                    dve.drain()
                    dve.wait_ge(sig_ready, i + 1)
                    v.tensor_tensor(act_h[:, :], lin[:, :], sig[:, :], ALU.mult).then_inc(h_ready, 1)
                    dve.wait_ge(gathered, i + 2)
                    take_gathered()
                dve.wait_ge(summed, 1)
                for tc in range(TC):
                    for h in range(2):
                        s = c.x[:, tc, h * BANK:(h + 1) * BANK]
                        v.tensor_tensor(s, s, c.banks[:, SUM + 2 * tc + h, :], ALU.add)


def embedding_stage(c):
    nc, d = c.nc, c.dram
    PK = PLE // P
    with ExitStack() as es:
        def sb(name, shape, dt=F32):
            return es.enter_context(nc.sbuf_tensor(name, shape, dt))

        def sem(name):
            return c.semaphore(name)

        c.open_ring(es, 7)
        xn = sb("p_xn", [P, TC, D])
        pT = sb("pT", [P, PK, T])
        w_proj = sb("w_proj", [P, PK, D])
        opened = sb("opened", [P, 2, BANK])
        part = sb("part", [P, BANK])
        w_gate = c.ring[:, 0:KC * D].rearrange("p (k n) -> p k n", k=KC)
        norm = Norm(c, es, "ple_norm", "g_ple", xn)
        gate_in, proj_in = [sem(f"gate_in{h}") for h in range(2)], sem("proj_in")
        gate_done, proj_done, sig_done, sig_used = (sem(n) for n in (
            "gate_done", "proj_done", "p_sig_done", "p_sig_used"))
        with nc.Block() as block:
            @block.sync
            def _(sp):
                sp.dma_start(pT[:, :, :], d["pT"].rearrange("(k p) t -> p k t", p=P)).then_inc(proj_in, 16)
                sp.dma_start(w_proj[:, :, :], d["w_ple_proj"].rearrange("(k p) n -> p k n", p=P)).then_inc(
                    proj_in, 16)
                w = d["w_ple_gate"].rearrange("(k p) n -> p k n", p=P)
                for h in range(2):
                    sp.dma_start(w_gate[:, 4 * h:4 * h + 4, :], w[:, 4 * h:4 * h + 4, :]).then_inc(gate_in[h], 16)

            @block.tensor
            def _(pe):
                pe.wait_ge(proj_in, 32)
                for tc in range(TC):
                    for n in range(2):
                        matmuls(nc, c.banks[:, 4 + 2 * tc + n, :],
                                [pT[:, k, tc * P:(tc + 1) * P] for k in range(PK)],
                                [w_proj[:, k, n * BANK:(n + 1) * BANK] for k in range(PK)]).then_inc(proj_done, 1)
                norm.pe_turn(pe)
                norm.wait(pe)
                for h in range(2):
                    pe.wait_ge(gate_in[h], 16)
                for tc in range(TC):
                    for n in range(2):
                        matmuls(nc, c.banks[:, 2 * tc + n, :],
                                [c.xT[:, k, tc * P:(tc + 1) * P] for k in range(KC)],
                                [w_gate[:, k, n * BANK:(n + 1) * BANK] for k in range(KC)]).then_inc(gate_done, 1)

            @block.scalar
            def _(act):
                norm.act_take(act)
                for i in range(2 * TC):
                    act.wait_ge(gate_done, i + 1)
                    if i >= 2:
                        act.wait_ge(sig_used, i - 1)
                    nc.scalar.activation(opened[:, i % 2, :], c.banks[:, i, :], ACT.Sigmoid).then_inc(sig_done, 1)

            @block.vector
            def _(dve):
                for tc in range(TC):
                    norm.dve_rows(dve, tc)
                norm.dve_take(dve)
                dve.wait_ge(proj_done, 4)
                for i in range(2 * TC):
                    dve.wait_ge(sig_done, i + 1)
                    c.dve_chain(dve, nc.vector.tensor_tensor(part[:, :], c.banks[:, 4 + i, :], opened[:, i % 2, :],
                                                             ALU.mult))
                    s = c.x[:, i // 2, (i % 2) * BANK:(i % 2 + 1) * BANK]
                    nc.vector.tensor_tensor(s, s, part[:, :], ALU.add).then_inc(sig_used, 1)
                    dve.wait_ge(sig_used, i + 1)


def gating_stage(c):
    nc, d = c.nc, c.dram
    NB = SGU // BANK
    FK = SGU // P
    with ExitStack() as es:
        def sb(name, shape, dt=F32):
            return es.enter_context(nc.sbuf_tensor(name, shape, dt))

        def sem(name):
            return c.semaphore(name)

        c.open_ring(es, 7)
        xn = sb("g_xn", [P, TC, D])
        v_t = sb("v_t", [P, TC, SGU])
        uT = sb("uT", [P, FK, T])
        w_sT = sb("w_sT_sb", [P, GROUPS, P])
        b_v = sb("b_v_sb", [P, SGU])
        ln_g = sb("ln_g_sb", [P, SGU])
        ln_b = sb("ln_b_sb", [P, SGU])
        b_s = b_v[:, :].rearrange("p (g i) -> p g i", g=GROUPS)
        sums = sb("g_sums", [P, TC, NB])
        mom = sb("g_mom", [P, TC, 3])
        centred = xn[:, :, :].rearrange("p c n -> p (c n)")
        slots = [c.ring[:, s * 4096:(s + 1) * 4096] for s in range(7)]
        norm = Norm(c, es, "sgu_norm", "n_mix0", xn)
        w_seg = [sem(f"g_w{s}") for s in range(2 * NB)]
        out_in = [sem(f"g_out_in{s}") for s in range(4)]
        rows_in, b_s_in, ws_in, masked = (sem(n) for n in ("g_rows_in", "b_s_in", "ws_in", "ws_masked"))
        v_done, v_biased, v_gelu, v_centred, v_square, v_ready = (sem(n) for n in (
            "v_done", "v_biased", "v_gelu", "v_centred", "v_square", "v_ready"))
        u_done, u_ready, s_done, s_read, y_ready, out_done = (sem(n) for n in (
            "u_done", "u_ready", "gs_done", "gs_read", "g_y_ready", "g_out_done"))
        w_in = d["sgu_in"].rearrange("(k p) n -> p k n", p=P)
        w_out = d["sgu_out"].rearrange("(k p) n -> p k n", p=P)
        col_of = [SGU + j * BANK for j in range(NB)] + [j * BANK for j in range(NB)]

        def block_slot(j):
            return slots[j % 7].rearrange("p (k n) -> p k n", k=KC)

        def out_slot(q):
            return slots[1 + q].rearrange("p (k n) -> p k n", k=4)

        with nc.Block() as block:
            @block.sync
            def _(sp):
                for j in range(2 * NB - 1):
                    sp.dma_start(block_slot(j), w_in[:, :, col_of[j]:col_of[j] + BANK]).then_inc(w_seg[j], 16)
                    if j == 0:
                        sp.dma_start(b_v[:, :], rows_to_all(c.row("b_v"))).then_inc(rows_in, 16)
                        sp.dma_start(ln_g[:, :], rows_to_all(c.row("ln_g"))).then_inc(rows_in, 16)
                        sp.dma_start(ln_b[:, :], rows_to_all(c.row("ln_b"))).then_inc(rows_in, 16)
                        sp.dma_start(w_sT[:, :, :].rearrange("p g i -> p (g i)"), d["w_sT"]).then_inc(ws_in, 16)
                last = 2 * NB - 1
                sp.wait_ge(v_done, TC)
                sp.dma_start(block_slot(last), w_in[:, :, col_of[last]:col_of[last] + BANK]).then_inc(
                    w_seg[last], 16)
                for q in range(4):
                    if q < 3:
                        sp.wait_ge(v_done, TC * (q + 2))
                    else:
                        sp.wait_ge(u_done, 2)
                    sp.dma_start(out_slot(q), w_out[:, 4 * q:4 * q + 4, :]).then_inc(out_in[q], 16)
                    if q == 2:
                        sp.wait_ge(v_biased, NB * TC)
                        sp.dma_start(b_v[:, :], rows_to_all(c.row("b_s"))).then_inc(b_s_in, 16)

            @block.tensor
            def _(pe):
                norm.pe_turn(pe)
                norm.wait(pe)
                for j in range(NB):
                    pe.wait_ge(w_seg[j], 16)
                    for tc in range(TC):
                        matmuls(nc, c.banks[:, j * TC + tc, :],
                                [c.xT[:, k, tc * P:(tc + 1) * P] for k in range(KC)],
                                [block_slot(j)[:, k, :] for k in range(KC)]).then_inc(v_done, 1)
                for f in range(FK):
                    j = NB + f // 4
                    if f % 4 == 0:
                        pe.wait_ge(w_seg[j], 16)
                    if f % 2 == 0:
                        pe.wait_ge(v_biased, f // 2 + 1)
                    at = (f % 4) * P
                    ins = matmuls(nc, c.banks[:, f // 2, (f % 2) * T:(f % 2 + 1) * T],
                                  [block_slot(j)[:, k, at:at + P] for k in range(KC)],
                                  [c.xT[:, k, :] for k in range(KC)])
                    if f % 2:
                        ins.then_inc(u_done, 1)
                pe.wait_ge(masked, 1)
                pe.wait_ge(v_ready, TC)
                for g in range(GROUPS):
                    if g % 2 == 0:
                        pe.wait_ge(u_ready, g + 2)
                    for tc in range(TC):
                        at = (g % 2) * T + tc * P
                        ins = nc.tensor.matmul(c.banks[:, g // 2, at:at + P], v_t[:, tc, g * P:(g + 1) * P],
                                               w_sT[:, g, :], start=True, stop=True)
                    if g % 2:
                        ins.then_inc(s_done, 1)
                pe.wait_ge(y_ready, GROUPS // 2)
                for q in range(4):
                    pe.wait_ge(out_in[q], 16)
                for tc in range(TC):
                    for n in range(2):
                        matmuls(nc, c.banks[:, 2 * tc + n, :],
                                [uT[:, f, tc * P:(tc + 1) * P] for f in range(FK)],
                                [out_slot(f // 4)[:, f % 4, n * BANK:(n + 1) * BANK] for f in range(FK)]).then_inc(
                                    out_done, 1)

            @block.scalar
            def _(act):
                norm.act_take(act)
                for j in range(NB):
                    for tc in range(TC):
                        act.wait_ge(v_biased, j * TC + tc + 1)
                        s = v_t[:, tc, j * BANK:(j + 1) * BANK]
                        nc.scalar.activation(s, s, ACT.Gelu, accum_out=sums[:, tc, j:j + 1]).then_inc(v_gelu, 1)
                act.wait_ge(norm.turned, 4)
                for tc in range(TC):
                    act.wait_ge(v_centred, tc + 1)
                    act.wait_ge(v_square, tc)
                    nc.scalar.activation(centred, v_t[:, tc, :], ACT.Square, bias=mom[:, tc, 0:1],
                                         accum_out=mom[:, tc, 1:2]).then_inc(v_square, 1)
                for f in range(FK):
                    act.wait_ge(u_done, f // 2 + 1)
                    nc.scalar.activation(uT[:, f, :], c.banks[:, f // 2, (f % 2) * T:(f % 2 + 1) * T], ACT.Gelu,
                                         bias=c.col("b_u", f)).then_inc(u_ready, 1)

            @block.gpsimd
            def _(pool):
                pool.wait_ge(ws_in, 16)
                nc.gpsimd.memset(w_sT[P // 2:P, :, 0:P // 2], 0.0).then_inc(masked, 1)

            @block.vector
            def _(dve):
                chain, v = c.dve_chain, nc.vector
                for tc in range(TC):
                    norm.dve_rows(dve, tc)
                norm.dve_take(dve)
                dve.wait_ge(rows_in, 48)
                for j in range(NB):
                    for tc in range(TC):
                        dve.wait_ge(v_done, j * TC + tc + 1)
                        v.tensor_tensor(v_t[:, tc, j * BANK:(j + 1) * BANK], c.banks[:, j * TC + tc, :],
                                        b_v[:, j * BANK:(j + 1) * BANK], ALU.add).then_inc(v_biased, 1)
                for tc in range(TC):
                    dve.wait_ge(v_gelu, (NB - 1) * TC + tc + 1)
                    chain(dve, v.tensor_reduce(mom[:, tc, 0:1], sums[:, tc, :], AX.X, ALU.add))
                    v.tensor_scalar(mom[:, tc, 0:1], mom[:, tc, 0:1], -1.0 / SGU, None, ALU.mult).then_inc(
                        v_centred, 1)
                for tc in range(TC):
                    dve.wait_ge(v_square, tc + 1)
                    var = mom[:, tc, 1:2]
                    c.dve_rstd(dve, v.tensor_scalar(var, var, 1.0 / SGU, LN_EPS, ALU.mult, ALU.add), var)
                    s = v_t[:, tc, :]
                    chain(dve, v.tensor_scalar(s, s, mom[:, tc, 0:1], var, ALU.add, ALU.mult))
                    chain(dve, v.tensor_tensor(s, s, ln_g[:, :], ALU.mult))
                    v.tensor_tensor(s, s, ln_b[:, :], ALU.add).then_inc(v_ready, 1)
                dve.wait_ge(b_s_in, 16)
                for b in range(GROUPS // 2):
                    dve.wait_ge(s_done, b + 1)
                    bank = c.banks[:, b, :].rearrange("p (g c i) -> p g c i", g=2, c=TC)
                    chain(dve, v.tensor_tensor(bank, bank, b_s[:, 2 * b:2 * b + 2, :].unsqueeze(2).to_broadcast(
                        [P, 2, TC, P]), ALU.add))
                    s = uT[:, 2 * b:2 * b + 2, :].rearrange("p g t -> p (g t)")
                    v.tensor_tensor(s, c.banks[:, b, :], s, ALU.mult).then_inc(y_ready, 1)
                for i in range(2 * TC):
                    dve.wait_ge(out_done, i + 1)
                    s = c.x[:, i // 2, (i % 2) * BANK:(i % 2 + 1) * BANK]
                    v.tensor_tensor(s, s, c.banks[:, i, :], ALU.add)


def ffn_stage(c, layer):
    nc, d = c.nc, c.dram
    NB = FF // BANK
    FC = BANK // P
    with ExitStack() as es:
        def sb(name, shape, dt=F32):
            return es.enter_context(nc.sbuf_tensor(f"f{layer}_{name}", shape, dt))

        def sem(name):
            return c.semaphore(f"f{layer}_{name}")

        c.open_ring(es, 4)
        xn = sb("xn", [P, TC, D])
        xT_hi, xT_lo = sb("xT_hi", [P, KC, T], F32R), sb("xT_lo", [P, KC, T], F32R)
        w1_hi, w1_lo = sb("w1_hi", [P, FC, KC, P], F32R), sb("w1_lo", [P, FC, KC, P], F32R)
        w2_hi, w2_lo = sb("w2_hi", [P, FC, D], F32R), sb("w2_lo", [P, FC, D], F32R)
        relu = sb("relu", [P, FC, T])
        square = sb("square", [P, FC, T])
        h_hi, h_lo = sb("h_hi", [P, FC, T], F32R), sb("h_lo", [P, FC, T], F32R)
        norm = Norm(c, es, f"ffn{layer}_norm", f"n_ffn{layer}", xn)
        w1_in, w2_in = [[sem(f"w{w}_in{s}") for s in range(2)] for w in (1, 2)]
        x_hi_ready, x_lo_ready = sem("x_hi_ready"), sem("x_lo_ready")
        w1_high, w1_low, w2_high, w2_low = (sem(n) for n in ("w1_high", "w1_low", "w2_high", "w2_low"))
        up_done, relu_done, h_high, h_low, down_done = (sem(n) for n in (
            "up_done", "relu_done", "h_high", "h_low", "down_done"))
        w1_raw = [c.ring[:, s * 4096:(s + 1) * 4096].rearrange("p (k n) -> p k n", k=KC) for s in range(2)]
        w2_raw = [c.ring[:, (2 + s) * 4096:(3 + s) * 4096].rearrange("p (k n) -> p k n", k=FC) for s in range(2)]
        w1 = d["ffn_w1"][layer * D:(layer + 1) * D, :].rearrange("(k p) n -> p k n", p=P)
        w2 = d["ffn_w2"][layer * FF:(layer + 1) * FF, :]
        OUT = 4

        def turns(chunk_work, split1, split2):
            for j in range(FC):
                chunk_work(j)
                split1(j)
                if j >= 2:
                    split2(j - 2)
            split2(FC - 2)
            split2(FC - 1)

        def blocks(eng, body):
            with eng.Fori(0, NB // 2 - 1) as i:
                for s in range(2):
                    body(i, s, False)
            for s in range(2):
                body(NB // 2 - 1, s, s == 1)

        with nc.Block() as block:
            @block.sync
            def _(sp):
                def load1(s, b):
                    sp.dma_start(w1_raw[s], w1[:, :, bass.ds(b * BANK, BANK)]).then_inc(w1_in[s], 16)

                def load2(s, b):
                    sp.dma_start(w2_raw[s], w2[bass.ds(b * BANK, BANK), :].rearrange(
                        "(k p) n -> p k n", p=P)).then_inc(w2_in[s], 16)

                for s in range(2):
                    load1(s, s)
                    load2(s, s)
                with sp.Fori(1, NB // 2) as i:
                    for s in range(2):
                        sp.wait_ge(w1_low, i * (2 * FC) + (s - 1) * FC)
                        load1(s, i * 2 + s)
                        sp.wait_ge(w2_low, i * (2 * FC) + (s - 1) * FC)
                        load2(s, i * 2 + s)

            @block.tensor
            def _(pe):
                for i in range(2 * TC):
                    nc.tensor.matmul(c.banks[:, OUT + i, :], c.ident[:, :],
                                     c.x[:, i // 2, (i % 2) * BANK:(i % 2 + 1) * BANK], start=True, stop=False)
                norm.pe_turn(pe)
                pe.nop().then_inc(down_done, FC)
                pe.wait_ge(x_lo_ready, 1)

                def body(i, s, last):
                    chunks = i * (2 * FC) + s * FC

                    def up(j):
                        pe.wait_ge(w1_low, chunks + (j + 1))
                        pe.wait_ge(relu_done, chunks + (j + 1))
                        for k in range(KC):
                            for n, (w, x) in enumerate(((w1_hi, xT_hi), (w1_hi, xT_lo), (w1_lo, xT_hi))):
                                ins = nc.tensor.matmul(c.banks[:, j, 0:T], w[:, j, k, :], x[:, k, :],
                                                       start=k == 0 and n == 0, stop=k == KC - 1 and n == 2)
                        ins.then_inc(up_done, 1)

                    def down(j):
                        pe.wait_ge(h_low, chunks + (j + 1 + FC))
                        pe.wait_ge(w2_low, chunks + (j + 1))
                        for tc in range(TC):
                            for n, (h, w) in enumerate(((h_hi, w2_hi), (h_hi, w2_lo), (h_lo, w2_hi))):
                                for o in range(2):
                                    ins = nc.tensor.matmul(
                                        c.banks[:, OUT + 2 * tc + o, :], h[:, j, tc * P:(tc + 1) * P],
                                        w[:, j, o * BANK:(o + 1) * BANK], start=False,
                                        stop=last and j == FC - 1 and n == 2)
                        ins.then_inc(down_done, 1)

                    up(0)
                    up(1)
                    down(0)
                    up(2)
                    down(1)
                    up(3)
                    down(2)
                    down(3)

                blocks(pe, body)

            @block.scalar
            def _(act):
                norm.act_take(act)
                norm.wait(act)
                nc.scalar.activation(xT_hi[:, :, :], c.xT[:, :, :], ACT.Copy).then_inc(x_hi_ready, 1)

                def high1(s, count, j):
                    act.wait_ge(w1_in[s], count)
                    nc.scalar.activation(w1_hi[:, j, :, :], w1_raw[s][:, :, j * P:(j + 1) * P],
                                         ACT.Copy).then_inc(w1_high, 1)

                def high2(s, count, j):
                    act.wait_ge(w2_in[s], count)
                    nc.scalar.activation(w2_hi[:, j, :], w2_raw[s][:, j, :], ACT.Copy).then_inc(w2_high, 1)

                for j in range(FC):
                    high1(0, 16, j)
                for j in range(FC):
                    high2(0, 16, j)
                act.nop().then_inc(relu_done, FC)

                def body(i, s, last):
                    chunks = i * (2 * FC) + s * FC
                    nxt, count = 1 - s, i * 16 + (16 + 16 * s)

                    def work(j):
                        act.wait_ge(up_done, chunks + (j + 1))
                        act.wait_ge(h_low, chunks + (j + 1))
                        nc.scalar.activation(relu[:, j, :], c.banks[:, j, 0:T], ACT.Relu).then_inc(relu_done, 1)
                        act.wait_ge(relu_done, chunks + (j + 1 + FC))
                        act.wait_ge(down_done, chunks + (j + 1))
                        nc.scalar.activation(h_hi[:, j, :], relu[:, j, :], ACT.Square).then_inc(h_high, 1)

                    def split1(j):
                        if not last:
                            high1(nxt, count, j)

                    def split2(j):
                        if not last:
                            act.wait_ge(down_done, chunks + (j + 1 + FC))
                            high2(nxt, count, j)

                    turns(work, split1, split2)

                blocks(act, body)

            @block.vector
            def _(dve):
                vec = nc.vector
                for tc in range(TC):
                    norm.dve_rows(dve, tc)
                norm.dve_take(dve)
                dve.wait_ge(x_hi_ready, 1)
                vec.tensor_tensor(xT_lo[:, :, :], c.xT[:, :, :], xT_hi[:, :, :], ALU.subtract).then_inc(x_lo_ready, 1)

                def low1(s, count, j):
                    dve.wait_ge(w1_high, count)
                    vec.tensor_tensor(w1_lo[:, j, :, :], w1_raw[s][:, :, j * P:(j + 1) * P], w1_hi[:, j, :, :],
                                      ALU.subtract).then_inc(w1_low, 1)

                def low2(s, count, j):
                    dve.wait_ge(w2_high, count)
                    vec.tensor_tensor(w2_lo[:, j, :], w2_raw[s][:, j, :], w2_hi[:, j, :],
                                      ALU.subtract).then_inc(w2_low, 1)

                for j in range(FC):
                    low1(0, j + 1, j)
                for j in range(FC):
                    low2(0, j + 1, j)
                dve.nop().then_inc(h_low, FC)

                def body(i, s, last):
                    chunks = i * (2 * FC) + s * FC
                    nxt = 1 - s

                    def work(j):
                        dve.wait_ge(relu_done, chunks + (j + 1 + FC))
                        vec.tensor_tensor(square[:, j, :], relu[:, j, :], relu[:, j, :], ALU.mult)
                        dve.drain()
                        dve.wait_ge(h_high, chunks + (j + 1))
                        vec.tensor_tensor(h_lo[:, j, :], square[:, j, :], h_hi[:, j, :], ALU.subtract).then_inc(
                            h_low, 1)

                    def split1(j):
                        if not last:
                            low1(nxt, chunks + (FC + j + 1), j)

                    def split2(j):
                        if not last:
                            low2(nxt, chunks + (FC + j + 1), j)

                    turns(work, split1, split2)

                blocks(dve, body)
                dve.wait_ge(down_done, (NB + 1) * FC)
                for i in range(2 * TC):
                    vec.tensor_copy(c.x[:, i // 2, (i % 2) * BANK:(i % 2 + 1) * BANK], c.banks[:, OUT + i, :])


def rwkv_stage(c):
    nc, d = c.nc, c.dram
    H2 = 2 * HD
    RP = RH // 2
    NCH = T // CH
    J = P // CH
    DECAY = float(np.exp(-0.5))
    UNIT = TC * D
    LORA = 64
    with ExitStack() as es:
        def sb(name, shape, dt=F32):
            return es.enter_context(nc.sbuf_tensor(f"w_{name}", shape, dt))

        def sem(name):
            return c.semaphore(f"w_{name}")

        RING = 14
        c.open_ring(es, 7)
        pool_t = sb("pool", [P, 8 * UNIT])

        def unit(i, n=1):
            t, i = (c.ring, i) if i < RING else (pool_t, i - RING)
            return t[:, i * UNIT:(i + n) * UNIT]

        def feat(i):
            return unit(i).rearrange("p (k t) -> p k t", k=KC)

        def tok(i):
            return unit(i).rearrange("p (c n) -> p c n", c=TC)

        xn, xx, xs = tok(14), feat(15), [feat(16), feat(14)]
        r, k, v, a, sig, g = feat(12), feat(13), tok(17), feat(18), feat(19), tok(20)
        w_rkv_sb = [unit(4 * i, 4).rearrange("p (k n) -> p k n", k=KC) for i in range(3)]
        lora = unit(12, 2)
        w_la = lora[:, 0:512].rearrange("p (k n) -> p k n", k=KC)
        a_la = lora[:, 512:1024].rearrange("p (k n) -> p k n", k=KC)
        g_la = lora[:, 1024:2048].rearrange("p (k n) -> p k n", k=KC)
        wa_lb = lora[:, 2048:3072]
        g_lb = lora[:, 3072:4096]
        hid = sb("hid", [P, 2, T])
        head_of = sb("head_of", [P, RP, RH])
        head_to = sb("head_to", [RH, RP, P])
        bonus = sb("bonus", [P, TC, RH])
        last_w = sb("last_w", [P, RP, NCH])
        moments = sb("moments", [P, 2, RH])

        norm = Norm(c, es, "rwkv_norm", "n_mix1", xn)
        w_in = [sem(f"in{i}") for i in range(3)]
        lora_in, sel_in = sem("lora_in"), sem("sel_in")
        mixed, mix_used = sem("mixed"), sem("mix_used")
        p_done, took_a, took_v = sem("p_done"), sem("took_a"), sem("took_v")
        ORDER = (MIX_W, MIX_A, MIX_G, MIX_R, MIX_K, MIX_V)

        with nc.Block() as block:
            @block.sync
            def _(sp):
                for dst, name in ((w_la, "w_la"), (a_la, "a_la"), (g_la, "g_la")):
                    sp.dma_start(dst, d[name].rearrange("(k p) n -> p k n", p=P)).then_inc(lora_in, 16)
                sp.dma_start(wa_lb[0:LORA, :], d["w_lb"]).then_inc(lora_in, 16)
                sp.dma_start(wa_lb[LORA:P, :], d["a_lb"]).then_inc(lora_in, 16)
                sp.dma_start(g_lb, d["g_lb"]).then_inc(lora_in, 16)
                for i in range(3):
                    sp.dma_start(w_rkv_sb[i], d["w_rkv"][i * D:(i + 1) * D, :].rearrange(
                        "(k p) n -> p k n", p=P)).then_inc(w_in[i], 16)
                sp.dma_start(head_of[:, :, :].rearrange("p c h -> p (c h)"), d["head_of"]).then_inc(sel_in, 16)
                sp.dma_start(head_to[:, :, :].rearrange("p c h -> p (c h)"), d["head_to"]).then_inc(sel_in, 16)

            TAKER = "AVA" + "AAAA" + "AAAA" + "VVVV" + "AVAV" + "AVAV" + "AVAV"

            def taken(eng, n):
                if n >= 0:
                    eng.wait_ge(took_a, TAKER[:n + 1].count("A"))
                    if TAKER[:n + 1].count("V"):
                        eng.wait_ge(took_v, TAKER[:n + 1].count("V"))

            @block.tensor
            def _(pe):
                norm.pe_turn(pe)
                norm.wait(pe)
                at = [0]

                def bank(n):
                    return c.banks[:, n % 8, :]

                def start(n):
                    taken(pe, n - 8)
                    at[0] = n

                pe.wait_ge(lora_in, 96)
                for n, (first, lo, width) in enumerate(((w_la, 0, LORA), (a_la, LORA, LORA), (g_la, 0, P))):
                    pe.wait_ge(mixed, n + 1)
                    start(n)
                    ins = matmuls(nc, bank(n)[lo:lo + width, 0:T], [first[:, q, :] for q in range(KC)],
                                  [xs[n % 2][:, q, :] for q in range(KC)])
                    ins.then_inc(p_done, 1)
                for n0, lo in ((3, 0), (7, LORA)):
                    taken(pe, 1)
                    for b in range(4):
                        start(n0 + b)
                        for i in range(2):
                            f = 2 * b + i
                            ins = nc.tensor.matmul(bank(n0 + b)[:, i * T:(i + 1) * T],
                                                   wa_lb[lo:lo + LORA, f * P:(f + 1) * P],
                                                   hid[lo:lo + LORA, 0, :], start=True, stop=True)
                        ins.then_inc(p_done, 1)
                taken(pe, 2)
                for i in range(2 * TC):
                    start(11 + i)
                    nc.tensor.matmul(bank(11 + i), hid[:, 1, (i // 2) * P:(i // 2 + 1) * P],
                                     g_lb[:, (i % 2) * BANK:(i % 2 + 1) * BANK], start=True,
                                     stop=True).then_inc(p_done, 1)
                for m in range(3):
                    pe.wait_ge(w_in[m], 16)
                    pe.wait_ge(mixed, 4 + m)
                    src, w = xs[(3 + m) % 2], w_rkv_sb[m]
                    for b in range(4):
                        n = 15 + 4 * m + b
                        start(n)
                        if m < 2:
                            for i in range(2):
                                f = 2 * b + i
                                ins = matmuls(nc, bank(n)[:, i * T:(i + 1) * T],
                                              [w[:, q, f * P:(f + 1) * P] for q in range(KC)],
                                              [src[:, q, :] for q in range(KC)])
                        else:
                            ins = matmuls(nc, bank(n), [src[:, q, (b // 2) * P:(b // 2 + 1) * P] for q in range(KC)],
                                          [w[:, q, (b % 2) * BANK:(b % 2 + 1) * BANK] for q in range(KC)])
                        ins.then_inc(p_done, 1)

            def two(dst, b):
                return dst[:, 2 * b:2 * b + 2, :].rearrange("p a b -> p (a b)")

            def half_row(dst, i):
                return dst[:, i // 2, (i % 2) * BANK:(i % 2 + 1) * BANK]

            def take(eng, who, n, copy):
                m, b = divmod(n - 15, 4)
                dst = two((r, k)[m], b) if m < 2 else half_row(v, b)
                copy(dst, c.banks[:, n % 8, :])

            @block.scalar
            def _(act):
                norm.act_take(act)
                bank = [c.banks[:, i, :] for i in range(8)]
                act.wait_ge(p_done, 1)
                nc.scalar.activation(hid[0:LORA, 0, :], bank[0][0:LORA, 0:T], ACT.Tanh).then_inc(took_a, 1)
                act.wait_ge(p_done, 3)
                nc.scalar.activation(hid[:, 1, :], bank[2][:, 0:T], ACT.Sigmoid).then_inc(took_a, 1)
                for n0, dst, bias in ((3, sig, "w0"), (7, a, "a0")):
                    for b in range(4):
                        act.wait_ge(p_done, n0 + b + 1)
                        for i in range(2):
                            f = 2 * b + i
                            ins = nc.scalar.activation(dst[:, f, :], bank[(n0 + b) % 8][:, i * T:(i + 1) * T],
                                                       ACT.Sigmoid, bias=c.col(bias, f))
                        ins.then_inc(took_a, 1)
                for n in range(15, 27):
                    if TAKER[n] == "A":
                        act.wait_ge(p_done, n + 1)
                        take(act, "A", n, lambda o, i: nc.scalar.activation(o, i, ACT.Copy).then_inc(took_a, 1))

            @block.vector
            def _(dve):
                chain, vec = c.dve_chain, nc.vector
                for tc in range(TC):
                    norm.dve_rows(dve, tc)
                norm.dve_take(dve)
                dve.wait_ge(norm.by_act, 4)
                dve.wait_ge(norm.by_dve, 4)
                vec.tensor_tensor(xx[:, :, 1:T], c.xT[:, :, 0:T - 1], c.xT[:, :, 1:T], ALU.subtract)
                chain(dve, vec.tensor_scalar(xx[:, :, 0:1], c.xT[:, :, 0:1], -1.0, None, ALU.mult))

                def mix(n):
                    if n >= 2:
                        dve.wait_ge(p_done, (1, 2, 3, 19)[n - 2])
                    for q in range(KC):
                        ins = vec.scalar_tensor_tensor(xs[n % 2][:, q, :], xx[:, q, :],
                                                       c.col("mu", ORDER[n] * KC + q), c.xT[:, q, :],
                                                       ALU.mult, ALU.add)
                    ins.then_inc(mixed, 1)

                mix(0)
                mix(1)
                mix(2)
                dve.wait_ge(p_done, 2)
                vec.tensor_copy(hid[LORA:P, 0, :], c.banks[LORA:P, 1, 0:T]).then_inc(took_v, 1)
                mix(3)
                mix(4)
                for i in range(4):
                    dve.wait_ge(p_done, 12 + i)
                    vec.tensor_copy(half_row(g, i), c.banks[:, (11 + i) % 8, :]).then_inc(took_v, 1)
                for n in range(15, 27):
                    if n == 21:
                        mix(5)
                    if TAKER[n] == "V":
                        dve.wait_ge(p_done, n + 1)
                        take(dve, "V", n, lambda o, i: vec.tensor_copy(o, i).then_inc(took_v, 1))

        ar = unit(0, 2).rearrange("p (k f t) -> p k f t", k=KC, f=2)
        bT, kT = feat(2), feat(3)
        kk, run, w_run, tmp, keep = (feat(i) for i in range(4, 9))
        norms = sb("norms", [RH, 3, T])
        mask = sb("mask", [P, 4 * P])
        mask_in, scan_ready = sem("mask_in"), sem("scan_ready")
        kk_squared, ss_done, inv_ready, inv_spread = (sem(n) for n in (
            "kk_squared", "ss_done", "inv_ready", "inv_spread"))
        run_ready, run_excl, w_incl, w_used = (sem(n) for n in ("run_ready", "run_excl", "w_incl", "w_used"))
        prod_ready, bonus_done = sem("prod_ready"), sem("bonus_done")

        def flat(x):
            return x.rearrange("p k t -> p (k t)")

        with nc.Block() as block:
            @block.sync
            def _(sp):
                sp.dma_start(mask[:, :], d["chunk_mask"]).then_inc(mask_in, 16)
                sp.wait_ge(mask_in, 16)

            @block.gpsimd
            def _(pool):
                nc.gpsimd.memset(keep, 1.0).then_inc(scan_ready, 1)
                pool.wait_ge(scan_ready, 1)
                nc.gpsimd.memset(flat(keep).rearrange("p (n t) -> p n t", t=CH)[:, :, 0:1], 0.0).then_inc(scan_ready, 1)

            @block.tensor
            def _(pe):
                pe.wait_ge(sel_in, 32)
                pe.wait_ge(kk_squared, 1)
                matmuls(nc, c.banks[0:RH, 0, 0:T], [head_of[:, q, :] for q in range(KC)],
                        [tmp[:, q, :] for q in range(KC)]).then_inc(ss_done, 1)
                pe.wait_ge(inv_ready, 1)
                for q in range(KC):
                    ins = nc.tensor.matmul(c.banks[:, 1 + q // 2, (q % 2) * T:(q % 2 + 1) * T], head_to[:, q, :],
                                           norms[:, 0, :], start=True, stop=True)
                    if q % 2:
                        ins.then_inc(inv_spread, 1)
                pe.wait_ge(prod_ready, 1)
                for tc in range(TC):
                    ins = matmuls(nc, c.banks[:, 5, tc * RH:(tc + 1) * RH],
                                  [tmp[:, q, tc * P:(tc + 1) * P] for q in range(KC)],
                                  [head_of[:, q, :] for q in range(KC)])
                ins.then_inc(bonus_done, 1)

            @block.scalar
            def _(act):
                act.wait_ge(run_ready, 1)
                nc.scalar.activation(w_run, run, ACT.Exp, scale=-DECAY).then_inc(w_incl, 1)
                act.wait_ge(run_ready, 2)
                nc.scalar.activation(w_run, run, ACT.Exp, scale=DECAY).then_inc(w_incl, 1)
                act.wait_ge(run_excl, 1)
                nc.scalar.activation(w_run, sig, ACT.Exp, scale=-DECAY).then_inc(w_incl, 1)

            @block.vector
            def _(dve):
                chain, vec = c.dve_chain, nc.vector
                for q in range(KC):
                    vec.tensor_scalar(kk[:, q, :], k[:, q, :], c.col("k_k", q), None, ALU.mult)
                dve.drain()
                vec.tensor_tensor(tmp, kk, kk, ALU.mult).then_inc(kk_squared, 1)
                dve.wait_ge(scan_ready, 2)
                vec.tensor_tensor_scan(flat(run), flat(keep), flat(sig), 0.0, ALU.mult, ALU.add).then_inc(run_ready, 1)
                dve.wait_ge(ss_done, 1)
                ss = norms[:, 0, :]
                c.dve_rstd(dve, vec.tensor_scalar(ss, c.banks[0:RH, 0, 0:T], 1e-24, None, ALU.max), ss,
                           (norms[:, 1, :], norms[:, 2, :]))
                dve.nop().then_inc(inv_ready, 1)
                for q in range(KC):
                    vec.tensor_scalar(tmp[:, q, :], a[:, q, :], -1.0, c.col("k_a", q), ALU.add, ALU.mult)
                dve.drain()
                chain(dve, vec.scalar_tensor_tensor(flat(k), flat(tmp), 1.0, flat(k), ALU.add, ALU.mult))
                for q in range(KC):
                    last = vec.scalar_tensor_tensor(tmp[:, q, :], r[:, q, :], c.col("r_k", q), k[:, q, :], ALU.mult,
                                                    ALU.mult)
                last.then_inc(prod_ready, 1)
                for b in range(4):
                    dve.wait_ge(inv_spread, b + 1)
                    s = kk[:, 2 * b:2 * b + 2, :].rearrange("p a b -> p (a b)")
                    last = vec.tensor_tensor(s, s, c.banks[:, 1 + b, :], ALU.mult)
                chain(dve, last)
                dve.wait_ge(w_incl, 1)
                vec.tensor_tensor(ar[:, :, 1, :], r, w_run, ALU.mult)
                vec.tensor_copy(last_w[:, :, :], w_run.rearrange("p k (n t) -> p k n t", t=CH)[:, :, :, CH - 1])
                chain(dve, vec.tensor_tensor(sig, run, sig, ALU.subtract))
                dve.nop().then_inc(run_ready, 1)
                dve.wait_ge(w_incl, 2)
                vec.tensor_tensor(kT, k, w_run, ALU.mult)
                chain(dve, vec.tensor_tensor(a, kk, a, ALU.mult))
                chain(dve, vec.tensor_tensor(bT, a, w_run, ALU.mult))
                dve.nop().then_inc(run_excl, 1)
                dve.wait_ge(w_incl, 3)
                vec.scalar_tensor_tensor(ar[:, :, 0, :], kk, -1.0, w_run, ALU.mult, ALU.mult)
                dve.wait_ge(bonus_done, 1)
                vec.tensor_copy(bonus[:, :, :].rearrange("p c h -> p (c h)"), c.banks[:, 5, 0:TC * RH])

        G_AB, G_QB, G_AK, G_QK = range(4)
        gram = unit(4, 8).rearrange("p (c h n) -> p c h n", c=TC, h=RH)
        inv = unit(12, 2).rearrange("p (c h t) -> p c h t", c=TC, h=RH)
        tokA, tokB, tokK = tok(16), tok(18), tok(19)
        P_T, akv, u, sa = c.xT[:, :, :], tok(21), tok(14), tok(21)
        sys_a = unit(14)[:, 0:1024].rearrange("p (s t) -> p s t", s=CH)
        sys_x = unit(14)[:, 1024:2048].rearrange("p (s t) -> p s t", s=CH)
        work = unit(15)[:, 0:1024]
        dram_a = nc.dram_tensor("chunk_a", (J, TC * RH, CH, CH), F32, kind="Internal").ap()
        dram_x = nc.dram_tensor("chunk_x", (J, TC * RH, CH, CH), F32, kind="Internal").ap()
        gram_done, gram_dve = sem("gram_done"), sem("gram_dve")
        a_out, a_back, x_out, x_back, inv_zero, sys_zero, solved = (sem(n) for n in (
            "a_out", "a_back", "x_out", "x_back", "inv_zero", "sys_zero", "solved"))
        tok_done, tok_act = sem("tok_done"), sem("tok_act")
        akv_done, akv_act, pt_done, pt_act, u_done, u_act = (sem(n) for n in (
            "akv_done", "akv_act", "pt_done", "pt_act", "u_done", "u_act"))

        def part(h):
            return slice(HD * (h % 2), HD * (h % 2) + HD)

        def at_head(h):
            return slice(h * HD, (h + 1) * HD)

        with nc.Block() as block:
            @block.sync
            def _(sp):
                sp.wait_ge(gram_dve, TC * RH)
                for j in range(J):
                    s = slice(CH * j, CH * (j + 1))
                    src = gram[s, :, :, G_AB * P + CH * j:G_AB * P + CH * (j + 1)].rearrange("s c h t -> s (c h) t")
                    sp.dma_start(dram_a[j].rearrange("n s t -> s n t"), src).then_inc(a_out, 16)
                sp.wait_ge(a_out, 16 * J)
                sp.dma_start(sys_a, dram_a.rearrange("j n s t -> (j n) s t")).then_inc(a_back, 16)
                sp.wait_ge(solved, 1)
                sp.dma_start(dram_x.rearrange("j n s t -> (j n) s t"), sys_x).then_inc(x_out, 16)
                sp.wait_ge(x_out, 16)
                sp.wait_ge(inv_zero, 1)
                for j in range(J):
                    s = slice(CH * j, CH * (j + 1))
                    dst = inv[s, :, :, CH * j:CH * (j + 1)].rearrange("s c h t -> s (c h) t")
                    sp.dma_start(dst, dram_x[j].rearrange("n s t -> s n t")).then_inc(x_back, 16)

            @block.gpsimd
            def _(pool):
                nc.gpsimd.memset(unit(14)[:, 1024:2048], 0.0).then_inc(sys_zero, 1)
                pool.wait_ge(sys_zero, 1)
                nc.gpsimd.memset(unit(14)[:, 1024:2048:CH + 1], 1.0).then_inc(sys_zero, 1)
                nc.gpsimd.memset(unit(12, 2), 0.0).then_inc(inv_zero, 1)

            @block.tensor
            def _(pe):
                n = 0
                for tc in range(TC):
                    for h in range(RH):
                        if n >= 4:
                            pe.wait_ge(gram_dve, n - 3)
                        p, t = h // 2, slice(tc * P, (tc + 1) * P)
                        out = c.banks[:, n % 4, :]
                        nc.tensor.matmul(out[:, 0:2 * P], bT[part(h), p, t], ar[part(h), p, :, t], start=True,
                                         stop=True)
                        nc.tensor.matmul(out[:, 2 * P:4 * P], kT[part(h), p, t], ar[part(h), p, :, t], start=True,
                                         stop=True).then_inc(gram_done, 1)
                        n += 1
                n = 0
                for src in (ar[:, :, 0, :], bT, kT):
                    for tc in range(TC):
                        for q in range(2):
                            if n >= 2:
                                pe.wait_ge(tok_act, n - 1)
                            for i in range(4):
                                ins = nc.tensor.transpose(c.banks[:, 4 + n % 2, i * P:(i + 1) * P],
                                                          src[:, 4 * q + i, tc * P:(tc + 1) * P], c.ident[:, :])
                            ins.then_inc(tok_done, 1)
                            n += 1
                pe.wait_ge(gram_dve, TC * RH)
                for tc in range(TC):
                    for q in range(2):
                        for i in range(8):
                            h = 8 * q + i
                            ins = nc.tensor.matmul(c.banks[:, 2 * tc + q, i * HD:(i + 1) * HD],
                                                   gram[:, tc, h, G_AK * P:(G_AK + 1) * P], v[:, tc, at_head(h)],
                                                   start=True, stop=True)
                        ins.then_inc(akv_done, 1)
                pe.wait_ge(x_back, 16 * J)
                pe.wait_ge(tok_act, 12)
                for p in range(RP):
                    for s in range(2):
                        h = 2 * p + s
                        for tc in range(TC):
                            o = (p % 2) * T + tc * P
                            ins = nc.tensor.matmul(c.banks[part(h), 4 + p // 2, o:o + P], tokA[:, tc, at_head(h)],
                                                   inv[:, tc, h, :], start=True, stop=True)
                    if p % 2:
                        ins.then_inc(pt_done, 1)
                for tc in range(TC):
                    for q in range(2):
                        pe.wait_ge(akv_act, 2 * tc + q + 1)
                        for i in range(8):
                            h = 8 * q + i
                            ins = nc.tensor.matmul(c.banks[:, 2 * tc + q, i * HD:(i + 1) * HD],
                                                   inv[:, tc, h, :], akv[:, tc, at_head(h)],
                                                   start=True, stop=True)
                        ins.then_inc(u_done, 1)

            @block.scalar
            def _(act):
                n = 0
                for dst in (tokA, tokB, tokK):
                    for tc in range(TC):
                        for q in range(2):
                            act.wait_ge(tok_done, n + 1)
                            nc.scalar.activation(dst[:, tc, q * BANK:(q + 1) * BANK], c.banks[:, 4 + n % 2, :],
                                                 ACT.Copy).then_inc(tok_act, 1)
                            n += 1
                for done, dst, ready in ((akv_done, akv, akv_act), (pt_done, None, pt_act), (u_done, u, u_act)):
                    for i in range(4):
                        act.wait_ge(done, i + 1)
                        if dst is None:
                            nc.scalar.activation(two(P_T, i), c.banks[:, 4 + i, :], ACT.Copy).then_inc(ready, 1)
                        else:
                            nc.scalar.activation(half_row(dst, i), c.banks[:, i, :], ACT.Copy).then_inc(ready, 1)

            @block.vector
            def _(dve):
                vec = nc.vector
                n = 0
                for tc in range(TC):
                    for h in range(RH):
                        dve.wait_ge(gram_done, n + 1)
                        vec.tensor_tensor(gram[:, tc, h, :], c.banks[:, n % 4, :], mask[:, :],
                                          ALU.mult).then_inc(gram_dve, 1)
                        n += 1
                dve.wait_ge(a_back, 16)
                dve.wait_ge(sys_zero, 2)
                for t in range(1, CH):
                    w = work[:, 0:t * t].rearrange("p (j s) -> p j s", j=t)
                    c.dve_chain(dve, vec.tensor_tensor(w, sys_x[:, 0:t, 0:t],
                                                       sys_a[:, 0:t, t].unsqueeze(1).to_broadcast([P, t, t]),
                                                       ALU.mult))
                    c.dve_chain(dve, vec.tensor_reduce(sys_x[:, 0:t, t], w, AX.X, ALU.add))
                dve.nop().then_inc(solved, 1)

        states = unit(15, 2).rearrange("p (n f) -> p n f", n=NCH)
        grown = sb("grown", [P, BANK])
        sa_done, sa_ready, s_done, s_ready, s_zero = (sem(n) for n in (
            "sa_done", "sa_ready", "s_done", "s_ready", "s_zero"))
        y_done, y_out, yT_done, yT_act, o_done = (sem(n) for n in (
            "y_done", "y_out", "yT_done", "yT_act", "o_done"))
        w_o = [unit(i, 2).rearrange("p (k n) -> p k n", k=4) for i in (2, 12)]
        o_in = [sem(f"o_in{i}") for i in range(2)]
        rows_in = sem("rows_in")
        ln_g, ln_b = unit(14)[:, 0:D], unit(14)[:, D:2 * D]
        y_tok, centred, yT = tok(18), tok(19), P_T
        SA_B, ST_B, Y_B = 0, 2, 4

        def split_heads(x):
            return x.rearrange("p (q s n) -> p s q n", s=2, n=HD)

        with nc.Block() as block:
            @block.sync
            def _(sp):
                w = d["w_o"].rearrange("(k p) n -> p k n", p=P)
                for i in range(2):
                    sp.dma_start(w_o[i], w[:, 4 * i:4 * i + 4, :]).then_inc(o_in[i], 16)
                sp.wait_ge(sa_ready, 2 * NCH)
                sp.dma_start(ln_g, rows_to_all(c.row("rln_g"))).then_inc(rows_in, 16)
                sp.dma_start(ln_b, rows_to_all(c.row("rln_b"))).then_inc(rows_in, 16)

            @block.gpsimd
            def _(pool):
                nc.gpsimd.memset(states[:, 0, :], 0.0).then_inc(s_zero, 1)

            @block.tensor
            def _(pe):
                pe.wait_ge(s_zero, 1)
                for n in range(NCH):
                    tc, j = divmod(n, J)
                    rows, cols = slice(CH * j, CH * (j + 1)), slice(n * CH, (n + 1) * CH)
                    pe.wait_ge(s_ready, n)
                    for s in range(2):
                        for p in range(RP):
                            ins = nc.tensor.matmul(c.banks[rows, SA_B + s, p * HD:(p + 1) * HD],
                                                   P_T[part(s), p, cols],
                                                   states[part(s), n, p * HD:(p + 1) * HD], start=True, stop=True)
                    ins.then_inc(sa_done, 1)
                    if n == NCH - 1:
                        break
                    for h in range(RH):
                        nc.tensor.matmul(c.banks[part(h), ST_B, (h // 2) * HD:(h // 2 + 1) * HD],
                                         tokK[rows, tc, at_head(h)], v[rows, tc, at_head(h)],
                                         start=h < 2, stop=False, skip_group_check=True)
                    pe.wait_ge(sa_ready, 2 * (n + 1))
                    for h in range(RH):
                        ins = nc.tensor.matmul(c.banks[part(h), ST_B, (h // 2) * HD:(h // 2 + 1) * HD],
                                               tokB[rows, tc, at_head(h)], sa[rows, tc, at_head(h)],
                                               start=False, stop=True, skip_group_check=True)
                    ins.then_inc(s_done, 1)
                pe.wait_ge(sa_ready, 2 * NCH)
                for i in range(2 * TC):
                    tc = i // 2
                    for m in range(RP):
                        h = 2 * m + i % 2
                        out = c.banks[:, Y_B + i, m * HD:(m + 1) * HD]
                        nc.tensor.matmul(out, gram[:, tc, h, G_QK * P:(G_QK + 1) * P], v[:, tc, at_head(h)],
                                         start=True, stop=False)
                        nc.tensor.matmul(out, gram[:, tc, h, G_QB * P:(G_QB + 1) * P], sa[:, tc, at_head(h)],
                                         start=False, stop=False)
                        for j in range(J):
                            n = tc * J + j
                            ins = nc.tensor.matmul(out[CH * j:CH * (j + 1), :],
                                                   ar[part(h), h // 2, 1, n * CH:(n + 1) * CH],
                                                   states[part(h), n, (h // 2) * HD:(h // 2 + 1) * HD],
                                                   start=False, stop=True)
                    ins.then_inc(y_done, 1)
                for k2 in range(4):
                    pe.wait_ge(y_out, TC)
                    for i in range(2):
                        for tc in range(TC):
                            q = 2 * k2 + i
                            ins = nc.tensor.transpose(c.banks[:, k2, i * T + tc * P:i * T + (tc + 1) * P],
                                                      y_tok[:, tc, q * P:(q + 1) * P], c.ident[:, :])
                    ins.then_inc(yT_done, 1)
                pe.wait_ge(yT_act, 4)
                for i in range(2):
                    pe.wait_ge(o_in[i], 16)
                for i in range(2 * TC):
                    matmuls(nc, c.banks[:, Y_B + i, :],
                            [yT[:, q, (i // 2) * P:(i // 2 + 1) * P] for q in range(KC)],
                            [w_o[q // 4][:, q % 4, (i % 2) * BANK:(i % 2 + 1) * BANK] for q in range(KC)]).then_inc(
                                o_done, 1)

            @block.scalar
            def _(act):
                for i in range(4):
                    act.wait_ge(yT_done, i + 1)
                    nc.scalar.activation(two(yT, i), c.banks[:, i, :], ACT.Copy).then_inc(yT_act, 1)

            @block.vector
            def _(dve):
                chain, vec = c.dve_chain, nc.vector
                for n in range(NCH):
                    tc, j = divmod(n, J)
                    rows = slice(CH * j, CH * (j + 1))
                    dve.wait_ge(sa_done, n + 1)
                    for s in range(2):
                        vec.tensor_tensor(split_heads(sa[rows, tc, :])[:, s, :, :],
                                          c.banks[rows, SA_B + s, :].rearrange("p (q n) -> p q n", n=HD),
                                          split_heads(u[rows, tc, :])[:, s, :, :], ALU.add).then_inc(sa_ready, 1)
                    if n == NCH - 1:
                        break
                    dve.wait_ge(s_done, n + 1)
                    chain(dve, vec.tensor_tensor(grown[:, :], c.banks[:, ST_B, :], states[:, n, :], ALU.add))
                    vec.tensor_tensor(states[:, n + 1, :].rearrange("p (q n) -> p q n", n=HD),
                                      grown[:, :].rearrange("p (q n) -> p q n", n=HD),
                                      last_w[:, :, n:n + 1].to_broadcast([P, RP, HD]), ALU.mult).then_inc(s_ready, 1)
                    dve.wait_ge(s_ready, n + 1)
                dve.wait_ge(rows_in, 32)
                for tc in range(TC):
                    mu, var = moments[:, 0, :], moments[:, 1, :]
                    y3, t3, v3 = (x[:, tc, :].rearrange("p (h n) -> p h n", h=RH) for x in (y_tok, centred, v))
                    for i in range(2):
                        dve.wait_ge(y_done, 2 * tc + i + 1)
                        last = vec.tensor_reduce(mu[:, i:RH:2], c.banks[:, Y_B + 2 * tc + i, :].rearrange(
                            "p (h n) -> p h n", n=HD), AX.X, ALU.add)
                    chain(dve, last)
                    chain(dve, vec.tensor_scalar(mu, mu, 1.0 / HD, None, ALU.mult))
                    for i in range(2):
                        hs = slice(i, RH, 2)
                        last = vec.tensor_tensor(y3[:, hs, :], c.banks[:, Y_B + 2 * tc + i, :].rearrange(
                            "p (h n) -> p h n", n=HD), mu[:, hs].unsqueeze(2).to_broadcast([P, 8, HD]), ALU.subtract)
                    chain(dve, last)
                    chain(dve, vec.tensor_tensor(t3, y3, y3, ALU.mult))
                    chain(dve, vec.tensor_reduce(var, t3, AX.X, ALU.add))
                    c.dve_rstd(dve, vec.tensor_scalar(var, var, 1.0 / HD, GN_EPS, ALU.mult, ALU.add), var)
                    chain(dve, vec.tensor_tensor(y3, y3, var.unsqueeze(2).to_broadcast([P, RH, HD]), ALU.mult))
                    y = y_tok[:, tc, :]
                    chain(dve, vec.tensor_tensor(y, y, ln_g, ALU.mult))
                    vec.tensor_tensor(t3, v3, bonus[:, tc, :].unsqueeze(2).to_broadcast([P, RH, HD]), ALU.mult)
                    chain(dve, vec.tensor_tensor(y, y, ln_b, ALU.add))
                    chain(dve, vec.tensor_tensor(y, y, centred[:, tc, :], ALU.add))
                    vec.tensor_tensor(y, y, g[:, tc, :], ALU.mult).then_inc(y_out, 1)
                for i in range(2 * TC):
                    dve.wait_ge(o_done, i + 1)
                    s = c.x[:, i // 2, (i % 2) * BANK:(i % 2 + 1) * BANK]
                    vec.tensor_tensor(s, s, c.banks[:, Y_B + i, :], ALU.add)


STAGES = [mixer_stage, expert_stage, embedding_stage, gating_stage, lambda c: ffn_stage(c, 0), rwkv_stage,
          lambda c: ffn_stage(c, 1)]


def finish_stage(c):
    nc, d = c.nc, c.dram
    with ExitStack() as es:
        gain = es.enter_context(nc.sbuf_tensor("final_gain", [P, D], F32))
        y = es.enter_context(nc.sbuf_tensor("y_out", [P, TC, D], F32))
        gain_in = c.semaphore("gain_in")
        y_ready = c.semaphore("y_ready")
        stored = c.semaphore("stored")
        out = c.out.rearrange("b (c p) n -> p (b c) n", p=P)
        with nc.Block() as block:
            @block.sync
            def _(sp):
                sp.dma_start(gain[:, :], rows_to_all(c.row("final"))).then_inc(gain_in, 16)
                for tc in range(TC):
                    sp.wait_ge(y_ready, tc + 1)
                    sp.dma_start(out[:, tc, :], y[:, tc, :]).then_inc(stored, 16)
                sp.wait_ge(stored, 16 * TC)

            @block.vector
            def _(dve):
                chain, s = c.dve_chain, c.stat
                for tc in range(TC):
                    x = c.x[:, tc, :]
                    if not FINAL:
                        nc.vector.tensor_copy(y[:, tc, :], x).then_inc(y_ready, 1)
                        continue
                    chain(dve, nc.vector.tensor_tensor_reduce(y[:, tc, :], x, x, 1.0, 0.0, ALU.mult, ALU.add,
                                                              s[:, tc:tc + 1]))
                    c.dve_rstd(dve, nc.vector.tensor_scalar(s[:, tc:tc + 1], s[:, tc:tc + 1], 1.0 / D, EPS, ALU.mult,
                                                       ALU.add), s[:, tc:tc + 1])
                    dve.wait_ge(gain_in, 16)
                    nc.vector.scalar_tensor_tensor(y[:, tc, :], x, s[:, tc:tc + 1], gain[:, :], ALU.mult,
                                                   ALU.mult).then_inc(y_ready, 1)


FINAL = True


def program(nc, dram, out):
    with ExitStack() as ctx:
        core = Core(nc, dram, out, ctx)
        for stage in STAGES:
            stage(core)
            core.end_stage()
        finish_stage(core)


def shape_constants():
    i = np.arange(P)
    f32 = np.float32
    log_g = np.log(1.0 - 2.0 ** (-5.0 - np.arange(HEADS)))
    key = np.concatenate([i[:, None] + 0 * np.arange(T)[None], i[:, None] + P + 0 * i[None]], 1)
    query = np.concatenate([np.arange(T)[None] + 0 * i[:, None], P + i[None] + 0 * i[:, None]], 1)
    gap = query - key
    decay = np.stack([np.where(gap >= 0, np.exp(g * np.maximum(gap, 0)), 0.0) for g in log_g], 1)
    return {
        "ident": np.eye(P, dtype=f32),
        "decay": decay.reshape(P, -1).astype(f32),
        "sufsum": -(i[:, None] >= i[None]).astype(f32),
        "head_of": (np.arange(RH)[None, None] == (2 * np.arange(RH // 2)[None, :, None]
                                                  + i[:, None, None] // HD)).reshape(P, -1).astype(f32),
        "head_to": (np.arange(RH)[:, None, None] == (2 * np.arange(RH // 2)[None, :, None]
                                                     + i[None, None] // HD)).reshape(RH, -1).astype(f32),
        "chunk_mask": np.concatenate([(i[:, None] // CH == i[None] // CH) & before for before in (
            i[:, None] < i[None], i[:, None] <= i[None]) * 2], 1).astype(f32),
        "upto": (i[:, None] <= i[None]).astype(f32),
        "number": np.tile(np.tile(np.arange(T).reshape(BLOCKS, 1, CAP), (1, 2, 1)).reshape(1, -1), (P, 1)).astype(f32),
        "expert_no": np.tile(np.arange(EXPERTS), (P, 1)).astype(f32),
        "extra_col": np.stack([(i // EXPERTS + 1) * CAP, i % EXPERTS, i // EXPERTS + 1], 1).astype(f32),
        "work_list": np.concatenate([np.zeros(64), np.arange(EXPERTS), np.zeros(96)]).reshape(1, -1).astype(np.int32),
    }


def kernel(**a):
    from concourse import bacc
    from concourse.bass_utils import run_bass_kernel_spmd

    def col(v):
        return v.reshape(-1, P).T

    def row(v):
        return v.reshape(1, -1)

    cols = {"g_mix": a["g_mix_norm"], "g_ffn": a["g_ffn_norm"], "g_ple": a["g_ple_norm"],
            "n_mix0": a["norm_mix_g_2"][0], "n_mix1": a["norm_mix_g_2"][1],
            "n_ffn0": a["norm_ffn_g_2"][0], "n_ffn1": a["norm_ffn_g_2"][1],
            "b_u": a["sgu_b_in_2"][0, :SGU], "mu": a["rwkv_mu_2"], "w0": a["rwkv_w0_2"], "a0": a["rwkv_a0_2"],
            "k_k": a["rwkv_k_k_2"], "k_a": a["rwkv_k_a_2"], "r_k": a["rwkv_r_k_2"]}
    inv_freq = (10000.0 ** (-np.arange(HD // 2) / (HD // 2))).astype(np.float32)
    rows = {"sb_q": a["sb_q_gain"], "sb_k": a["sb_k_gain"], "ret_q": a["ret_q_gain"], "ret_k": a["ret_k_gain"],
            "gn_g": a["ret_gn_gain"], "gn_b": a["ret_gn_bias"], "b_router": a["b_router"], "inv_freq": inv_freq,
            "b_v": a["sgu_b_in_2"][0, SGU:], "ln_g": a["sgu_ln_g_2"], "ln_b": a["sgu_ln_b_2"],
            "b_s": a["sgu_b_s_2"], "final": a["final_norm_g_2"], "rln_g": a["rwkv_ln_g_2"],
            "rln_b": a["rwkv_ln_b_2"]}
    arrays = {
        "x": a["x"][0],
        "pT": a["p"][0, 0].T,
        "positions": a["positions"].reshape(TC, P).T,
        "cols": np.concatenate([col(cols[n]) for n in COLS], 1),
        "rows": np.concatenate([row(rows[n]) for n in ROWS], 1),
        "w_in": a["w_in"][0], "w_out": a["w_out"][0],
        "w_router": a["w_router"][0],
        "w_up": a["w_up_gate"].reshape(EXPERTS * D, 2 * D), "b_up": a["b_up_gate"][0],
        "w_down": a["w_down"].reshape(EXPERTS * D, D), "b_down": a["b_down"][0],
        "w_ple_gate": a["w_ple_gate"][0], "w_ple_proj": a["w_ple_proj"][0],
        "ffn_w1": a["ffn_w1_2"].reshape(2 * D, FF), "ffn_w2": a["ffn_w2_2"].reshape(2 * FF, D),
        "sgu_in": a["sgu_w_in_2"][0], "sgu_out": a["sgu_w_out_2"][0],
        "w_sT": a["sgu_w_s_2"][0].transpose(2, 0, 1).reshape(P, GROUPS * P),
        "w_rkv": a["rwkv_w_rkv_2"][0].reshape(3 * D, D), "w_o": a["rwkv_w_o_2"][0],
        "w_la": a["rwkv_w_lora_a_2"][0], "w_lb": a["rwkv_w_lora_b_2"][0],
        "a_la": a["rwkv_a_lora_a_2"][0], "a_lb": a["rwkv_a_lora_b_2"][0],
        "g_la": a["rwkv_g_lora_a_2"][0], "g_lb": a["rwkv_g_lora_b_2"][0],
    }
    arrays.update(shape_constants())
    arrays = {n: np.ascontiguousarray(v) for n, v in arrays.items()}
    nc = bacc.Bacc("TRN2", target_bir_lowering=False, num_devices=1)
    dram = {n: nc.dram_tensor(f"in_{n}", v.shape, mybir.dt.from_np(v.dtype), kind="ExternalInput").ap()
            for n, v in arrays.items()}
    out = nc.dram_tensor("out_y", (1, T, D), F32, kind="ExternalOutput").ap()
    program(nc, dram, out)
    r = run_bass_kernel_spmd(nc, [{f"in_{n}": v for n, v in arrays.items()}], core_ids=[0])
    return r.results[0]["out_y"]
```

```python
from contextlib import ExitStack

import numpy as np

import concourse.bass as bass
from concourse import mybir

F32 = mybir.dt.float32
F32R = mybir.dt.float32r
BF16 = mybir.dt.bfloat16
I32 = mybir.dt.int32
U32 = mybir.dt.uint32
ALU = mybir.AluOpType
ACT = mybir.ActivationFunctionType
AX = mybir.AxisListType

P = 128
T = 256
TC = T // P
D = 1024
KC = D // P
BANK = 512
HD = 64
HEADS = 8
PAIRS = HEADS // 2
HW = HEADS * HD
PLE = 256
EXPERTS = 32
TOPK = 4
CAP = 64
MAX_EXTRA = T * TOPK // (CAP + 1) + 1
BLOCKS = T // CAP
LIMIT = 7.0
ALPHA = 1.702
EPS = 1e-6
SGU = 2048
GROUPS = 16
FF = 4096
RH = 16
CH = 32
GN_EPS = 64e-5
LN_EPS = 1e-5
MIX_R, MIX_K, MIX_V, MIX_W, MIX_A, MIX_G = range(6)

COLS = {}
for _name, _n in (("g_mix", 8), ("g_ffn", 8), ("g_ple", 8), ("n_mix0", 8), ("n_mix1", 8), ("n_ffn0", 8),
                  ("n_ffn1", 8), ("b_u", 16), ("mu", 48), ("w0", 8), ("a0", 8), ("k_k", 8), ("k_a", 8),
                  ("r_k", 8)):
    COLS[_name] = sum(_n for _, _n in COLS.values()), _n
NCOLS = sum(_n for _, _n in COLS.values())
ROWS = {}
for _name, _n in (("sb_q", HD), ("sb_k", HD), ("ret_q", HD), ("ret_k", HD), ("gn_g", HW), ("gn_b", HW),
                  ("b_router", EXPERTS), ("inv_freq", HD // 2), ("b_v", SGU), ("ln_g", SGU), ("ln_b", SGU),
                  ("b_s", SGU), ("final", D), ("rln_g", D), ("rln_b", D)):
    ROWS[_name] = sum(_n for _, _n in ROWS.values()), _n
NROWS = sum(_n for _, _n in ROWS.values())


class Chain:

    def __init__(self, sem):
        self.sem, self.n = sem, 0

    def __call__(self, eng, ins):
        self.n += 1
        ins.then_inc(self.sem, 1)
        eng.wait_ge(self.sem, self.n)


class Core:

    def __init__(self, nc, dram, out, ctx):
        self.nc, self.dram, self.out, self.ctx = nc, dram, out, ctx
        self.stage_semaphores = []
        self.stage = 1
        self.x = ctx.enter_context(nc.sbuf_tensor("x", [P, TC, D], F32))
        self.xT = ctx.enter_context(nc.sbuf_tensor("xT", [P, KC, T], F32))
        self.ident = ctx.enter_context(nc.sbuf_tensor("ident", [P, P], F32))
        self.cols = ctx.enter_context(nc.sbuf_tensor("cols", [P, NCOLS], F32))
        self.diag = ctx.enter_context(nc.sbuf_tensor("diag", [P, TC, P], F32))
        self.stat = ctx.enter_context(nc.sbuf_tensor("stat", [P, 8], F32))
        self.banks = ctx.enter_context(nc.psum_tensor("banks", [P, 8, BANK], F32))
        self.dve_chain = Chain(ctx.enter_context(nc.semaphore("dve_chain")))
        self.act_chain = Chain(ctx.enter_context(nc.semaphore("act_chain")))
        self.root = ctx.enter_context(nc.sbuf_tensor("root", [P, 2, RH], F32))

    def dve_rstd(self, dve, ins, var, work=None):
        v, chain, n = self.nc.vector, self.dve_chain, var.shape[1]
        y, t = work or (self.root[:, 0, 0:n], self.root[:, 1, 0:n])
        chain(dve, ins)
        chain(dve, v.tensor_scalar(t.bitcast(I32), var.bitcast(I32), 1, None, ALU.logical_shift_right))
        chain(dve, v.tensor_scalar(y.bitcast(I32), t.bitcast(I32), -1.0, float(0x5F3759DF), ALU.mult, ALU.add))
        for step in range(3):
            chain(dve, v.scalar_tensor_tensor(t, y, -0.5, y, ALU.mult, ALU.mult))
            chain(dve, v.tensor_tensor(t, t, var, ALU.mult))
            chain(dve, v.scalar_tensor_tensor(y if step < 2 else var, t, 1.5, y, ALU.add, ALU.mult))

    def open_ring(self, es, slots):
        self.ring = es.enter_context(self.nc.sbuf_tensor(f"ring_{self.stage}", [P, slots * 4096], F32))

    def semaphore(self, name):
        self.stage_semaphores.append(self.nc.alloc_semaphore(f"{name}_{self.stage}"))
        return self.stage_semaphores[-1]

    def end_stage(self):
        self.nc.clear_and_free_semaphores(self.stage_semaphores)
        self.nc.all_engine_barrier()
        self.stage_semaphores = []
        self.stage += 1

    def col(self, name, c=0, n=1):
        at = COLS[name][0] + c
        return self.cols[:, at:at + n]

    def row(self, name):
        at, n = ROWS[name]
        return self.dram["rows"][0:1, at:at + n]


def rows_to_all(row):
    return row.to_broadcast([P, row.shape[1]])


class Norm:

    def __init__(self, core, es, tag, gain, xn, first_bank=0):
        self.core, self.gain, self.xn, self.b0 = core, gain, xn, first_bank
        self.diagonal = core.semaphore(f"{tag}_diagonal")
        self.turned = core.semaphore(f"{tag}_turned")
        self.by_act = core.semaphore(f"{tag}_by_act")
        self.by_dve = core.semaphore(f"{tag}_by_dve")

    def dve_scales(self, dve):
        c, v, chain = self.core, self.core.nc.vector, self.core.dve_chain
        for tc in range(TC):
            ins = v.tensor_tensor_reduce(self.xn[:, tc, :], c.x[:, tc, :], c.x[:, tc, :], 1.0, 0.0, ALU.mult,
                                         ALU.add, c.stat[:, tc:tc + 1])
        chain(dve, ins)
        s = c.stat[:, 0:TC]
        c.dve_rstd(dve, v.tensor_scalar(s, s, 1.0 / D, EPS, ALU.mult, ALU.add), s)
        for tc in range(TC):
            v.tensor_scalar(c.diag[:, tc, :], c.ident[:, :], c.stat[:, tc:tc + 1], None, ALU.mult).then_inc(
                self.diagonal, 1)

    def pe_turn(self, pe):
        c = self.core
        pe.wait_ge(self.diagonal, TC)
        for k in range(KC):
            for tc in range(TC):
                at = (k % 2) * T + tc * P
                ins = c.nc.tensor.matmul(c.banks[:, self.b0 + k // 2, at:at + P], c.x[:, tc, k * P:(k + 1) * P],
                                         c.diag[:, tc, :], start=True, stop=True)
            if k % 2:
                ins.then_inc(self.turned, 1)

    def _bank(self, b):
        return self.core.banks[:, self.b0 + b, :]

    def act_take(self, act):
        c = self.core
        for b in (0, 2):
            act.wait_ge(self.turned, b + 1)
            for k in (2 * b, 2 * b + 1):
                c.nc.scalar.activation(c.xT[:, k, :], self._bank(b)[:, (k % 2) * T:(k % 2 + 1) * T], ACT.Copy,
                                       scale=c.col(self.gain, k)).then_inc(self.by_act, 1)

    def dve_take(self, dve):
        c = self.core
        for b in (1, 3):
            dve.wait_ge(self.turned, b + 1)
            for k in (2 * b, 2 * b + 1):
                c.nc.vector.tensor_scalar(c.xT[:, k, :], self._bank(b)[:, (k % 2) * T:(k % 2 + 1) * T],
                                          c.col(self.gain, k), None, ALU.mult).then_inc(self.by_dve, 1)

    def act_high(self, act, high):
        c = self.core
        for k in range(KC):
            act.wait_ge(self.turned, k // 2 + 1)
            c.nc.scalar.activation(high[:, k, :], self._bank(k // 2)[:, (k % 2) * T:(k % 2 + 1) * T], ACT.Copy,
                                   scale=c.col(self.gain, k)).then_inc(self.by_act, 1)

    def dve_low(self, dve, low, high):
        c = self.core
        for k in range(KC):
            dve.wait_ge(self.by_act, k // 2 * 2 + 2)
            c.nc.vector.scalar_tensor_tensor(low[:, k, :], self._bank(k // 2)[:, (k % 2) * T:(k % 2 + 1) * T],
                                             c.col(self.gain, k), high[:, k, :], ALU.mult,
                                             ALU.subtract).then_inc(self.by_dve, 1)

    def wait_parts(self, eng):
        eng.wait_ge(self.by_dve, KC)

    def wait(self, eng):
        eng.wait_ge(self.by_act, 4)
        eng.wait_ge(self.by_dve, 4)


def matmuls(nc, out, lhs, rhs, start=True, stop=True):
    n = len(lhs)
    for i in range(n):
        ins = nc.tensor.matmul(out, lhs[i], rhs[i], start=start and i == 0, stop=stop and i == n - 1)
    return ins


def mixer_stage(c):
    nc, d = c.nc, c.dram
    SEGS = 7
    SB_Q, SB_K, SB_V, R_Q, R_K, R_V, R_G = range(SEGS)
    NORMED = {SB_Q: 0, SB_K: 1, R_Q: 2, R_K: 3}
    VALUES = {SB_V: 0, R_V: 1}
    GAINS = ("sb_q", "sb_k", "ret_q", "ret_k")
    w_in = d["w_in"].rearrange("(k p) n -> p k n", p=P)
    w_out = d["w_out"].rearrange("(k p) n -> p k n", p=P)
    with ExitStack() as es:
        def sb(name, shape, dt=F32):
            return es.enter_context(nc.sbuf_tensor(name, shape, dt))

        def sem(name):
            return c.semaphore(name)

        xn = sb("m_xn", [P, TC, D])
        qk = sb("qk", [P, 4, TC, HW])
        val = sb("val", [P, 2, TC, HW])
        silu_g = sb("silu_g", [P, TC, HW])
        squares = sb("squares", [P, 2, HW])
        ssum = sb("ssum", [P, HEADS])
        gains = sb("gains", [P, 4, HD])
        gn_g = sb("gn_g", [P, HW])
        gn_b = sb("gn_b", [P, HW])
        pos_i = sb("pos_i", [P, TC], I32)
        pos = sb("pos", [P, TC])
        inv_freq = sb("inv_freq", [P, HD // 2])
        angle = sb("angle", [P, 2, TC, HD // 2])
        turns = sb("turns", [P, 2, TC, HD // 2])
        sincos = sb("sincos", [P, 2, TC, HD // 2])
        rope = sb("rope", [P, 4, HW // 2])
        x_in, small_in, rope_in = sem("x_in"), sem("small_in"), sem("rope_in")
        RAW = 4
        THREE = ((0, 0), (0, 1), (1, 0))
        es_parts = es.enter_context(ExitStack())

        def part(name, shape, dt=F32R):
            return es_parts.enter_context(nc.sbuf_tensor(name, shape, dt))

        raw = part("m_raw", [P, RAW, KC, BANK], F32)
        x_part = [part(f"m_x_{n}", [P, KC, T]) for n in ("hi", "lo")]
        w_part = [part(f"m_w_{n}", [P, KC, BANK]) for n in ("hi", "lo")]
        w_seg = [sem(f"w_seg{s}") for s in range(SEGS)]
        norm = Norm(c, es, "mix_norm", "g_mix", xn)
        w_high, w_used = sem("m_w_high"), sem("m_w_used")
        w_low = [sem(f"m_w_low_{by}") for by in ("dve", "pool")]
        squared = sem("squared")
        squares_read = sem("squares_read")
        bank_dve, bank_act = sem("bank_dve"), sem("bank_act")
        angles_done, sines_done = sem("angles_done"), sem("sines_done")

        ORDER = sorted(range(SEGS), key=lambda s: s not in NORMED)

        def bank_of(seg, tc):
            return (ORDER.index(seg) * TC + tc) % 8

        def bank_free(pe, n):
            if n >= 8:
                at, tc = divmod(n - 8, TC)
                pe.wait_ge(bank_dve, at * TC + tc + 1)

        with nc.Block() as block:
            @block.sync
            def _(sp):
                sp.dma_start(c.x[:, :, :], d["x"].rearrange("(c p) n -> p c n", p=P)).then_inc(x_in, 16)
                sp.dma_start(c.ident[:, :], d["ident"]).then_inc(x_in, 16)
                sp.dma_start(c.cols[:, :], d["cols"]).then_inc(x_in, 16)
                for at, s in enumerate(ORDER):
                    if at >= RAW:
                        for low in w_low:
                            sp.wait_ge(low, (at - RAW + 1) * KC // 2)
                    sp.dma_start(raw[:, at % RAW, :, :], w_in[:, :, s * HW:(s + 1) * HW]).then_inc(w_seg[s], 16)
                    if at == 0:
                        sp.dma_start(pos_i[:, :], d["positions"]).then_inc(rope_in, 16)
                        sp.dma_start(inv_freq[:, :], rows_to_all(c.row("inv_freq"))).then_inc(rope_in, 16)
                        for i, g in enumerate(GAINS):
                            sp.dma_start(gains[:, i, :], rows_to_all(c.row(g))).then_inc(small_in, 16)
                        sp.dma_start(gn_g[:, :], rows_to_all(c.row("gn_g"))).then_inc(small_in, 16)
                        sp.dma_start(gn_b[:, :], rows_to_all(c.row("gn_b"))).then_inc(small_in, 16)

            @block.tensor
            def _(pe):
                pe.wait_ge(x_in, 48)
                norm.pe_turn(pe)
                norm.wait_parts(pe)
                for at, s in enumerate(ORDER):
                    for tc in range(TC):
                        bank_free(pe, at * TC + tc)
                    for k in range(KC):
                        pe.wait_ge(w_low[k % 2], (at * KC + k) // 2 + 1)
                        for tc in range(TC):
                            for n, (a, b) in enumerate(THREE):
                                ins = nc.tensor.matmul(
                                    c.banks[:, bank_of(s, tc), :], x_part[a][:, k, tc * P:(tc + 1) * P],
                                    w_part[b][:, k, :], start=k == 0 and n == 0, stop=k == KC - 1 and n == 2)
                        ins.then_inc(w_used, 1)

            def low_part(eng, vec, at, which, first=0, end=KC):
                for k in range(first + which, end, 2):
                    eng.wait_ge(w_high, at * KC + k + 1)
                    vec.tensor_tensor(w_part[1][:, k, :], raw[:, at % RAW, k, :], w_part[0][:, k, :],
                                      ALU.subtract).then_inc(w_low[which], 1)

            @block.gpsimd
            def _(pool):
                for at in range(SEGS):
                    low_part(pool, nc.gpsimd, at, 1)

            @block.scalar
            def _(act):
                act.wait_ge(x_in, 48)
                norm.act_high(act, x_part[0])

                def high_part(at):
                    act.wait_ge(w_seg[ORDER[at]], 16)
                    for k in range(KC):
                        if at:
                            act.wait_ge(w_used, (at - 1) * KC + k + 1)
                        nc.scalar.activation(w_part[0][:, k, :], raw[:, at % RAW, k, :], ACT.Copy).then_inc(w_high, 1)

                high_part(0)
                n_sq = 0
                for at, s in enumerate(ORDER):
                    if at + 1 < SEGS:
                        high_part(at + 1)
                    if at == len(NORMED):
                        act.wait_ge(angles_done, 1)
                        nc.scalar.activation(sincos[:, :, :, :], angle[:, :, :, :], ACT.Sin).then_inc(sines_done, 1)
                    for tc in range(TC):
                        bank = c.banks[:, bank_of(s, tc), :]
                        act.wait_ge(w_used, (at + 1) * KC)
                        if s in NORMED:
                            if n_sq >= 2:
                                act.wait_ge(squares_read, n_sq - 1)
                            nc.scalar.activation(squares[:, n_sq % 2, :], bank, ACT.Square).then_inc(squared, 1)
                            n_sq += 1
                        elif s in VALUES:
                            nc.scalar.activation(val[:, VALUES[s], tc, :], bank, ACT.Copy).then_inc(bank_act, 1)
                        else:
                            nc.scalar.activation(silu_g[:, tc, :], bank, ACT.Silu).then_inc(bank_act, 1)

            @block.vector
            def _(dve):
                chain = c.dve_chain
                dve.wait_ge(x_in, 48)
                norm.dve_scales(dve)
                norm.dve_low(dve, x_part[1], x_part[0])
                low_part(dve, nc.vector, 0, 0)
                dve.wait_ge(rope_in, 32)
                chain(dve, nc.vector.tensor_copy(pos[:, :], pos_i[:, :]))
                MAGIC = 12582912.0
                two_pi = 2 * np.pi
                c1 = 6.28125
                c2 = float(np.float32(two_pi - c1) - np.float32(two_pi - c1) % np.float32(2.0 ** -20))
                c3 = two_pi - c1 - c2
                for tc in range(TC):
                    chain(dve, nc.vector.tensor_scalar(turns[:, 0, tc, :], inv_freq[:, :], pos[:, tc:tc + 1], None,
                                                       ALU.mult))
                for f in range(2):
                    chain(dve, nc.vector.tensor_scalar(angle[:, f, :, :], turns[:, 0, :, :], 1 / two_pi,
                                                       0.25 * f, ALU.mult, ALU.add))
                    chain(dve, nc.vector.tensor_scalar(angle[:, f, :, :], angle[:, f, :, :], MAGIC, None, ALU.add))
                    chain(dve, nc.vector.tensor_scalar(angle[:, f, :, :], angle[:, f, :, :], -MAGIC, None, ALU.add))
                    for i, part in enumerate((c1, c2, c3)):
                        src = turns[:, 0, :, :] if i == 0 else turns[:, 1, :, :]
                        chain(dve, nc.vector.scalar_tensor_tensor(turns[:, 1, :, :], angle[:, f, :, :], -part, src,
                                                                  ALU.mult, ALU.add))
                    chain(dve, nc.vector.tensor_scalar(angle[:, f, :, :], turns[:, 1, :, :], f * np.pi / 2, 3.1415925,
                                                       ALU.add, ALU.min))
                    chain(dve, nc.vector.tensor_scalar(angle[:, f, :, :], angle[:, f, :, :], -3.1415925, None,
                                                       ALU.max))
                dve.nop().then_inc(angles_done, 1)
                dve.wait_ge(small_in, 96)
                n_sq = 0
                for place, s in enumerate(ORDER):
                    if place == 0:
                        low_part(dve, nc.vector, 1, 0)
                    if s not in NORMED:
                        if place + 2 < SEGS:
                            low_part(dve, nc.vector, place + 2, 0)
                        continue
                    at = NORMED[s]
                    for tc in range(TC):
                        bank = c.banks[:, bank_of(s, tc), :]
                        out = qk[:, at, tc, :].rearrange("p (h d) -> p h d", h=HEADS)
                        dve.wait_ge(squared, n_sq + 1)
                        nc.vector.tensor_reduce(ssum[:, :], squares[:, n_sq % 2, :].rearrange(
                            "p (h d) -> p h d", h=HEADS), AX.X, ALU.add).then_inc(squares_read, 1)
                        dve.wait_ge(squares_read, n_sq + 1)
                        c.dve_rstd(dve, nc.vector.tensor_scalar(ssum[:, :], ssum[:, :], 1.0 / HD, EPS, ALU.mult, ALU.add), ssum[:, :])
                        nc.vector.tensor_tensor(out, bank.rearrange("p (h d) -> p h d", h=HEADS),
                                                ssum[:, :].unsqueeze(2).to_broadcast([P, HEADS, HD]),
                                                ALU.mult).then_inc(bank_dve, 1)
                        dve.wait_ge(bank_dve, n_sq + 1)
                        chain(dve, nc.vector.tensor_tensor(out, out, gains[:, at, :].unsqueeze(1).to_broadcast(
                            [P, HEADS, HD]), ALU.mult))
                        if place + 2 < SEGS:
                            low_part(dve, nc.vector, place + 2, 0, KC // 2 * tc, KC // 2 * (tc + 1))
                        n_sq += 1
                dve.wait_ge(sines_done, 1)
                for at in (2, 3):
                    for tc in range(TC):
                        v = qk[:, at, tc, :].rearrange("p (h f d) -> p h f d", h=HEADS, f=2)
                        tmp = [rope[:, i, :].rearrange("p (h d) -> p h d", h=HEADS) for i in range(4)]
                        sin, cos = (sincos[:, f, tc, :].unsqueeze(1).to_broadcast([P, HEADS, HD // 2])
                                    for f in range(2))
                        nc.vector.tensor_tensor(tmp[0], v[:, :, 0, :], cos, ALU.mult)
                        nc.vector.tensor_tensor(tmp[1], v[:, :, 1, :], sin, ALU.mult)
                        nc.vector.tensor_tensor(tmp[2], v[:, :, 1, :], cos, ALU.mult)
                        chain(dve, nc.vector.tensor_tensor(tmp[3], v[:, :, 0, :], sin, ALU.mult))
                        nc.vector.tensor_tensor(v[:, :, 0, :], tmp[0], tmp[1], ALU.subtract)
                        chain(dve, nc.vector.tensor_tensor(v[:, :, 1, :], tmp[2], tmp[3], ALU.add))

        es_parts.close()
        c.open_ring(es, 6)
        DIAG = 2 * P + P
        qkT = c.ring[:, 8192:12288].rearrange("p (a b t) -> p a b t", a=4, b=PAIRS)
        decay = c.ring[:, 12288:15360].rearrange("p (h n) -> p h n", h=HEADS)
        sufsum = sb("sufsum", [P, P])
        allneg = sb("allneg", [P, P])
        soft, positive = (c.ring[:, at:at + HEADS * DIAG].rearrange("p (h n) -> p h n", h=HEADS)
                          for at in (18432, 18432 + HEADS * DIAG))
        weight = sb("weight", [P, 2, DIAG])
        scored = sb("scored", [P, 2, DIAG])
        yT = c.ring[:, 16384:18432].rearrange("p (k t) -> p k t", k=KC)
        yb = sb("yb", [P, TC, HW])
        tmp = sb("gn_tmp", [P, HW])
        mean = sb("gn_mean", [P, 2, HEADS])
        const_in, allneg_done = sem("const_in"), sem("allneg_done")
        w_out_in = sem("w_out_in")
        turned, took_act, took_dve = sem("h_turned"), sem("h_took_act"), sem("h_took_dve")
        z_done, z_read, soft_done, soft_masked = (sem(n) for n in ("z_done", "z_read", "soft_done", "soft_masked"))
        small_exp = sem("small_exp")
        ln_done = sem("ln_done")
        arg_done, exp_done, w_masked = sem("arg_done"), sem("exp_done"), sem("w_masked")
        y_done, y_taken = sem("y_done"), sem("y_taken")
        s_done, s_decayed, r_done = sem("s_done"), sem("s_decayed"), sem("r_done")
        yb_done, yb_turned, yb_taken = sem("yb_done"), sem("yb_turned"), sem("yb_taken")
        mixed = sem("mixed")
        Z, S, A, Y, R = (0, 1), (5, 2), (0, 1, 3, 2), 4, (6, 7)

        def half(h):
            return slice(HD * (h % 2), HD * (h % 2) + HD)

        def scores(out, kT, qT, h, start, stop):
            s, p = half(h), h // 2
            nc.tensor.matmul(out[:, 0:T], kT[s, p, 0:P], qT[s, p, :], start=start, stop=stop,
                             skip_group_check=True)
            return nc.tensor.matmul(out[:, T:DIAG], kT[s, p, P:T], qT[s, p, P:T], start=False, stop=stop,
                                    skip_group_check=True)

        with nc.Block() as block:
            @block.sync
            def _(sp):
                sp.dma_start(sufsum[:, :], d["sufsum"]).then_inc(const_in, 16)
                sp.dma_start(decay, d["decay"].rearrange("p (h n) -> p h n", h=HEADS)).then_inc(
                    const_in, 16)
                sp.dma_start(c.ring[:, 0:KC * D].rearrange("p (k n) -> p k n", k=KC), w_out).then_inc(w_out_in, 16)

            @block.tensor
            def _(pe):
                for g in range(8):
                    for i in range(2):
                        at, p = divmod(2 * g + i, PAIRS)
                        for tc in range(TC):
                            ins = nc.tensor.transpose(
                                c.banks[:, g, i * T + tc * P:i * T + (tc + 1) * P],
                                qk[:, at, tc, p * P:(p + 1) * P], c.ident[:, :])
                    ins.then_inc(turned, 1)
                pe.wait_ge(took_act, 4)
                pe.wait_ge(took_dve, 4)
                pe.wait_ge(const_in, 32)
                pe.wait_ge(allneg_done, 1)
                qT, kT, rqT, rkT = (qkT[:, i, :, :] for i in range(4))

                def first(h):
                    if h >= 2:
                        pe.wait_ge(z_read, h - 1)
                    scores(c.banks[:, Z[h % 2], :], kT, qT, h, True, True).then_inc(z_done, 1)

                def retention_scores(h):
                    if h >= 2:
                        pe.wait_ge(s_decayed, h - 1)
                    scores(c.banks[:, S[h % 2], :], rkT, rqT, h, True, True).then_inc(s_done, 1)

                def second(h):
                    pe.wait_ge(soft_masked, h + 1)
                    if h >= 4:
                        pe.wait_ge(exp_done, h - 3)
                    out, sp = c.banks[:, A[h % 4], :], soft[:, h, :]
                    scores(out, kT, qT, h, True, False)
                    nc.tensor.matmul(out[:, P:T], allneg[:, :], sp[:, T:DIAG], start=False, stop=False,
                                     skip_group_check=True)
                    nc.tensor.matmul(out[:, 0:T], sufsum[:, :], sp[:, 0:T], start=False, stop=True,
                                     skip_group_check=True)
                    nc.tensor.matmul(out[:, T:DIAG], sufsum[:, :], sp[:, T:DIAG], start=False, stop=True,
                                     skip_group_check=True).then_inc(arg_done, 1)

                def values(h):
                    pe.wait_ge(w_masked, h + 1)
                    if h % 2 == 0 and h:
                        pe.wait_ge(y_taken, h // 2)
                    out, w, v = c.banks[half(h), Y, :], weight[:, h % 2, :], val[:, 0, :, h * HD:(h + 1) * HD]
                    nc.tensor.matmul(out[:, P:T], v[:, 1, :], w[:, T:DIAG], start=True, stop=False,
                                     skip_group_check=True)
                    nc.tensor.matmul(out[:, 0:T], v[:, 0, :], w[:, 0:T], start=False, stop=True,
                                     skip_group_check=True).then_inc(y_done, 1)

                def retention_values(h):
                    pe.wait_ge(s_decayed, h + 1)
                    s, v, at = scored[:, h % 2, :], val[:, 1, :, h * HD:(h + 1) * HD], slice(h * HD, (h + 1) * HD)
                    nc.tensor.matmul(c.banks[:, R[0], at], s[:, 0:P], v[:, 0, :], start=True, stop=True)
                    nc.tensor.matmul(c.banks[:, R[1], at], s[:, P:T], v[:, 0, :], start=True, stop=False)
                    nc.tensor.matmul(c.banks[:, R[1], at], s[:, T:DIAG], v[:, 1, :], start=False,
                                     stop=True).then_inc(r_done, 1)

                for h in range(HEADS):
                    first(h)
                    retention_scores(h)
                    if h:
                        retention_values(h - 1)
                retention_values(HEADS - 1)
                pe.wait_ge(z_read, HEADS)
                for h in range(HEADS):
                    second(h)
                    if h:
                        values(h - 1)
                values(HEADS - 1)
                pe.wait_ge(yb_done, TC)
                for p in range(PAIRS):
                    for tc in range(TC):
                        ins = nc.tensor.transpose(c.banks[:, p // 2, (p % 2) * T + tc * P:(p % 2) * T + (tc + 1) * P],
                                                  yb[:, tc, p * P:(p + 1) * P], c.ident[:, :])
                    if p % 2:
                        ins.then_inc(yb_turned, 1)
                pe.wait_ge(y_taken, PAIRS)
                pe.wait_ge(yb_taken, PAIRS)
                pe.wait_ge(w_out_in, 16)
                w = c.ring[:, 0:KC * D].rearrange("p (k n) -> p k n", k=KC)
                for tc in range(TC):
                    for n in range(2):
                        matmuls(nc, c.banks[:, 2 + 2 * tc + n, :],
                                [yT[:, k, tc * P:(tc + 1) * P] for k in range(KC)],
                                [w[:, k, n * BANK:(n + 1) * BANK] for k in range(KC)]).then_inc(mixed, 1)

            SCALED = (0, 3)

            @block.scalar
            def _(act):
                for g in range(0, 8, 2):
                    act.wait_ge(turned, g + 1)
                    at, p = divmod(2 * g, PAIRS)
                    nc.scalar.activation(qkT[:, at, p:p + 2, :].rearrange("p a b -> p (a b)"), c.banks[:, g, :],
                                         ACT.Copy, scale=HD ** -0.5 if at in SCALED else 1.0).then_inc(took_act, 1)

                def exponent(h):
                    act.wait_ge(arg_done, h + 1)
                    if h >= 2:
                        act.wait_ge(y_done, h - 1)
                    nc.scalar.activation(weight[:, h % 2, :], c.banks[:, A[h % 4], 0:DIAG], ACT.Exp).then_inc(
                        exp_done, 1)

                def take(p):
                    act.wait_ge(y_done, 2 * p + 2)
                    nc.scalar.activation(yT[:, p, :], c.banks[:, Y, 0:T], ACT.Copy).then_inc(y_taken, 1)

                for h in range(HEADS):
                    act.wait_ge(z_read, h + 1)
                    nc.scalar.activation(soft[:, h, :], soft[:, h, :], ACT.Exp, scale=-1.0).then_inc(small_exp, 1)
                for h in range(HEADS):
                    act.wait_ge(small_exp, h + 1)
                    nc.scalar.activation(soft[:, h, :], soft[:, h, :], ACT.Ln, bias=1.0).then_inc(ln_done, 1)
                for h in range(HEADS):
                    exponent(h)
                    if h % 2 == 0 and h:
                        take(h // 2 - 1)
                take(PAIRS - 1)
                for b in range(2):
                    act.wait_ge(yb_turned, b + 1)
                    nc.scalar.activation(yT[:, PAIRS + 2 * b:PAIRS + 2 * b + 2, :].rearrange("p a b -> p (a b)"),
                                         c.banks[:, b, :], ACT.Copy).then_inc(yb_taken, 2)

            @block.gpsimd
            def _(pool):
                nc.gpsimd.memset(allneg[:, :], -1.0).then_inc(allneg_done, 1)
                for h in range(HEADS):
                    for src, ready, done in ((soft[:, h, :], soft_done, soft_masked),
                                             (weight[:, h % 2, :], exp_done, w_masked)):
                        pool.wait_ge(ready, h + 1)
                        v = src[:, 0:P]
                        nc.gpsimd.affine_select(out=v, in_=v, compare_op=ALU.is_gt, fill=0.0, base=0,
                                                pattern=[[1, P]], channel_multiplier=-1)
                        v = src[:, T:DIAG]
                        nc.gpsimd.affine_select(out=v, in_=v, compare_op=ALU.is_gt, fill=0.0, base=0,
                                                pattern=[[1, P]], channel_multiplier=-1).then_inc(done, 1)

            @block.vector
            def _(dve):
                chain = c.dve_chain
                for g in range(1, 8, 2):
                    dve.wait_ge(turned, g + 1)
                    at, p = divmod(2 * g, PAIRS)
                    nc.vector.tensor_scalar(qkT[:, at, p:p + 2, :].rearrange("p a b -> p (a b)"), c.banks[:, g, :],
                                            HD ** -0.5 if at in SCALED else 1.0, None, ALU.mult).then_inc(took_dve, 1)
                dve.wait_ge(const_in, 32)

                for h in range(HEADS):
                    z = c.banks[:, Z[h % 2], 0:DIAG]
                    dve.wait_ge(z_done, h + 1)
                    chain(dve, nc.vector.tensor_scalar(positive[:, h, :], z, 0.0, None, ALU.max))
                    nc.vector.scalar_tensor_tensor(soft[:, h, :], positive[:, h, :], 2.0, z, ALU.mult,
                                                   ALU.subtract).then_inc(z_read, 1)
                    dve.wait_ge(s_done, h + 1)
                    if h >= 2:
                        dve.wait_ge(r_done, h - 1)
                    nc.vector.tensor_tensor(scored[:, h % 2, :], c.banks[:, S[h % 2], 0:DIAG], decay[:, h, :],
                                            ALU.mult).then_inc(s_decayed, 1)
                for h in range(HEADS):
                    dve.wait_ge(ln_done, h + 1)
                    nc.vector.tensor_tensor(soft[:, h, :], positive[:, h, :], soft[:, h, :], ALU.add).then_inc(
                        soft_done, 1)
                dve.wait_ge(r_done, HEADS)
                for tc in range(TC):
                    y3 = yb[:, tc, :].rearrange("p (h d) -> p h d", h=HEADS)
                    r3 = c.banks[:, R[tc], :].rearrange("p (h d) -> p h d", h=HEADS)
                    t3 = tmp[:, :].rearrange("p (h d) -> p h d", h=HEADS)
                    mu, var = mean[:, 0, :], mean[:, 1, :]
                    chain(dve, nc.vector.tensor_reduce(mu, r3, AX.X, ALU.add))
                    chain(dve, nc.vector.tensor_scalar(mu, mu, 1.0 / HD, None, ALU.mult))
                    chain(dve, nc.vector.tensor_tensor(y3, r3, mu.unsqueeze(2).to_broadcast([P, HEADS, HD]),
                                                       ALU.subtract))
                    chain(dve, nc.vector.tensor_tensor(t3, y3, y3, ALU.mult))
                    chain(dve, nc.vector.tensor_reduce(var, t3, AX.X, ALU.add))
                    c.dve_rstd(dve, nc.vector.tensor_scalar(var, var, 1.0 / HD, EPS, ALU.mult, ALU.add), var)
                    chain(dve, nc.vector.tensor_tensor(y3, y3, var.unsqueeze(2).to_broadcast([P, HEADS, HD]),
                                                       ALU.mult))
                    chain(dve, nc.vector.tensor_tensor(yb[:, tc, :], yb[:, tc, :], gn_g[:, :], ALU.mult))
                    chain(dve, nc.vector.tensor_tensor(yb[:, tc, :], yb[:, tc, :], gn_b[:, :], ALU.add))
                    nc.vector.tensor_tensor(yb[:, tc, :], yb[:, tc, :], silu_g[:, tc, :], ALU.mult).then_inc(
                        yb_done, 1)
                for tc in range(TC):
                    for n in range(2):
                        dve.wait_ge(mixed, 2 * tc + n + 1)
                        v = c.x[:, tc, n * BANK:(n + 1) * BANK]
                        nc.vector.tensor_tensor(v, v, c.banks[:, 2 + 2 * tc + n, :], ALU.add)


def expert_stage(c):
    nc, d = c.nc, c.dram
    E, E3 = EXPERTS, EXPERTS * (BLOCKS - 1)
    w_up, w_down, b_up = d["w_up"], d["w_down"], d["b_up"]
    COUNT, EXPERT_AT, BLOCK_AT, LIST = 0, 64, 128, 192
    with ExitStack() as es:
        def sb(name, shape, dt=F32):
            return es.enter_context(nc.sbuf_tensor(name, shape, dt))

        def sem(name):
            return c.semaphore(name)

        c.open_ring(es, 6)
        xn = sb("e_xn", [P, TC, D])
        parts = sb("parts", [P, 3, TC, D], BF16)
        w_router = sb("w_router_sb", [P, KC, E])
        b_router = sb("b_router_sb", [P, E])
        upto = sb("upto", [P, P])
        ones = sb("ones", [P, P])
        nothing = sb("nothing", [1, BANK], BF16)
        number = sb("number", [P, BLOCKS * 2 * CAP])
        expert_no = sb("expert_no", [P, E])
        extra_col = sb("extra_col", [P, 3])
        work_list = sb("work_list", [1, LIST], I32)
        logits = sb("logits", [P, TC, E])
        top = sb("top", [P, TC, 8])
        top_i = sb("top_i", [P, TC, 8], U32)
        top_f = sb("top_f", [P, TC, 8])
        neg_max = sb("neg_max", [P, TC])
        gate = sb("gate", [P, TC, TOPK])
        gate_sum = sb("gate_sum", [P, TC])
        hit = sb("hit", [P, 2, TC, TOPK, E])
        gates = sb("gates", [P, TC, E])
        chosen = sb("chosen", [P, TC, BLOCKS - 1, E])
        rank = sb("rank", [P, TC, E])
        y = sb("e_y", [P, BANK])
        spreadT = sb("spreadT", [2 * CAP, T])
        flag = sb("flag", [E3, 1])
        place = sb("place", [E3, 1])
        spot = sb("spot", [E3, MAX_EXTRA])

        norm = Norm(c, es, "ffn_norm", "g_ffn", xn)
        router_in, const_in, list_in = sem("router_in"), sem("r_const_in"), sem("list_in")
        b_down_in = sem("b_down_in")
        xn_ready = sem("xn_ready")
        split_act, split_dve = sem("split_act"), sem("split_dve")
        routed, negated, exped = sem("routed"), sem("negated"), sem("exped")
        marked, counted, flagged, placed, spotted, listed = (sem(n) for n in (
            "marked", "counted", "flagged", "placed", "spotted", "listed"))
        gates_turned = sem("gates_turned")
        up_slot = [c.ring[:, k * 2048:(k + 1) * 2048] for k in range(KC)]
        down_slot = [c.ring[:, (KC + j) * 2048:(KC + j + 1) * 2048].rearrange("p (c n) -> p c n", c=2)
                     for j in range(KC // 2)]
        up_in = [sem(f"up_in{k}") for k in range(KC)]
        down_in = [sem(f"down_in{j}") for j in range(KC // 2)]
        bias_in, bias_cleared = sem("bias_in"), sem("bias_cleared")
        bias = sb("bias", [P, 2 * D])

        def load_up(sp, e, k):
            sp.dma_start(up_slot[k], w_up[bass.ds(e * D + k * P, P), :]).then_inc(up_in[k], 16)

        def load_down(sp, e, j):
            rows = w_down[bass.ds(e * D + j * 2 * P, 2 * P), :].rearrange("(c p) n -> p c n", p=P)
            sp.dma_start(down_slot[j], rows).then_inc(down_in[j], 16)

        def load_bias(sp, e):
            sp.dma_start(bias[0:1, :], b_up[bass.ds(e, 1), :]).then_inc(bias_in, 16)

        with nc.Block() as block:
            @block.sync
            def _(sp):
                sp.dma_start(w_router[:, :, :], d["w_router"].rearrange("(k p) n -> p k n", p=P)).then_inc(
                    router_in, 16)
                sp.dma_start(b_router[:, :], rows_to_all(c.row("b_router"))).then_inc(router_in, 16)
                sp.dma_start(upto[:, :], d["upto"]).then_inc(const_in, 16)
                sp.dma_start(number[:, :], d["number"]).then_inc(const_in, 16)
                sp.dma_start(expert_no[:, :], d["expert_no"]).then_inc(const_in, 16)
                sp.dma_start(extra_col[:, :], d["extra_col"]).then_inc(const_in, 16)
                for h in range(2):
                    sp.dma_start(y[CAP * h:CAP * h + E, :], d["b_down"][:, h * BANK:(h + 1) * BANK]).then_inc(
                        b_down_in, 16)
                sp.dma_start(work_list[:, :], d["work_list"]).then_inc(list_in, 16)
                for k in range(KC):
                    load_up(sp, 0, k)
                    if k == 0:
                        sp.wait_ge(bias_cleared, 1)
                        load_bias(sp, 0)
                for j in range(KC // 2):
                    load_down(sp, 0, j)

            LOGIT, RANK, EXTRA, TURN = 4, 5, 6, 7

            @block.tensor
            def _(pe):
                norm.pe_turn(pe)
                norm.wait(pe)
                pe.wait_ge(router_in, 32)
                for tc in range(TC):
                    matmuls(nc, c.banks[:, LOGIT, tc * E:(tc + 1) * E],
                            [c.xT[:, k, tc * P:(tc + 1) * P] for k in range(KC)],
                            [w_router[:, k, :] for k in range(KC)]).then_inc(routed, 1)
                pe.wait_ge(const_in, 64)
                pe.wait_ge(marked, 2)
                for tc in range(TC):
                    out = c.banks[:, RANK, tc * E:(tc + 1) * E]
                    if tc:
                        nc.tensor.matmul(out, ones[:, :], chosen[:, 0, 0, :], start=True, stop=False)
                    nc.tensor.matmul(out, upto[:, :], chosen[:, tc, 0, :], start=not tc, stop=True)
                for tc in range(TC):
                    nc.tensor.matmul(c.banks[0:E3, EXTRA, 0:1], chosen[:, tc, :, :].rearrange("p b e -> p (b e)"),
                                     ones[:, 0:1], start=tc == 0, stop=tc == 1)
                for lo in (0, CAP):
                    for tc in range(TC):
                        ins = nc.tensor.matmul(c.banks[lo:lo + E, TURN, tc * P:(tc + 1) * P], gates[:, tc, :],
                                               c.ident[:, :], start=True, stop=True)
                ins.then_inc(counted, 1)
                pe.wait_ge(flagged, 1)
                nc.tensor.matmul(c.banks[0:E3, EXTRA, 1:2], upto[0:E3, 0:E3], flag[:, :], start=True,
                                 stop=True).then_inc(placed, 1)
                pe.wait_ge(spotted, 1)
                nc.tensor.matmul(c.banks[0:1, EXTRA, 8:8 + MAX_EXTRA], extra_col[0:E3, 1:2], spot[:, :],
                                 start=True, stop=True)
                nc.tensor.matmul(c.banks[0:1, EXTRA, 32:32 + MAX_EXTRA], extra_col[0:E3, 2:3], spot[:, :],
                                 start=True, stop=True)
                nc.tensor.matmul(c.banks[0:1, EXTRA, 64:65], flag[:, :], ones[0:E3, 0:1],
                                 start=True, stop=True).then_inc(placed, 1)

            @block.scalar
            def _(act):
                norm.act_take(act)
                act.wait_ge(norm.diagonal, TC)
                for tc in range(TC):
                    nc.scalar.activation(xn[:, tc, :], c.x[:, tc, :], ACT.Copy,
                                         scale=c.stat[:, tc:tc + 1]).then_inc(xn_ready, 1)
                act.wait_ge(xn_ready, TC)
                nc.scalar.activation(parts[:, 0, :, :], xn[:, :, :], ACT.Copy).then_inc(split_act, 1)
                act.wait_ge(split_dve, 1)
                nc.scalar.activation(parts[:, 1, :, :], xn[:, :, :], ACT.Copy).then_inc(split_act, 1)
                for tc in range(TC):
                    act.wait_ge(negated, tc + 1)
                    nc.scalar.activation(gate[:, tc, :], top[:, tc, 0:TOPK], ACT.Exp, bias=neg_max[:, tc:tc + 1],
                                         accum_out=gate_sum[:, tc:tc + 1]).then_inc(exped, 1)

            @block.gpsimd
            def _(pool):
                nc.gpsimd.memset(bias[:, :], 0.0).then_inc(bias_cleared, 1)
                pool.drain()
                for lo in (E, CAP + E):
                    nc.gpsimd.memset(y[lo:lo + E, :], 0.0)
                    pool.drain()
                    nc.gpsimd.memset(spreadT[lo:lo + E, :], 0.0)
                    pool.drain()
                nc.gpsimd.memset(nothing[:, :], 0.0)
                pool.drain()
                nc.gpsimd.memset(ones[:, :], 1.0).then_inc(marked, 1)

            @block.vector
            def _(dve):
                chain, v = c.dve_chain, nc.vector
                norm.dve_scales(dve)
                norm.dve_take(dve)
                dve.wait_ge(split_act, 1)
                v.tensor_tensor(xn[:, :, :], xn[:, :, :], parts[:, 0, :, :], ALU.subtract).then_inc(split_dve, 1)
                dve.wait_ge(router_in, 32)
                dve.wait_ge(const_in, 64)
                for tc in range(TC):
                    dve.wait_ge(routed, TC)
                    chain(dve, v.tensor_tensor(logits[:, tc, :], c.banks[:, LOGIT, tc * E:(tc + 1) * E],
                                               b_router[:, :], ALU.add))
                    chain(dve, v.max(top[:, tc, :], logits[:, tc, :]))
                    v.tensor_scalar(neg_max[:, tc:tc + 1], top[:, tc, 0:1], -1.0, None, ALU.mult).then_inc(negated, 1)
                    chain(dve, v.max_index(top_i[:, tc, :], top[:, tc, :], logits[:, tc, :]))
                    chain(dve, v.tensor_copy(top_f[:, tc, :], top_i[:, tc, :]))
                dve.wait_ge(exped, TC)
                chain(dve, v.reciprocal(gate_sum[:, :], gate_sum[:, :]))
                chain(dve, v.tensor_tensor(gate[:, :, :], gate[:, :, :],
                                           gate_sum[:, :].unsqueeze(2).to_broadcast([P, TC, TOPK]), ALU.mult))
                for tc in range(TC):
                    for j in range(TOPK):
                        v.tensor_scalar(hit[:, 0, tc, j, :], expert_no[:, :], top_f[:, tc, j:j + 1], None,
                                        ALU.is_equal)
                        last = v.tensor_scalar(hit[:, 1, tc, j, :], expert_no[:, :], top_f[:, tc, j:j + 1],
                                               gate[:, tc, j:j + 1], ALU.is_equal, ALU.mult)
                chain(dve, last)
                pairs = [hit[:, i, :, :, :] for i in range(2)]
                for pair in pairs:
                    last = v.tensor_tensor(pair[:, :, 0:2, :], pair[:, :, 0:2, :], pair[:, :, 2:4, :], ALU.add)
                chain(dve, last)
                v.tensor_tensor(gates[:, :, :], pairs[1][:, :, 0, :], pairs[1][:, :, 1, :], ALU.add)
                for b in range(BLOCKS - 1):
                    last = v.tensor_tensor(chosen[:, :, b, :], pairs[0][:, :, 0, :], pairs[0][:, :, 1, :], ALU.add)
                chain(dve, last)
                v.nop().then_inc(marked, 1)
                dve.wait_ge(split_act, 2)
                v.tensor_tensor(parts[:, 2, :, :], xn[:, :, :], parts[:, 1, :, :], ALU.subtract)
                dve.wait_ge(counted, 1)
                for tc in range(TC):
                    ins = v.tensor_tensor(rank[:, tc, :], c.banks[:, RANK, tc * E:(tc + 1) * E],
                                          chosen[:, tc, 0, :], ALU.mult)
                chain(dve, ins)
                v.tensor_scalar(rank[:, :, :], rank[:, :, :], -1.0, None, ALU.add)
                for lo in (0, CAP):
                    ins = v.tensor_copy(spreadT[lo:lo + E, :], c.banks[lo:lo + E, TURN, 0:T])
                ins.then_inc(gates_turned, 1)
                v.tensor_tensor(flag[:, :], c.banks[0:E3, EXTRA, 0:1], extra_col[0:E3, 0:1], ALU.is_gt).then_inc(
                    flagged, 1)
                dve.wait_ge(flagged, 1)
                dve.wait_ge(placed, 1)
                chain(dve, v.tensor_tensor(place[:, :], c.banks[0:E3, EXTRA, 1:2], flag[:, :], ALU.mult))
                chain(dve, v.tensor_scalar(place[:, :], place[:, :], -1.0, None, ALU.add))
                v.tensor_scalar(spot[:, :], number[0:E3, 0:MAX_EXTRA], place[:, :], None, ALU.is_equal).then_inc(
                    spotted, 1)
                dve.wait_ge(placed, 2)
                dve.wait_ge(list_in, 16)
                v.tensor_copy(work_list[:, EXPERT_AT + E:EXPERT_AT + E + MAX_EXTRA],
                              c.banks[0:1, EXTRA, 8:8 + MAX_EXTRA])
                v.tensor_copy(work_list[:, BLOCK_AT + E:BLOCK_AT + E + MAX_EXTRA],
                              c.banks[0:1, EXTRA, 32:32 + MAX_EXTRA])
                v.tensor_scalar(work_list[:, COUNT:COUNT + 1], c.banks[0:1, EXTRA, 64:65], float(E), None, ALU.add)

        xsT = sb("xsT", [P, KC, CAP])
        pick = sb("pick", [P, TC, CAP], BF16)
        spread = sb("spread", [P, TC, 2 * CAP])
        glu = sb("glu", [P, BANK])
        sig = sb("sig", [P, BANK])
        lin = sb("lin", [P, BANK])
        act_h = sb("act_h", [P, BANK])
        hT = sb("hT", [P, BANK])
        GLU, LIN, DOWN, TURN, SUM = 0, 1, 2, 3, 4
        picked, spread_ready, spread_turned, spreadT_ready = (sem(n) for n in (
            "picked", "spread_ready", "spread_turned", "spreadT_ready"))
        gathered, xs_ready, up_used, up_done, halves_read = (sem(n) for n in (
            "gathered", "xs_ready", "up_used", "up_done", "halves_read"))
        glu_ready, sig_ready, h_ready, h_turned, hT_ready = (sem(n) for n in (
            "glu_ready", "sig_ready", "h_ready", "h_turned", "hT_ready"))
        down_used, down_done, y_ready, bias_used, summed = (sem(n) for n in (
            "down_used", "down_done", "e_y_ready", "bias_used", "summed"))

        def listed_at(eng, at, top_value):
            return eng.value_load(work_list[0:1, bass.ds(at, 1)], min_val=0, max_val=top_value)

        def count(eng):
            return eng.value_load(work_list[0:1, 0:1], min_val=E, max_val=E + MAX_EXTRA)

        with nc.Block() as block:
            @block.sync
            def _(sp):
                items = count(sp)
                with sp.Fori(1, items) as i:
                    e = listed_at(sp, i + EXPERT_AT, E - 1)
                    for k in range(KC):
                        sp.wait_ge(up_used, i * KC + (k + 1 - KC))
                        load_up(sp, e, k)
                        if k == 0:
                            sp.wait_ge(bias_used, i)
                            load_bias(sp, e)
                    for j in range(KC // 2):
                        sp.wait_ge(down_used, i * (KC // 2) + (j + 1 - KC // 2))
                        load_down(sp, e, j)

            @block.tensor
            def _(pe):
                def gather(n):
                    pe.wait_ge(picked, n + 1)
                    for k in range(KC):
                        out = c.banks[:, TURN, k * CAP:(k + 1) * CAP]
                        ins = matmuls(nc, out,
                                      [parts[:, a, tc, k * P:(k + 1) * P] for tc in range(TC) for a in range(3)],
                                      [pick[:, tc, :] for tc in range(TC) for a in range(3)])
                    ins.then_inc(gathered, 1)

                def combine(stop):
                    for tc in range(TC):
                        for h in range(2):
                            half = slice(CAP * h, CAP * (h + 1))
                            ins = nc.tensor.matmul(c.banks[:, SUM + 2 * tc + h, :],
                                                   spreadT[half, tc * P:(tc + 1) * P], y[half, :],
                                                   start=False, stop=stop)
                    return ins

                items = count(pe)
                for i in range(2 * TC):
                    nc.tensor.matmul(c.banks[:, SUM + i, :], nothing[:, 0:P], nothing[:, :], start=True, stop=False)
                pe.wait_ge(b_down_in, 32)
                pe.nop().then_inc(spread_turned, 1)
                gather(0)
                with pe.Fori(0, items) as i:
                    pe.wait_ge(xs_ready, i + 1)
                    pe.wait_ge(halves_read, i + 1)
                    quarters = [(bank, h, bank * D + h * BANK) for bank in (GLU, LIN) for h in range(2)]
                    for k in range(KC):
                        pe.wait_ge(up_in[k], i * 16 + 16)
                        for bank, h, at in quarters:
                            ins = nc.tensor.matmul(c.banks[CAP * h:CAP * (h + 1), bank, :], xsT[:, k, :],
                                                   up_slot[k][:, at:at + BANK], start=k == 0, stop=k == KC - 1)
                        ins.then_inc(up_used, 1)
                        if k == 0:
                            pe.wait_ge(bias_in, i * 16 + 16)
                            for bank, h, at in quarters:
                                ins = nc.tensor.matmul(c.banks[CAP * h:CAP * (h + 1), bank, :], ones[:, 0:CAP],
                                                       bias[:, at:at + BANK], start=False, stop=False)
                            ins.then_inc(bias_used, 1)
                    pe.wait_ge(y_ready, i + 1)
                    pe.wait_ge(spreadT_ready, i + 1)
                    combine(False)
                    pe.wait_ge(spread_ready, i + 1)
                    for tc in range(TC):
                        ins = nc.tensor.transpose(c.banks[:, DOWN, tc * P:(tc + 1) * P], spread[:, tc, :],
                                                  c.ident[:, :])
                    ins.then_inc(spread_turned, 1)
                    pe.wait_ge(hT_ready, i + 1)
                    gather(i + 1)
                    pe.wait_ge(h_ready, i + 1)
                    pe.wait_ge(xs_ready, i + 2)
                    for j in range(KC // 2):
                        ins = nc.tensor.transpose(c.banks[:, TURN, j * P:(j + 1) * P],
                                                  act_h[:, j * P:(j + 1) * P], c.ident[:, :])
                    ins.then_inc(h_turned, 1)
                    pe.wait_ge(hT_ready, i + 2)
                    pe.wait_ge(spreadT_ready, i + 2)
                    for k in range(KC):
                        at = (k % 4) * P + (k // 4) * CAP
                        if k % 2 == 0:
                            pe.wait_ge(down_in[k // 2], i * 16 + 16)
                        for h in range(2):
                            ins = nc.tensor.matmul(c.banks[CAP * h:CAP * (h + 1), DOWN, :], hT[:, at:at + CAP],
                                                   down_slot[k // 2][:, k % 2, h * BANK:(h + 1) * BANK],
                                                   start=k == 0, stop=k == KC - 1)
                        if k % 2:
                            ins.then_inc(down_used, 1)
                pe.wait_ge(y_ready, items + 1)
                pe.wait_ge(spreadT_ready, items + 1)
                combine(True).then_inc(summed, 1)

            @block.scalar
            def _(act):
                items = count(act)
                for s in (spreadT_ready, hT_ready, y_ready):
                    act.nop().then_inc(s, 1)
                with act.Fori(0, items) as i:
                    act.wait_ge(glu_ready, i + 1)
                    nc.scalar.activation(sig[:, :], glu[:, :], ACT.Sigmoid, scale=ALPHA).then_inc(sig_ready, 1)
                    act.wait_ge(spread_turned, i + 2)
                    nc.scalar.activation(spreadT[:, :], c.banks[:, DOWN, 0:T], ACT.Copy).then_inc(spreadT_ready, 1)
                    act.wait_ge(h_turned, i + 1)
                    nc.scalar.activation(hT[:, :], c.banks[:, TURN, :], ACT.Copy).then_inc(hT_ready, 1)
                    act.wait_ge(down_used, i * (KC // 2) + KC // 2)
                    nc.scalar.activation(y[:, :], c.banks[:, DOWN, :], ACT.Copy).then_inc(y_ready, 1)

            @block.vector
            def _(dve):
                v = nc.vector

                def pick_item(e, b):
                    for tc in range(TC):
                        ins = v.tensor_scalar(pick[:, tc, :], number[:, bass.ds(b * (2 * CAP), CAP)],
                                              rank[:, tc, bass.ds(e, 1)], None, ALU.is_equal)
                    ins.then_inc(picked, 1)

                def take_gathered():
                    v.tensor_tensor(xsT[:, :, :], c.banks[:, TURN, :].rearrange("p (k s) -> p k s", k=KC),
                                    c.col("g_ffn", 0, KC).unsqueeze(2).to_broadcast([P, KC, CAP]),
                                    ALU.mult).then_inc(xs_ready, 1)

                items = count(dve)
                v.nop().then_inc(halves_read, 1)
                pick_item(0, 0)
                dve.wait_ge(gathered, 1)
                take_gathered()
                with dve.Fori(0, items) as i:
                    e = listed_at(dve, i + EXPERT_AT, E - 1)
                    b = listed_at(dve, i + BLOCK_AT, BLOCKS - 1)
                    dve.wait_ge(spread_turned, i + 1)
                    for tc in range(TC):
                        ins = v.tensor_scalar(spread[:, tc, :], number[:, bass.ds(b * (2 * CAP), 2 * CAP)],
                                              rank[:, tc, bass.ds(e, 1)], gates[:, tc, bass.ds(e, 1)],
                                              ALU.is_equal, ALU.mult)
                    ins.then_inc(spread_ready, 1)
                    dve.wait_ge(gathered, i + 1)
                    pick_item(listed_at(dve, i + (EXPERT_AT + 1), E - 1), listed_at(dve, i + (BLOCK_AT + 1),
                                                                                   BLOCKS - 1))
                    dve.wait_ge(up_used, i * KC + KC)
                    v.tensor_scalar(glu[:, :], c.banks[:, GLU, :], LIMIT, None, ALU.min).then_inc(glu_ready, 1)
                    v.tensor_scalar(lin[:, :], c.banks[:, LIN, :], LIMIT, -LIMIT, ALU.min, ALU.max).then_inc(
                        halves_read, 1)
                    dve.wait_ge(glu_ready, i + 1)
                    dve.wait_ge(halves_read, i + 2)
                    v.scalar_tensor_tensor(lin[:, :], lin[:, :], 1.0, glu[:, :], ALU.add, ALU.mult)
                    dve.drain()
                    dve.wait_ge(sig_ready, i + 1)
                    v.tensor_tensor(act_h[:, :], lin[:, :], sig[:, :], ALU.mult).then_inc(h_ready, 1)
                    dve.wait_ge(gathered, i + 2)
                    take_gathered()
                dve.wait_ge(summed, 1)
                for tc in range(TC):
                    for h in range(2):
                        s = c.x[:, tc, h * BANK:(h + 1) * BANK]
                        v.tensor_tensor(s, s, c.banks[:, SUM + 2 * tc + h, :], ALU.add)


def embedding_stage(c):
    nc, d = c.nc, c.dram
    PK = PLE // P
    with ExitStack() as es:
        def sb(name, shape, dt=F32):
            return es.enter_context(nc.sbuf_tensor(name, shape, dt))

        def sem(name):
            return c.semaphore(name)

        c.open_ring(es, 7)
        xn = sb("p_xn", [P, TC, D])
        pT = sb("pT", [P, PK, T])
        w_proj = sb("w_proj", [P, PK, D])
        opened = sb("opened", [P, 2, BANK])
        part = sb("part", [P, BANK])
        w_gate = c.ring[:, 0:KC * D].rearrange("p (k n) -> p k n", k=KC)
        norm = Norm(c, es, "ple_norm", "g_ple", xn)
        gate_in, proj_in = [sem(f"gate_in{h}") for h in range(2)], sem("proj_in")
        gate_done, proj_done, sig_done, sig_used = (sem(n) for n in (
            "gate_done", "proj_done", "p_sig_done", "p_sig_used"))
        with nc.Block() as block:
            @block.sync
            def _(sp):
                sp.dma_start(pT[:, :, :], d["pT"].rearrange("(k p) t -> p k t", p=P)).then_inc(proj_in, 16)
                sp.dma_start(w_proj[:, :, :], d["w_ple_proj"].rearrange("(k p) n -> p k n", p=P)).then_inc(
                    proj_in, 16)
                w = d["w_ple_gate"].rearrange("(k p) n -> p k n", p=P)
                for h in range(2):
                    sp.dma_start(w_gate[:, 4 * h:4 * h + 4, :], w[:, 4 * h:4 * h + 4, :]).then_inc(gate_in[h], 16)

            @block.tensor
            def _(pe):
                pe.wait_ge(proj_in, 32)
                for tc in range(TC):
                    for n in range(2):
                        matmuls(nc, c.banks[:, 4 + 2 * tc + n, :],
                                [pT[:, k, tc * P:(tc + 1) * P] for k in range(PK)],
                                [w_proj[:, k, n * BANK:(n + 1) * BANK] for k in range(PK)]).then_inc(proj_done, 1)
                norm.pe_turn(pe)
                norm.wait(pe)
                for h in range(2):
                    pe.wait_ge(gate_in[h], 16)
                for tc in range(TC):
                    for n in range(2):
                        matmuls(nc, c.banks[:, 2 * tc + n, :],
                                [c.xT[:, k, tc * P:(tc + 1) * P] for k in range(KC)],
                                [w_gate[:, k, n * BANK:(n + 1) * BANK] for k in range(KC)]).then_inc(gate_done, 1)

            @block.scalar
            def _(act):
                norm.act_take(act)
                for i in range(2 * TC):
                    act.wait_ge(gate_done, i + 1)
                    if i >= 2:
                        act.wait_ge(sig_used, i - 1)
                    nc.scalar.activation(opened[:, i % 2, :], c.banks[:, i, :], ACT.Sigmoid).then_inc(sig_done, 1)

            @block.vector
            def _(dve):
                norm.dve_scales(dve)
                norm.dve_take(dve)
                dve.wait_ge(proj_done, 4)
                for i in range(2 * TC):
                    dve.wait_ge(sig_done, i + 1)
                    c.dve_chain(dve, nc.vector.tensor_tensor(part[:, :], c.banks[:, 4 + i, :], opened[:, i % 2, :],
                                                             ALU.mult))
                    s = c.x[:, i // 2, (i % 2) * BANK:(i % 2 + 1) * BANK]
                    nc.vector.tensor_tensor(s, s, part[:, :], ALU.add).then_inc(sig_used, 1)
                    dve.wait_ge(sig_used, i + 1)


def gating_stage(c):
    nc, d = c.nc, c.dram
    NB = SGU // BANK
    FK = SGU // P
    FB = BANK // P
    THREE = ((0, 0), (0, 1), (1, 0))
    with ExitStack() as es:
        def sem(name):
            return c.semaphore(name)

        c.open_ring(es, 2)
        raw = [c.ring[:, s * 4096:(s + 1) * 4096] for s in range(2)]
        y_part = [es.enter_context(nc.sbuf_tensor(f"g_y_{n}", [P, FK, T], F32R)) for n in ("hi", "lo")]
        w_raw = [sem(f"g_w{j}") for j in range(2 * NB)]
        out_in = [sem(f"g_out_in{q}") for q in range(4)]
        w_in = d["sgu_in"].rearrange("(k p) n -> p k n", p=P)
        w_out = d["sgu_out"].rearrange("(k p) n -> p k n", p=P)
        col_of = [SGU + j * BANK for j in range(NB)] + [j * BANK for j in range(NB)]

        OUT0 = 2 * NB * KC
        def sb(name, shape, dt=F32):
            return es.enter_context(nc.sbuf_tensor(name, shape, dt))

        xn = sb("g_xn", [P, TC, D])
        v_t = sb("v_t", [P, TC, SGU])
        uT = sb("uT", [P, FK, T])
        w_sT = sb("w_sT_sb", [P, GROUPS, P])
        b_v = sb("b_v_sb", [P, SGU])
        ln_g = sb("ln_g_sb", [P, SGU])
        ln_b = sb("ln_b_sb", [P, SGU])
        b_s = b_v[:, :].rearrange("p (g i) -> p g i", g=GROUPS)
        sums = sb("g_sums", [P, TC, NB])
        mom = sb("g_mom", [P, 2, TC])
        centred = xn[:, :, :].rearrange("p c n -> p (c n)")
        x_part = [sb(f"g_x_{n}", [P, KC, T], F32R) for n in ("hi", "lo")]
        w_part = [sb(f"g_w_{n}", [P, KC, BANK], F32R) for n in ("hi", "lo")]
        norm = Norm(c, es, "sgu_norm", "n_mix0", xn)

        def out_place(part, f):
            at = 2 * (f % 4)
            return w_part[part][:, at:at + 2, :].rearrange("p k n -> p (k n)")

        def out_raw(f):
            return raw[f // 4 % 2][:, (f % 4) * D:(f % 4 + 1) * D]

        rows_in, b_s_in, ws_in, masked = (sem(n) for n in ("g_rows_in", "b_s_in", "ws_in", "ws_masked"))
        w_high, w_low, w_used = (sem(n) for n in (
            "g_w_high", "g_w_low", "g_w_used"))
        v_biased, v_gelu, v_centred, v_square, v_ready = (sem(n) for n in (
            "v_biased", "v_gelu", "v_centred", "v_square", "v_ready"))
        u_ready, s_done, y_ready, y_high, y_low = (sem(n) for n in (
            "u_ready", "gs_done", "g_y_ready", "g_y_high", "g_y_low"))

        with nc.Block() as block:
            @block.sync
            def _(sp):
                for j in range(2 * NB):
                    if j >= 2:
                        sp.wait_ge(w_low, KC * (j - 1))
                    sp.dma_start(raw[j % 2].rearrange("p (k n) -> p k n", k=KC),
                                 w_in[:, :, col_of[j]:col_of[j] + BANK]).then_inc(w_raw[j], 16)
                    if j == 1:
                        sp.dma_start(b_v[:, :], rows_to_all(c.row("b_v"))).then_inc(rows_in, 16)
                        sp.dma_start(ln_g[:, :], rows_to_all(c.row("ln_g"))).then_inc(rows_in, 16)
                        sp.dma_start(ln_b[:, :], rows_to_all(c.row("ln_b"))).then_inc(rows_in, 16)
                        sp.dma_start(w_sT[:, :, :].rearrange("p g i -> p (g i)"), d["w_sT"]).then_inc(ws_in, 16)
                sp.wait_ge(v_biased, NB * TC)
                sp.dma_start(b_v[:, :], rows_to_all(c.row("b_s"))).then_inc(b_s_in, 16)
                for q in range(4):
                    sp.wait_ge(w_low, KC * (2 * NB - 1 + q) if q < 2 else OUT0 + 4 * (q - 1))
                    sp.dma_start(raw[q % 2].rearrange("p (k n) -> p k n", k=4),
                                 w_out[:, 4 * q:4 * q + 4, :]).then_inc(out_in[q], 16)

            @block.tensor
            def _(pe):
                norm.pe_turn(pe)
                norm.wait_parts(pe)
                for j in range(NB):
                    for k in range(KC):
                        pe.wait_ge(w_low, KC * j + k + 1)
                        for tc in range(TC):
                            for n, (a, b) in enumerate(THREE):
                                ins = nc.tensor.matmul(
                                    c.banks[:, j * TC + tc, :], x_part[a][:, k, tc * P:(tc + 1) * P],
                                    w_part[b][:, k, :], start=k == 0 and n == 0, stop=k == KC - 1 and n == 2)
                        ins.then_inc(w_used, 1)
                for j in range(NB, 2 * NB):
                    if j < NB + 2:
                        pe.wait_ge(v_biased, 4 * (j - NB + 1))
                    else:
                        pe.wait_ge(u_ready, FB * (j - NB - 1))
                    for k in range(KC):
                        pe.wait_ge(w_low, KC * j + k + 1)
                        for f in range(FB):
                            for n, (a, b) in enumerate(THREE):
                                ins = nc.tensor.matmul(
                                    c.banks[:, (j % 2) * FB + f, 0:T], w_part[a][:, k, f * P:(f + 1) * P],
                                    x_part[b][:, k, :], start=k == 0 and n == 0, stop=k == KC - 1 and n == 2)
                        ins.then_inc(w_used, 1)
                pe.wait_ge(masked, 1)
                pe.wait_ge(v_ready, TC)
                for g in range(GROUPS):
                    if g % 2 == 0:
                        pe.wait_ge(u_ready, FK // 2 + g // 2 + 1)
                    for tc in range(TC):
                        at = (g % 2) * T + tc * P
                        ins = nc.tensor.matmul(c.banks[:, g // 2, at:at + P], v_t[:, tc, g * P:(g + 1) * P],
                                               w_sT[:, g, :], start=True, stop=True)
                    if g % 2:
                        ins.then_inc(s_done, 1)
                pe.wait_ge(y_low, TC * 2)
                for f in range(FK):
                    pe.wait_ge(w_low, OUT0 + f + 1)
                    pe.wait_ge(y_low, max(f // 2 + 1, TC * 2))
                    for tc in range(TC):
                        for n, (a, b) in enumerate(THREE):
                            for h in range(2):
                                ins = nc.tensor.matmul(
                                    c.banks[:, 2 * tc + h, :], y_part[a][:, f, tc * P:(tc + 1) * P],
                                    out_place(b, f)[:, h * BANK:(h + 1) * BANK],
                                    start=f == 0 and n == 0, stop=f == FK - 1 and n == 2)
                    ins.then_inc(w_used, 1)

            @block.scalar
            def _(act):
                def high(j):
                    act.wait_ge(w_raw[j], 16)
                    for k in range(KC):
                        if j:
                            act.wait_ge(w_used, KC * (j - 1) + k + 1)
                        nc.scalar.activation(w_part[0][:, k, :], raw[j % 2][:, k * BANK:(k + 1) * BANK],
                                             ACT.Copy).then_inc(w_high, 1)

                def gelu_u(j):
                    act.wait_ge(w_used, KC * (j + 1))
                    for f in range(FB):
                        at = FB * (j - NB) + f
                        nc.scalar.activation(uT[:, at, :], c.banks[:, (j % 2) * FB + f, 0:T], ACT.Gelu,
                                             bias=c.col("b_u", at)).then_inc(u_ready, 1)

                norm.act_high(act, x_part[0])
                high(0)
                for j in range(NB):
                    high(j + 1)
                    for tc in range(TC):
                        act.wait_ge(v_biased, j * TC + tc + 1)
                        s = v_t[:, tc, j * BANK:(j + 1) * BANK]
                        nc.scalar.activation(s, s, ACT.Gelu, accum_out=sums[:, tc, j:j + 1]).then_inc(v_gelu, 1)
                high(NB + 1)
                for tc in range(TC):
                    act.wait_ge(v_centred, 1)
                    act.wait_ge(v_square, tc)
                    nc.scalar.activation(centred, v_t[:, tc, :], ACT.Square, bias=mom[:, 0, tc:tc + 1],
                                         accum_out=mom[:, 1, tc:tc + 1]).then_inc(v_square, 1)
                gelu_u(NB)
                for j in range(NB + 1, 2 * NB):
                    if j + 1 < 2 * NB:
                        high(j + 1)
                    gelu_u(j)
                def high_out(f):
                    act.wait_ge(out_in[f // 4], 16)
                    act.wait_ge(w_used, OUT0 + f - 3 if f >= 4 else OUT0 - KC + 2 * f + 2)
                    nc.scalar.activation(out_place(0, f), out_raw(f), ACT.Copy).then_inc(w_high, 1)

                for f in range(4):
                    high_out(f)
                for b in range(GROUPS // 2):
                    act.wait_ge(y_ready, b + 1)
                    nc.scalar.activation(y_part[0][:, 2 * b:2 * b + 2, :], uT[:, 2 * b:2 * b + 2, :],
                                         ACT.Copy).then_inc(y_high, 1)
                for f in range(4, FK):
                    high_out(f)

            @block.gpsimd
            def _(pool):
                pool.wait_ge(ws_in, 16)
                nc.gpsimd.memset(w_sT[P // 2:P, :, 0:P // 2], 0.0).then_inc(masked, 1)

            @block.vector
            def _(dve):
                chain, v = c.dve_chain, nc.vector

                def low(j, first=0, last=KC):
                    for k in range(first, last):
                        dve.wait_ge(w_high, KC * j + k + 1)
                        v.tensor_tensor(w_part[1][:, k, :], raw[j % 2][:, k * BANK:(k + 1) * BANK],
                                        w_part[0][:, k, :], ALU.subtract).then_inc(w_low, 1)

                norm.dve_scales(dve)
                norm.dve_low(dve, x_part[1], x_part[0])
                low(0)
                dve.wait_ge(rows_in, 48)
                for j in range(NB):
                    low(j + 1)
                    dve.wait_ge(w_used, KC * (j + 1))
                    for tc in range(TC):
                        v.tensor_tensor(v_t[:, tc, j * BANK:(j + 1) * BANK], c.banks[:, j * TC + tc, :],
                                        b_v[:, j * BANK:(j + 1) * BANK], ALU.add).then_inc(v_biased, 1)
                low(NB + 1, 0, 2)
                dve.wait_ge(v_gelu, NB * TC)
                chain(dve, v.tensor_reduce(mom[:, 0, :], sums[:, :, :], AX.X, ALU.add))
                v.tensor_scalar(mom[:, 0, :], mom[:, 0, :], -1.0 / SGU, None, ALU.mult).then_inc(v_centred, 1)
                low(NB + 1, 2)
                low(NB + 2, 0, 2)
                dve.wait_ge(v_square, TC)
                var = mom[:, 1, :]
                c.dve_rstd(dve, v.tensor_scalar(var, var, 1.0 / SGU, LN_EPS, ALU.mult, ALU.add), var)
                for tc in range(TC):
                    for half in range(2):
                        low(*((NB + 2, 2, 5), (NB + 2, 5, 8), (NB + 3, 0, 4), (NB + 3, 4, 8))[2 * tc + half])
                        s = v_t[:, tc, :]
                        if not half:
                            chain(dve, v.scalar_tensor_tensor(s, s, mom[:, 0, tc:tc + 1], ln_g[:, :], ALU.add,
                                                              ALU.mult))
                        else:
                            v.scalar_tensor_tensor(s, s, mom[:, 1, tc:tc + 1], ln_b[:, :], ALU.mult,
                                                   ALU.add).then_inc(v_ready, 1)
                def low_out(f):
                    dve.wait_ge(w_high, OUT0 + f + 1)
                    v.tensor_tensor(out_place(1, f), out_raw(f), out_place(0, f), ALU.subtract).then_inc(
                        w_low, 1)

                dve.wait_ge(b_s_in, 16)
                for b in range(GROUPS // 2 + 1):
                    if b < GROUPS // 2:
                        dve.wait_ge(s_done, b + 1)
                        bank = c.banks[:, b, :].rearrange("p (g c i) -> p g c i", g=2, c=TC)
                        chain(dve, v.tensor_tensor(bank, bank, b_s[:, 2 * b:2 * b + 2, :].unsqueeze(
                            2).to_broadcast([P, 2, TC, P]), ALU.add))
                        s = uT[:, 2 * b:2 * b + 2, :].rearrange("p g t -> p (g t)")
                        v.tensor_tensor(s, c.banks[:, b, :], s, ALU.mult).then_inc(y_ready, 1)
                    if b:
                        dve.wait_ge(y_high, b)
                        at = slice(2 * b - 2, 2 * b)
                        v.tensor_tensor(y_part[1][:, at, :], uT[:, at, :], y_part[0][:, at, :],
                                        ALU.subtract).then_inc(y_low, 1)
                    if b in (1, 3, 5, 7):
                        low_out(b // 2)
                for f in range(4, FK):
                    low_out(f)
                dve.wait_ge(w_used, OUT0 + FK)
                for tc in range(TC):
                    v.tensor_tensor(c.x[:, tc, :], c.x[:, tc, :],
                                    c.banks[:, 2 * tc:2 * tc + 2, :].rearrange("p h n -> p (h n)"), ALU.add)


def ffn_stage(c, layer):
    nc, d = c.nc, c.dram
    NB = FF // BANK
    FC = BANK // P
    with ExitStack() as es:
        def sb(name, shape, dt=F32):
            return es.enter_context(nc.sbuf_tensor(f"f{layer}_{name}", shape, dt))

        def sem(name):
            return c.semaphore(f"f{layer}_{name}")

        c.open_ring(es, 4)
        xn = sb("xn", [P, TC, D])
        xT_hi, xT_lo = sb("xT_hi", [P, KC, T], F32R), sb("xT_lo", [P, KC, T], F32R)
        w1_hi, w1_lo = sb("w1_hi", [P, FC, KC, P], F32R), sb("w1_lo", [P, FC, KC, P], F32R)
        w2_hi, w2_lo = sb("w2_hi", [P, FC, D], F32R), sb("w2_lo", [P, FC, D], F32R)
        relu = sb("relu", [P, FC, T])
        square = sb("square", [P, FC, T])
        h_hi, h_lo = sb("h_hi", [P, FC, T], F32R), sb("h_lo", [P, FC, T], F32R)
        norm = Norm(c, es, f"ffn{layer}_norm", f"n_ffn{layer}", xn)
        w1_in, w2_in = [[sem(f"w{w}_in{s}") for s in range(2)] for w in (1, 2)]
        w1_high, w1_low, w2_high, w2_low = (sem(n) for n in ("w1_high", "w1_low", "w2_high", "w2_low"))
        up_done, relu_done, h_high, h_low, down_done = (sem(n) for n in (
            "up_done", "relu_done", "h_high", "h_low", "down_done"))
        w1_raw = [c.ring[:, s * 4096:(s + 1) * 4096].rearrange("p (k n) -> p k n", k=KC) for s in range(2)]
        w2_raw = [c.ring[:, (2 + s) * 4096:(3 + s) * 4096].rearrange("p (k n) -> p k n", k=FC) for s in range(2)]
        w1 = d["ffn_w1"][layer * D:(layer + 1) * D, :].rearrange("(k p) n -> p k n", p=P)
        w2 = d["ffn_w2"][layer * FF:(layer + 1) * FF, :]
        OUT = 4

        def turns(chunk_work, split1, split2):
            for j in range(FC):
                chunk_work(j)
                split1(j)
                if j >= 2:
                    split2(j - 2)
            split2(FC - 2)
            split2(FC - 1)

        def blocks(eng, body):
            with eng.Fori(0, NB // 2 - 1) as i:
                for s in range(2):
                    body(i, s, False)
            for s in range(2):
                body(NB // 2 - 1, s, s == 1)

        with nc.Block() as block:
            @block.sync
            def _(sp):
                def load1(s, b):
                    sp.dma_start(w1_raw[s], w1[:, :, bass.ds(b * BANK, BANK)]).then_inc(w1_in[s], 16)

                def load2(s, b):
                    sp.dma_start(w2_raw[s], w2[bass.ds(b * BANK, BANK), :].rearrange(
                        "(k p) n -> p k n", p=P)).then_inc(w2_in[s], 16)

                for s in range(2):
                    load1(s, s)
                    load2(s, s)
                with sp.Fori(1, NB // 2) as i:
                    for s in range(2):
                        sp.wait_ge(w1_low, i * (2 * FC) + (s - 1) * FC)
                        load1(s, i * 2 + s)
                        sp.wait_ge(w2_low, i * (2 * FC) + (s - 1) * FC)
                        load2(s, i * 2 + s)

            @block.tensor
            def _(pe):
                for i in range(2 * TC):
                    nc.tensor.matmul(c.banks[:, OUT + i, :], c.ident[:, :],
                                     c.x[:, i // 2, (i % 2) * BANK:(i % 2 + 1) * BANK], start=True, stop=False)
                norm.pe_turn(pe)
                pe.nop().then_inc(down_done, FC)
                norm.wait_parts(pe)

                def body(i, s, last):
                    chunks = i * (2 * FC) + s * FC

                    def up(j):
                        pe.wait_ge(w1_low, chunks + (j + 1))
                        pe.wait_ge(relu_done, chunks + (j + 1))
                        for k in range(KC):
                            for n, (w, x) in enumerate(((w1_hi, xT_hi), (w1_hi, xT_lo), (w1_lo, xT_hi))):
                                ins = nc.tensor.matmul(c.banks[:, j, 0:T], w[:, j, k, :], x[:, k, :],
                                                       start=k == 0 and n == 0, stop=k == KC - 1 and n == 2)
                        ins.then_inc(up_done, 1)

                    def down(j):
                        pe.wait_ge(h_low, chunks + (j + 1 + FC))
                        pe.wait_ge(w2_low, chunks + (j + 1))
                        for tc in range(TC):
                            for n, (h, w) in enumerate(((h_hi, w2_hi), (h_hi, w2_lo), (h_lo, w2_hi))):
                                for o in range(2):
                                    ins = nc.tensor.matmul(
                                        c.banks[:, OUT + 2 * tc + o, :], h[:, j, tc * P:(tc + 1) * P],
                                        w[:, j, o * BANK:(o + 1) * BANK], start=False,
                                        stop=last and j == FC - 1 and n == 2)
                        ins.then_inc(down_done, 1)

                    up(0)
                    up(1)
                    down(0)
                    up(2)
                    down(1)
                    up(3)
                    down(2)
                    down(3)

                blocks(pe, body)

            @block.scalar
            def _(act):
                norm.act_high(act, xT_hi)

                def high1(s, count, j):
                    act.wait_ge(w1_in[s], count)
                    nc.scalar.activation(w1_hi[:, j, :, :], w1_raw[s][:, :, j * P:(j + 1) * P],
                                         ACT.Copy).then_inc(w1_high, 1)

                def high2(s, count, j):
                    act.wait_ge(w2_in[s], count)
                    nc.scalar.activation(w2_hi[:, j, :], w2_raw[s][:, j, :], ACT.Copy).then_inc(w2_high, 1)

                for j in range(FC):
                    high1(0, 16, j)
                for j in range(FC):
                    high2(0, 16, j)
                act.nop().then_inc(relu_done, FC)

                def body(i, s, last):
                    chunks = i * (2 * FC) + s * FC
                    nxt, count = 1 - s, i * 16 + (16 + 16 * s)

                    def work(j):
                        act.wait_ge(up_done, chunks + (j + 1))
                        act.wait_ge(h_low, chunks + (j + 1))
                        nc.scalar.activation(relu[:, j, :], c.banks[:, j, 0:T], ACT.Relu).then_inc(relu_done, 1)
                        act.wait_ge(relu_done, chunks + (j + 1 + FC))
                        act.wait_ge(down_done, chunks + (j + 1))
                        nc.scalar.activation(h_hi[:, j, :], relu[:, j, :], ACT.Square).then_inc(h_high, 1)

                    def split1(j):
                        if not last:
                            high1(nxt, count, j)

                    def split2(j):
                        if not last:
                            act.wait_ge(down_done, chunks + (j + 1 + FC))
                            high2(nxt, count, j)

                    turns(work, split1, split2)

                blocks(act, body)

            @block.vector
            def _(dve):
                vec = nc.vector
                norm.dve_scales(dve)
                norm.dve_low(dve, xT_lo, xT_hi)

                def low1(s, count, j):
                    dve.wait_ge(w1_high, count)
                    vec.tensor_tensor(w1_lo[:, j, :, :], w1_raw[s][:, :, j * P:(j + 1) * P], w1_hi[:, j, :, :],
                                      ALU.subtract).then_inc(w1_low, 1)

                def low2(s, count, j):
                    dve.wait_ge(w2_high, count)
                    vec.tensor_tensor(w2_lo[:, j, :], w2_raw[s][:, j, :], w2_hi[:, j, :],
                                      ALU.subtract).then_inc(w2_low, 1)

                for j in range(FC):
                    low1(0, j + 1, j)
                for j in range(FC):
                    low2(0, j + 1, j)
                dve.nop().then_inc(h_low, FC)

                def body(i, s, last):
                    chunks = i * (2 * FC) + s * FC
                    nxt = 1 - s

                    def work(j):
                        dve.wait_ge(relu_done, chunks + (j + 1 + FC))
                        vec.tensor_tensor(square[:, j, :], relu[:, j, :], relu[:, j, :], ALU.mult)
                        dve.drain()
                        dve.wait_ge(h_high, chunks + (j + 1))
                        vec.tensor_tensor(h_lo[:, j, :], square[:, j, :], h_hi[:, j, :], ALU.subtract).then_inc(
                            h_low, 1)

                    def split1(j):
                        if not last:
                            low1(nxt, chunks + (FC + j + 1), j)

                    def split2(j):
                        if not last:
                            low2(nxt, chunks + (FC + j + 1), j)

                    turns(work, split1, split2)

                blocks(dve, body)
                dve.wait_ge(down_done, (NB + 1) * FC)
                for i in range(2 * TC):
                    vec.tensor_copy(c.x[:, i // 2, (i % 2) * BANK:(i % 2 + 1) * BANK], c.banks[:, OUT + i, :])


def rwkv_stage(c):
    nc, d = c.nc, c.dram
    H2 = 2 * HD
    RP = RH // 2
    NCH = T // CH
    J = P // CH
    DECAY = float(np.exp(-0.5))
    UNIT = TC * D
    LORA = 64
    with ExitStack() as es:
        def sb(name, shape, dt=F32):
            return es.enter_context(nc.sbuf_tensor(f"w_{name}", shape, dt))

        def sem(name):
            return c.semaphore(f"w_{name}")

        RING = 14
        c.open_ring(es, 7)
        pool_t = sb("pool", [P, 8 * UNIT])

        def unit(i, n=1):
            t, i = (c.ring, i) if i < RING else (pool_t, i - RING)
            return t[:, i * UNIT:(i + n) * UNIT]

        def feat(i):
            return unit(i).rearrange("p (k t) -> p k t", k=KC)

        def tok(i):
            return unit(i).rearrange("p (c n) -> p c n", c=TC)

        xn, xx, xs = tok(14), feat(15), [feat(16), feat(14)]
        r, k, v, a, sig, g = feat(12), feat(13), tok(17), feat(18), feat(19), tok(20)
        w_rkv_sb = [unit(4 * i, 4).rearrange("p (k n) -> p k n", k=KC) for i in range(3)]
        lora = unit(12, 2)
        w_la = lora[:, 0:512].rearrange("p (k n) -> p k n", k=KC)
        a_la = lora[:, 512:1024].rearrange("p (k n) -> p k n", k=KC)
        g_la = lora[:, 1024:2048].rearrange("p (k n) -> p k n", k=KC)
        wa_lb = lora[:, 2048:3072]
        g_lb = lora[:, 3072:4096]
        hid = sb("hid", [P, 2, T])
        head_of = sb("head_of", [P, RP, RH])
        head_to = sb("head_to", [RH, RP, P])
        bonus = sb("bonus", [P, TC, RH])
        last_w = sb("last_w", [P, RP, NCH])
        moments = sb("moments", [P, 2, RH])

        norm = Norm(c, es, "rwkv_norm", "n_mix1", xn)
        w_in = [sem(f"in{i}") for i in range(3)]
        lora_in, sel_in = sem("lora_in"), sem("sel_in")
        mixed, mix_used = sem("mixed"), sem("mix_used")
        p_done, took_a, took_v = sem("p_done"), sem("took_a"), sem("took_v")
        ORDER = (MIX_W, MIX_A, MIX_G, MIX_R, MIX_K, MIX_V)

        ar = unit(0, 2).rearrange("p (k f t) -> p k f t", k=KC, f=2)
        bT, kT = feat(2), feat(3)
        kk, run, w_run, tmp, keep = (feat(i) for i in (4, 5, 6, 7, 21))
        norms = sb("norms", [RH, 3, T])
        mask = sb("mask", [P, 4 * P])
        mask_in, scan_ready = sem("mask_in"), sem("scan_ready")
        kk_squared, ss_done, inv_ready, inv_spread = (sem(n) for n in (
            "kk_squared", "ss_done", "inv_ready", "inv_spread"))
        run_ready, run_excl, w_incl, w_used = (sem(n) for n in ("run_ready", "run_excl", "w_incl", "w_used"))
        prod_ready, bonus_done, spread_read = sem("prod_ready"), sem("bonus_done"), sem("spread_read")
        SS_B = SPREAD_B = 3

        def flat(x):
            return x.rearrange("p k t -> p (k t)")

        with nc.Block() as block:
            @block.sync
            def _(sp):
                for dst, name in ((w_la, "w_la"), (a_la, "a_la"), (g_la, "g_la")):
                    sp.dma_start(dst, d[name].rearrange("(k p) n -> p k n", p=P)).then_inc(lora_in, 16)
                sp.dma_start(wa_lb[0:LORA, :], d["w_lb"]).then_inc(lora_in, 16)
                sp.dma_start(wa_lb[LORA:P, :], d["a_lb"]).then_inc(lora_in, 16)
                sp.dma_start(g_lb, d["g_lb"]).then_inc(lora_in, 16)
                for i in range(3):
                    sp.dma_start(w_rkv_sb[i], d["w_rkv"][i * D:(i + 1) * D, :].rearrange(
                        "(k p) n -> p k n", p=P)).then_inc(w_in[i], 16)
                sp.dma_start(head_of[:, :, :].rearrange("p c h -> p (c h)"), d["head_of"]).then_inc(sel_in, 16)
                sp.dma_start(head_to[:, :, :].rearrange("p c h -> p (c h)"), d["head_to"]).then_inc(sel_in, 16)
                sp.dma_start(mask[:, :], d["chunk_mask"]).then_inc(mask_in, 16)
                sp.wait_ge(mask_in, 16)

            @block.gpsimd
            def _(pool):
                nc.gpsimd.memset(keep, 1.0).then_inc(scan_ready, 1)
                pool.wait_ge(scan_ready, 1)
                nc.gpsimd.memset(flat(keep).rearrange("p (n t) -> p n t", t=CH)[:, :, 0:1], 0.0).then_inc(scan_ready, 1)

            TAKER = "AVA" + "AAAA" + "AAAA" + "VVVV" + "AVAV" + "AVAV" + "AAAA"

            def taken(eng, n):
                if n >= 0:
                    eng.wait_ge(took_a, TAKER[:n + 1].count("A"))
                    if TAKER[:n + 1].count("V"):
                        eng.wait_ge(took_v, TAKER[:n + 1].count("V"))

            @block.tensor
            def _(pe):
                norm.pe_turn(pe)
                norm.wait(pe)

                def bank(n):
                    return c.banks[:, n % 8, :]

                def start(n):
                    taken(pe, n - 8)

                def between_v(b):
                    if b == 1:
                        taken(pe, 22)
                        pe.wait_ge(sel_in, 32)
                        pe.wait_ge(kk_squared, 1)
                        matmuls(nc, c.banks[0:RH, SS_B, 0:T], [head_of[:, q, :] for q in range(KC)],
                                [tmp[:, q, :] for q in range(KC)]).then_inc(ss_done, 1)
                    if b == 2:
                        pe.wait_ge(inv_ready, 1)
                        for q in range(KC):
                            ins = nc.tensor.matmul(c.banks[:, SPREAD_B + q // 2, (q % 2) * T:(q % 2 + 1) * T],
                                                   head_to[:, q, :], norms[:, 0, :], start=True, stop=True)
                            if q % 2:
                                ins.then_inc(inv_spread, 1)

                pe.wait_ge(lora_in, 96)
                for n, (first, lo, width) in enumerate(((w_la, 0, LORA), (a_la, LORA, LORA), (g_la, 0, P))):
                    pe.wait_ge(mixed, n + 1)
                    start(n)
                    ins = matmuls(nc, bank(n)[lo:lo + width, 0:T], [first[:, q, :] for q in range(KC)],
                                  [xs[n % 2][:, q, :] for q in range(KC)])
                    ins.then_inc(p_done, 1)
                for n0, lo in ((3, 0), (7, LORA)):
                    taken(pe, 1)
                    for b in range(4):
                        start(n0 + b)
                        for i in range(2):
                            f = 2 * b + i
                            ins = nc.tensor.matmul(bank(n0 + b)[:, i * T:(i + 1) * T],
                                                   wa_lb[lo:lo + LORA, f * P:(f + 1) * P],
                                                   hid[lo:lo + LORA, 0, :], start=True, stop=True)
                        ins.then_inc(p_done, 1)
                taken(pe, 2)
                for i in range(2 * TC):
                    start(11 + i)
                    nc.tensor.matmul(bank(11 + i), hid[:, 1, (i // 2) * P:(i // 2 + 1) * P],
                                     g_lb[:, (i % 2) * BANK:(i % 2 + 1) * BANK], start=True,
                                     stop=True).then_inc(p_done, 1)
                for m in range(3):
                    pe.wait_ge(w_in[m], 16)
                    pe.wait_ge(mixed, 4 + m)
                    src, w = xs[(3 + m) % 2], w_rkv_sb[m]
                    for b in range(4):
                        n = 15 + 4 * m + b
                        start(n)
                        if m < 2:
                            for i in range(2):
                                f = 2 * b + i
                                ins = matmuls(nc, bank(n)[:, i * T:(i + 1) * T],
                                              [w[:, q, f * P:(f + 1) * P] for q in range(KC)],
                                              [src[:, q, :] for q in range(KC)])
                        else:
                            between_v(b)
                            ins = matmuls(nc, bank(n), [src[:, q, (b // 2) * P:(b // 2 + 1) * P] for q in range(KC)],
                                          [w[:, q, (b % 2) * BANK:(b % 2 + 1) * BANK] for q in range(KC)])
                        ins.then_inc(p_done, 1)
                pe.wait_ge(prod_ready, 1)
                pe.wait_ge(spread_read, 1)
                for tc in range(TC):
                    ins = matmuls(nc, c.banks[:, SS_B, tc * RH:(tc + 1) * RH],
                                  [tmp[:, q, tc * P:(tc + 1) * P] for q in range(KC)],
                                  [head_of[:, q, :] for q in range(KC)])
                ins.then_inc(bonus_done, 1)

            def two(dst, b):
                return dst[:, 2 * b:2 * b + 2, :].rearrange("p a b -> p (a b)")

            def half_row(dst, i):
                return dst[:, i // 2, (i % 2) * BANK:(i % 2 + 1) * BANK]

            def take(eng, who, n, copy):
                m, b = divmod(n - 15, 4)
                dst = two((r, k)[m], b) if m < 2 else half_row(v, b)
                copy(dst, c.banks[:, n % 8, :])

            @block.scalar
            def _(act):
                norm.act_take(act)
                bank = [c.banks[:, i, :] for i in range(8)]
                act.wait_ge(p_done, 1)
                nc.scalar.activation(hid[0:LORA, 0, :], bank[0][0:LORA, 0:T], ACT.Tanh).then_inc(took_a, 1)
                act.wait_ge(p_done, 3)
                nc.scalar.activation(hid[:, 1, :], bank[2][:, 0:T], ACT.Sigmoid).then_inc(took_a, 1)
                for n0, dst, bias in ((3, sig, "w0"), (7, a, "a0")):
                    for b in range(4):
                        act.wait_ge(p_done, n0 + b + 1)
                        for i in range(2):
                            f = 2 * b + i
                            ins = nc.scalar.activation(dst[:, f, :], bank[(n0 + b) % 8][:, i * T:(i + 1) * T],
                                                       ACT.Sigmoid, bias=c.col(bias, f))
                        ins.then_inc(took_a, 1)
                for n in range(15, 27):
                    if n == 23:
                        act.wait_ge(run_ready, 1)
                        nc.scalar.activation(w_run, run, ACT.Exp, scale=-DECAY).then_inc(w_incl, 1)
                        act.wait_ge(run_ready, 2)
                        nc.scalar.activation(w_run, run, ACT.Exp, scale=DECAY).then_inc(w_incl, 1)
                        act.wait_ge(run_excl, 1)
                        nc.scalar.activation(w_run, sig, ACT.Exp, scale=-DECAY).then_inc(w_incl, 1)
                    if TAKER[n] == "A":
                        act.wait_ge(p_done, n + 1)
                        take(act, "A", n, lambda o, i: nc.scalar.activation(o, i, ACT.Copy).then_inc(took_a, 1))

            @block.vector
            def _(dve):
                chain, vec = c.dve_chain, nc.vector
                norm.dve_scales(dve)
                norm.dve_take(dve)
                dve.wait_ge(norm.by_act, 4)
                dve.wait_ge(norm.by_dve, 4)
                vec.tensor_tensor(xx[:, :, 1:T], c.xT[:, :, 0:T - 1], c.xT[:, :, 1:T], ALU.subtract)
                chain(dve, vec.tensor_scalar(xx[:, :, 0:1], c.xT[:, :, 0:1], -1.0, None, ALU.mult))

                def mix(n):
                    if n >= 2:
                        dve.wait_ge(p_done, (1, 2, 3, 19)[n - 2])
                    for q in range(KC):
                        ins = vec.scalar_tensor_tensor(xs[n % 2][:, q, :], xx[:, q, :],
                                                       c.col("mu", ORDER[n] * KC + q), c.xT[:, q, :],
                                                       ALU.mult, ALU.add)
                    ins.then_inc(mixed, 1)

                mix(0)
                mix(1)
                mix(2)
                dve.wait_ge(p_done, 2)
                vec.tensor_copy(hid[LORA:P, 0, :], c.banks[LORA:P, 1, 0:T]).then_inc(took_v, 1)
                mix(3)
                mix(4)
                for i in range(4):
                    dve.wait_ge(p_done, 12 + i)
                    vec.tensor_copy(half_row(g, i), c.banks[:, (11 + i) % 8, :]).then_inc(took_v, 1)
                for n in range(15, 27):
                    if n == 21:
                        mix(5)
                    if TAKER[n] == "V":
                        dve.wait_ge(p_done, n + 1)
                        take(dve, "V", n, lambda o, i: vec.tensor_copy(o, i).then_inc(took_v, 1))
                taken(dve, 22)
                dve.wait_ge(p_done, 23)
                for q in range(KC):
                    vec.tensor_scalar(kk[:, q, :], k[:, q, :], c.col("k_k", q), None, ALU.mult)
                dve.drain()
                vec.tensor_tensor(tmp, kk, kk, ALU.mult).then_inc(kk_squared, 1)
                dve.wait_ge(scan_ready, 2)
                vec.tensor_tensor_scan(flat(run), flat(keep), flat(sig), 0.0, ALU.mult, ALU.add).then_inc(run_ready, 1)
                dve.wait_ge(ss_done, 1)
                ss = norms[:, 0, :]
                c.dve_rstd(dve, vec.tensor_scalar(ss, c.banks[0:RH, SS_B, 0:T], 1e-24, None, ALU.max), ss,
                           (norms[:, 1, :], norms[:, 2, :]))
                dve.nop().then_inc(inv_ready, 1)
                for q in range(KC):
                    vec.tensor_scalar(tmp[:, q, :], a[:, q, :], -1.0, c.col("k_a", q), ALU.add, ALU.mult)
                dve.drain()
                chain(dve, vec.scalar_tensor_tensor(flat(k), flat(tmp), 1.0, flat(k), ALU.add, ALU.mult))
                for q in range(KC):
                    last = vec.scalar_tensor_tensor(tmp[:, q, :], r[:, q, :], c.col("r_k", q), k[:, q, :], ALU.mult,
                                                    ALU.mult)
                last.then_inc(prod_ready, 1)
                for b in range(4):
                    dve.wait_ge(inv_spread, b + 1)
                    s = kk[:, 2 * b:2 * b + 2, :].rearrange("p a b -> p (a b)")
                    last = vec.tensor_tensor(s, s, c.banks[:, SPREAD_B + b, :], ALU.mult)
                last.then_inc(spread_read, 1)
                dve.wait_ge(spread_read, 1)
                dve.wait_ge(w_incl, 1)
                vec.tensor_tensor(ar[:, :, 1, :], r, w_run, ALU.mult)
                vec.tensor_copy(last_w[:, :, :], w_run.rearrange("p k (n t) -> p k n t", t=CH)[:, :, :, CH - 1])
                chain(dve, vec.tensor_tensor(sig, run, sig, ALU.subtract))
                dve.nop().then_inc(run_ready, 1)
                dve.wait_ge(w_incl, 2)
                vec.tensor_tensor(kT, k, w_run, ALU.mult)
                chain(dve, vec.tensor_tensor(a, kk, a, ALU.mult))
                chain(dve, vec.tensor_tensor(bT, a, w_run, ALU.mult))
                dve.nop().then_inc(run_excl, 1)
                dve.wait_ge(w_incl, 3)
                vec.scalar_tensor_tensor(ar[:, :, 0, :], kk, -1.0, w_run, ALU.mult, ALU.mult)
                dve.wait_ge(bonus_done, 1)
                vec.tensor_copy(bonus[:, :, :].rearrange("p c h -> p (c h)"), c.banks[:, SS_B, 0:TC * RH])


        G_AB, G_QB, G_AK, G_QK = range(4)
        gram = unit(4, 8).rearrange("p (c h n) -> p c h n", c=TC, h=RH)
        inv = unit(12, 2).rearrange("p (c h t) -> p c h t", c=TC, h=RH)
        tokA, tokB, tokK = tok(16), tok(18), tok(19)
        P_T, akv, u, sa = c.xT[:, :, :], tok(21), tok(14), tok(21)
        sys_a = unit(14)[:, 0:1024].rearrange("p (s t) -> p s t", s=CH)
        sys_x = unit(14)[:, 1024:2048].rearrange("p (s t) -> p s t", s=CH)
        work = unit(15)[:, 0:1024]
        dram_a = nc.dram_tensor("chunk_a", (J, TC * RH, CH, CH), F32, kind="Internal").ap()
        dram_x = nc.dram_tensor("chunk_x", (J, TC * RH, CH, CH), F32, kind="Internal").ap()
        ab_done, ab_ready, gram_done, gram_taken, gram_ready = (sem(n) for n in (
            "ab_done", "ab_ready", "gram_done", "gram_taken", "gram_ready"))
        a_out, a_back, x_out, x_back, inv_zero, sys_zero, solved = (sem(n) for n in (
            "a_out", "a_back", "x_out", "x_back", "inv_zero", "sys_zero", "solved"))
        tok_done, tok_act = sem("tok_done"), sem("tok_act")
        akv_done, akv_act, pt_done, pt_act, u_done, u_act = (sem(n) for n in (
            "akv_done", "akv_act", "pt_done", "pt_act", "u_done", "u_act"))

        def part(h):
            return slice(HD * (h % 2), HD * (h % 2) + HD)

        def at_head(h):
            return slice(h * HD, (h + 1) * HD)

        with nc.Block() as block:
            @block.sync
            def _(sp):
                sp.wait_ge(ab_ready, TC * RH // 4)
                for j in range(J):
                    s = slice(CH * j, CH * (j + 1))
                    src = gram[s, :, :, G_AB * P + CH * j:G_AB * P + CH * (j + 1)].rearrange("s c h t -> s (c h) t")
                    sp.dma_start(dram_a[j].rearrange("n s t -> s n t"), src).then_inc(a_out, 16)
                sp.wait_ge(a_out, 16 * J)
                sp.dma_start(sys_a, dram_a.rearrange("j n s t -> (j n) s t")).then_inc(a_back, 16)
                sp.wait_ge(solved, 1)
                sp.dma_start(dram_x.rearrange("j n s t -> (j n) s t"), sys_x).then_inc(x_out, 16)
                sp.wait_ge(x_out, 16)
                sp.wait_ge(inv_zero, 1)
                for j in range(J):
                    s = slice(CH * j, CH * (j + 1))
                    dst = inv[s, :, :, CH * j:CH * (j + 1)].rearrange("s c h t -> s (c h) t")
                    sp.dma_start(dst, dram_x[j].rearrange("n s t -> s n t")).then_inc(x_back, 16)

            @block.gpsimd
            def _(pool):
                nc.gpsimd.memset(unit(14)[:, 1024:2048], 0.0).then_inc(sys_zero, 1)
                pool.wait_ge(sys_zero, 1)
                nc.gpsimd.memset(unit(14)[:, 1024:2048:CH + 1], 1.0).then_inc(sys_zero, 1)
                nc.gpsimd.memset(unit(12, 2), 0.0).then_inc(inv_zero, 1)
                for n in range(TC * RH):
                    tc, h = divmod(n, RH)
                    pool.wait_ge(gram_taken, n + 1)
                    nc.gpsimd.tensor_tensor(gram[:, tc, h, P:4 * P], gram[:, tc, h, P:4 * P], mask[:, P:4 * P],
                                            ALU.mult).then_inc(gram_ready, 1)

            @block.tensor
            def _(pe):
                for n in range(TC * RH // 8):
                    if n >= 2:
                        pe.wait_ge(ab_ready, 2 * n - 2)
                    tc, h0 = n // (RH // 8), n % (RH // 8) * 8
                    t = slice(tc * P, (tc + 1) * P)
                    for i in range(8):
                        h = h0 + i
                        ins = nc.tensor.matmul(c.banks[:, 2 * n % 4 + i % 2, (i // 2) * P:(i // 2 + 1) * P],
                                               bT[part(h), h // 2, t], ar[part(h), h // 2, 0, t], start=True, stop=True)
                        if i >= 6:
                            ins.then_inc(ab_done, 1)
                for n in range(TC * RH):
                    if n < 4:
                        pe.wait_ge(ab_ready, TC * RH // 4 - 3 + n)
                    else:
                        pe.wait_ge(gram_taken, n - 3)
                    tc, h = divmod(n, RH)
                    p, t, out = h // 2, slice(tc * P, (tc + 1) * P), c.banks[:, n % 4, :]
                    nc.tensor.matmul(out[:, G_QB * P:(G_QB + 1) * P], bT[part(h), p, t], ar[part(h), p, 1, t],
                                     start=True, stop=True)
                    nc.tensor.matmul(out[:, G_AK * P:4 * P], kT[part(h), p, t], ar[part(h), p, :, t], start=True,
                                     stop=True).then_inc(gram_done, 1)
                n = 0
                for src in (ar[:, :, 0, :], bT, kT):
                    for tc in range(TC):
                        for q in range(2):
                            if n >= 2:
                                pe.wait_ge(tok_act, n - 1)
                            for i in range(4):
                                ins = nc.tensor.transpose(c.banks[:, 4 + n % 2, i * P:(i + 1) * P],
                                                          src[:, 4 * q + i, tc * P:(tc + 1) * P], c.ident[:, :])
                            ins.then_inc(tok_done, 1)
                            n += 1
                pe.wait_ge(gram_ready, TC * RH)
                for tc in range(TC):
                    for q in range(2):
                        for i in range(8):
                            h = 8 * q + i
                            ins = nc.tensor.matmul(c.banks[:, 2 * tc + q, i * HD:(i + 1) * HD],
                                                   gram[:, tc, h, G_AK * P:(G_AK + 1) * P], v[:, tc, at_head(h)],
                                                   start=True, stop=True)
                        ins.then_inc(akv_done, 1)
                pe.wait_ge(x_back, 16 * J)
                pe.wait_ge(tok_act, 12)
                for p in range(RP):
                    for s in range(2):
                        h = 2 * p + s
                        for tc in range(TC):
                            o = (p % 2) * T + tc * P
                            ins = nc.tensor.matmul(c.banks[part(h), 4 + p // 2, o:o + P], tokA[:, tc, at_head(h)],
                                                   inv[:, tc, h, :], start=True, stop=True)
                    if p % 2:
                        ins.then_inc(pt_done, 1)
                for tc in range(TC):
                    for q in range(2):
                        pe.wait_ge(akv_act, 2 * tc + q + 1)
                        for i in range(8):
                            h = 8 * q + i
                            ins = nc.tensor.matmul(c.banks[:, 2 * tc + q, i * HD:(i + 1) * HD],
                                                   inv[:, tc, h, :], akv[:, tc, at_head(h)],
                                                   start=True, stop=True)
                        ins.then_inc(u_done, 1)

            @block.scalar
            def _(act):
                for n in range(TC * RH):
                    act.wait_ge(gram_done, n + 1)
                    nc.scalar.activation(gram[:, n // RH, n % RH, P:4 * P], c.banks[:, n % 4, P:4 * P],
                                         ACT.Copy).then_inc(gram_taken, 1)
                n = 0
                for dst in (tokA, tokB, tokK):
                    for tc in range(TC):
                        for q in range(2):
                            act.wait_ge(tok_done, n + 1)
                            nc.scalar.activation(dst[:, tc, q * BANK:(q + 1) * BANK], c.banks[:, 4 + n % 2, :],
                                                 ACT.Copy).then_inc(tok_act, 1)
                            n += 1
                for done, dst, ready in ((akv_done, akv, akv_act), (pt_done, None, pt_act), (u_done, u, u_act)):
                    for i in range(4):
                        act.wait_ge(done, i + 1)
                        if dst is None:
                            nc.scalar.activation(two(P_T, i), c.banks[:, 4 + i, :], ACT.Copy).then_inc(ready, 1)
                        else:
                            nc.scalar.activation(half_row(dst, i), c.banks[:, i, :], ACT.Copy).then_inc(ready, 1)

            @block.vector
            def _(dve):
                vec = nc.vector
                for n in range(TC * RH // 4):
                    dve.wait_ge(ab_done, n + 1)
                    tc, h0 = n // 4, n // 2 % 2 * 8 + n % 2
                    vec.tensor_tensor(gram[:, tc, h0:h0 + 7:2, G_AB * P:(G_AB + 1) * P],
                                      c.banks[:, n % 4, :].rearrange("p (h t) -> p h t", h=4),
                                      mask[:, 0:P].unsqueeze(1).to_broadcast([P, 4, P]), ALU.mult).then_inc(ab_ready, 1)
                dve.wait_ge(a_back, 16)
                dve.wait_ge(sys_zero, 2)
                for t in range(1, CH):
                    w = work[:, 0:t * t].rearrange("p (j s) -> p j s", j=t)
                    c.dve_chain(dve, vec.tensor_tensor(w, sys_x[:, 0:t, 0:t],
                                                       sys_a[:, 0:t, t].unsqueeze(1).to_broadcast([P, t, t]),
                                                       ALU.mult))
                    c.dve_chain(dve, vec.tensor_reduce(sys_x[:, 0:t, t], w, AX.X, ALU.add))
                dve.nop().then_inc(solved, 1)

        states = unit(15, 2).rearrange("p (n f) -> p n f", n=NCH)
        grown = mask
        sa_done, sa_ready, s_done, s_ready, s_zero = (sem(n) for n in (
            "sa_done", "sa_ready", "s_done", "s_ready", "s_zero"))
        y_done, y_out, yT_done, yT_act, o_done = (sem(n) for n in (
            "y_done", "y_out", "yT_done", "yT_act", "o_done"))
        w_o = [unit(i, 2).rearrange("p (k n) -> p k n", k=4) for i in (2, 12)]
        o_in = [sem(f"o_in{i}") for i in range(2)]
        rows_in = sem("rows_in")
        ln_g, ln_b = ar[:, 0:KC // 2, 0, :], ar[:, KC // 2:KC, 0, :]
        addend = [gram[:, tc, :, G_AB * P:G_AB * P + HD] for tc in range(TC)]
        centred = [gram[:, tc, :, G_AB * P + HD:(G_AB + 1) * P] for tc in range(TC)]
        y_squared = [gram[:, tc, :, G_AK * P:G_AK * P + HD] for tc in range(TC)]
        addend_ready = sem("addend_ready")
        y_tok, yT = tok(18), P_T
        SA_B, ST_B, Y_B = 0, 2, 4

        def split_heads(x):
            return x.rearrange("p (q s n) -> p s q n", s=2, n=HD)

        with nc.Block() as block:
            @block.sync
            def _(sp):
                for dst, name in ((ln_g, "rln_g"), (ln_b, "rln_b")):
                    sp.dma_start(dst, c.row(name).rearrange("o (k t) -> o k t", t=T).to_broadcast(
                        [P, KC // 2, T])).then_inc(rows_in, 16)
                w = d["w_o"].rearrange("(k p) n -> p k n", p=P)
                for i in range(2):
                    sp.dma_start(w_o[i], w[:, 4 * i:4 * i + 4, :]).then_inc(o_in[i], 16)

            @block.gpsimd
            def _(pool):
                nc.gpsimd.memset(states[:, 0, :], 0.0).then_inc(s_zero, 1)
                pool.wait_ge(rows_in, 32)

                def like_rows(x):
                    return x.rearrange("p (k i) n -> p k i n", i=4)

                def by_head(row):
                    return row.rearrange("p k (i n) -> p k i n", n=HD)

                for tc in range(TC):
                    v3, g3 = (x[:, tc, :].rearrange("p (h n) -> p h n", h=RH) for x in (v, g))
                    nc.gpsimd.tensor_tensor(addend[tc], v3, bonus[:, tc, :].unsqueeze(2).to_broadcast([P, RH, HD]),
                                            ALU.mult)
                    pool.drain()
                    nc.gpsimd.tensor_tensor(like_rows(addend[tc]), like_rows(addend[tc]), by_head(ln_b), ALU.add)
                    pool.drain()
                    nc.gpsimd.tensor_tensor(addend[tc], addend[tc], g3, ALU.mult)
                    pool.drain()
                    nc.gpsimd.tensor_tensor(like_rows(g3), like_rows(g3), by_head(ln_g), ALU.mult).then_inc(
                        addend_ready, 1)

            @block.tensor
            def _(pe):
                def outcome(i, pairs):
                    tc = i // 2
                    outs = [(2 * m + i % 2, c.banks[:, Y_B + i, m * HD:(m + 1) * HD]) for m in pairs]
                    for h, out in outs:
                        nc.tensor.matmul(out, gram[:, tc, h, G_QK * P:(G_QK + 1) * P], v[:, tc, at_head(h)],
                                         start=h < 2, stop=False, skip_group_check=True)
                    for h, out in outs:
                        nc.tensor.matmul(out, gram[:, tc, h, G_QB * P:(G_QB + 1) * P], sa[:, tc, at_head(h)],
                                         start=False, stop=False, skip_group_check=True)
                    for h, out in outs:
                        for j in range(J):
                            n = tc * J + j
                            ins = nc.tensor.matmul(out[CH * j:CH * (j + 1), :],
                                                   ar[part(h), h // 2, 1, n * CH:(n + 1) * CH],
                                                   states[part(h), n, (h // 2) * HD:(h // 2 + 1) * HD],
                                                   start=False, stop=True, skip_group_check=True)
                    if RP - 1 in pairs:
                        ins.then_inc(y_done, 1)

                fill = {(J, 0): (0, range(0, 3)), (J, 1): (0, range(3, 5)), (J + 1, 0): (0, range(5, 8)),
                        (J + 1, 1): (1, range(0, 2)), (J + 2, 0): (1, range(2, 5)), (J + 2, 1): (1, range(5, 8))}
                pe.wait_ge(s_zero, 1)
                for n in range(NCH):
                    tc, j = divmod(n, J)
                    rows, cols = slice(CH * j, CH * (j + 1)), slice(n * CH, (n + 1) * CH)
                    pe.wait_ge(s_ready, n)
                    for s in range(2):
                        for p in range(RP):
                            ins = nc.tensor.matmul(c.banks[rows, SA_B + s, p * HD:(p + 1) * HD],
                                                   P_T[part(s), p, cols],
                                                   states[part(s), n, p * HD:(p + 1) * HD], start=True, stop=True)
                    ins.then_inc(sa_done, 1)
                    if n == NCH - 1:
                        break
                    for h in range(RH):
                        nc.tensor.matmul(c.banks[part(h), ST_B, (h // 2) * HD:(h // 2 + 1) * HD],
                                         tokK[rows, tc, at_head(h)], v[rows, tc, at_head(h)],
                                         start=h < 2, stop=False, skip_group_check=True)
                    if (n, 0) in fill:
                        outcome(*fill[n, 0])
                    pe.wait_ge(sa_ready, 2 * (n + 1))
                    for h in range(RH):
                        ins = nc.tensor.matmul(c.banks[part(h), ST_B, (h // 2) * HD:(h // 2 + 1) * HD],
                                               tokB[rows, tc, at_head(h)], sa[rows, tc, at_head(h)],
                                               start=False, stop=True, skip_group_check=True)
                    ins.then_inc(s_done, 1)
                    if (n, 1) in fill:
                        outcome(*fill[n, 1])
                pe.wait_ge(sa_ready, 2 * NCH)
                for i in range(2, 4):
                    outcome(i, range(RP))
                for i in range(2):
                    pe.wait_ge(o_in[i], 16)
                for tc in range(TC):
                    pe.wait_ge(y_out, tc + 1)
                    for q in range(KC):
                        ins = nc.tensor.transpose(c.banks[:, 2 * tc + q // 4, (q % 4) * P:(q % 4 + 1) * P],
                                                  y_tok[:, tc, q * P:(q + 1) * P], c.ident[:, :])
                        if q % 4 == 3:
                            ins.then_inc(yT_done, 1)
                    pe.wait_ge(yT_act, 2 * tc + 2)
                    for i in range(2):
                        matmuls(nc, c.banks[:, Y_B + 2 * tc + i, :],
                                [yT[:, q, tc * P:(tc + 1) * P] for q in range(KC)],
                                [w_o[q // 4][:, q % 4, i * BANK:(i + 1) * BANK] for q in range(KC)]).then_inc(
                                    o_done, 1)

            @block.scalar
            def _(act):
                for i in range(4):
                    act.wait_ge(yT_done, i + 1)
                    tc, q = i // 2, 4 * (i % 2)
                    nc.scalar.activation(yT[:, q:q + 4, tc * P:(tc + 1) * P],
                                         c.banks[:, i, :].rearrange("p (q t) -> p q t", q=4), ACT.Copy).then_inc(
                                             yT_act, 1)

            @block.vector
            def _(dve):
                chain, vec = c.dve_chain, nc.vector
                for n in range(NCH):
                    tc, j = divmod(n, J)
                    rows = slice(CH * j, CH * (j + 1))
                    dve.wait_ge(sa_done, n + 1)
                    for s in range(2):
                        vec.tensor_tensor(split_heads(sa[rows, tc, :])[:, s, :, :],
                                          c.banks[rows, SA_B + s, :].rearrange("p (q n) -> p q n", n=HD),
                                          split_heads(u[rows, tc, :])[:, s, :, :], ALU.add).then_inc(sa_ready, 1)
                    if n == NCH - 1:
                        break
                    dve.wait_ge(s_done, n + 1)
                    chain(dve, vec.tensor_tensor(grown[:, :], c.banks[:, ST_B, :], states[:, n, :], ALU.add))
                    vec.tensor_tensor(states[:, n + 1, :].rearrange("p (q n) -> p q n", n=HD),
                                      grown[:, :].rearrange("p (q n) -> p q n", n=HD),
                                      last_w[:, :, n:n + 1].to_broadcast([P, RP, HD]), ALU.mult).then_inc(s_ready, 1)
                    dve.wait_ge(s_ready, n + 1)
                for tc in range(TC):
                    mu, var = moments[:, 0, :], moments[:, 1, :]
                    y3, t3 = centred[tc], y_squared[tc]
                    for i in range(2):
                        dve.wait_ge(y_done, 2 * tc + i + 1)
                        last = vec.tensor_reduce(mu[:, i:RH:2], c.banks[:, Y_B + 2 * tc + i, :].rearrange(
                            "p (h n) -> p h n", n=HD), AX.X, ALU.add)
                    chain(dve, last)
                    chain(dve, vec.tensor_scalar(mu, mu, 1.0 / HD, None, ALU.mult))
                    for i in range(2):
                        hs = slice(i, RH, 2)
                        last = vec.tensor_tensor(y3[:, hs, :], c.banks[:, Y_B + 2 * tc + i, :].rearrange(
                            "p (h n) -> p h n", n=HD), mu[:, hs].unsqueeze(2).to_broadcast([P, 8, HD]), ALU.subtract)
                    chain(dve, last)
                    chain(dve, vec.tensor_tensor(t3, y3, y3, ALU.mult))
                    chain(dve, vec.tensor_reduce(var, t3, AX.X, ALU.add))
                    c.dve_rstd(dve, vec.tensor_scalar(var, var, 1.0 / HD, GN_EPS, ALU.mult, ALU.add), var)
                    chain(dve, vec.tensor_tensor(y3, y3, var.unsqueeze(2).to_broadcast([P, RH, HD]), ALU.mult))
                    dve.wait_ge(addend_ready, tc + 1)
                    chain(dve, vec.tensor_tensor(y3, y3, g[:, tc, :].rearrange("p (h n) -> p h n", h=RH), ALU.mult))
                    vec.tensor_tensor(y_tok[:, tc, :].rearrange("p (h n) -> p h n", h=RH), y3, addend[tc],
                                      ALU.add).then_inc(y_out, 1)
                for i in range(2 * TC):
                    dve.wait_ge(o_done, i + 1)
                    s = c.x[:, i // 2, (i % 2) * BANK:(i % 2 + 1) * BANK]
                    vec.tensor_tensor(s, s, c.banks[:, Y_B + i, :], ALU.add)


STAGES = [mixer_stage, expert_stage, embedding_stage, gating_stage, lambda c: ffn_stage(c, 0), rwkv_stage,
          lambda c: ffn_stage(c, 1)]


def finish_stage(c):
    nc, d = c.nc, c.dram
    with ExitStack() as es:
        gain = es.enter_context(nc.sbuf_tensor("final_gain", [P, D], F32))
        y = es.enter_context(nc.sbuf_tensor("y_out", [P, TC, D], F32))
        gain_in = c.semaphore("gain_in")
        y_ready = c.semaphore("y_ready")
        stored = c.semaphore("stored")
        out = c.out.rearrange("b (c p) n -> p (b c) n", p=P)
        with nc.Block() as block:
            @block.sync
            def _(sp):
                sp.dma_start(gain[:, :], rows_to_all(c.row("final"))).then_inc(gain_in, 16)
                for tc in range(TC):
                    sp.wait_ge(y_ready, tc + 1)
                    sp.dma_start(out[:, tc, :], y[:, tc, :]).then_inc(stored, 16)
                sp.wait_ge(stored, 16 * TC)

            @block.vector
            def _(dve):
                chain, s = c.dve_chain, c.stat
                for tc in range(TC):
                    x = c.x[:, tc, :]
                    if not FINAL:
                        nc.vector.tensor_copy(y[:, tc, :], x).then_inc(y_ready, 1)
                        continue
                    chain(dve, nc.vector.tensor_tensor_reduce(y[:, tc, :], x, x, 1.0, 0.0, ALU.mult, ALU.add,
                                                              s[:, tc:tc + 1]))
                    c.dve_rstd(dve, nc.vector.tensor_scalar(s[:, tc:tc + 1], s[:, tc:tc + 1], 1.0 / D, EPS, ALU.mult,
                                                       ALU.add), s[:, tc:tc + 1])
                    dve.wait_ge(gain_in, 16)
                    nc.vector.scalar_tensor_tensor(y[:, tc, :], x, s[:, tc:tc + 1], gain[:, :], ALU.mult,
                                                   ALU.mult).then_inc(y_ready, 1)


FINAL = True


def program(nc, dram, out):
    with ExitStack() as ctx:
        core = Core(nc, dram, out, ctx)
        for stage in STAGES:
            stage(core)
            core.end_stage()
        finish_stage(core)


def shape_constants():
    i = np.arange(P)
    f32 = np.float32
    log_g = np.log(1.0 - 2.0 ** (-5.0 - np.arange(HEADS)))
    key = np.concatenate([i[:, None] + 0 * np.arange(T)[None], i[:, None] + P + 0 * i[None]], 1)
    query = np.concatenate([np.arange(T)[None] + 0 * i[:, None], P + i[None] + 0 * i[:, None]], 1)
    gap = query - key
    decay = np.stack([np.where(gap >= 0, np.exp(g * np.maximum(gap, 0)), 0.0) for g in log_g], 1)
    return {
        "ident": np.eye(P, dtype=f32),
        "decay": decay.reshape(P, -1).astype(f32),
        "sufsum": -(i[:, None] >= i[None]).astype(f32),
        "head_of": (np.arange(RH)[None, None] == (2 * np.arange(RH // 2)[None, :, None]
                                                  + i[:, None, None] // HD)).reshape(P, -1).astype(f32),
        "head_to": (np.arange(RH)[:, None, None] == (2 * np.arange(RH // 2)[None, :, None]
                                                     + i[None, None] // HD)).reshape(RH, -1).astype(f32),
        "chunk_mask": np.concatenate([(i[:, None] // CH == i[None] // CH) & before for before in (
            i[:, None] < i[None], i[:, None] <= i[None]) * 2], 1).astype(f32),
        "upto": (i[:, None] <= i[None]).astype(f32),
        "number": np.tile(np.tile(np.arange(T).reshape(BLOCKS, 1, CAP), (1, 2, 1)).reshape(1, -1), (P, 1)).astype(f32),
        "expert_no": np.tile(np.arange(EXPERTS), (P, 1)).astype(f32),
        "extra_col": np.stack([(i // EXPERTS + 1) * CAP, i % EXPERTS, i // EXPERTS + 1], 1).astype(f32),
        "work_list": np.concatenate([np.zeros(64), np.arange(EXPERTS), np.zeros(96)]).reshape(1, -1).astype(np.int32),
    }


def kernel(**a):
    from concourse import bacc
    from concourse.bass_utils import run_bass_kernel_spmd

    def col(v):
        return v.reshape(-1, P).T

    def row(v):
        return v.reshape(1, -1)

    cols = {"g_mix": a["g_mix_norm"], "g_ffn": a["g_ffn_norm"], "g_ple": a["g_ple_norm"],
            "n_mix0": a["norm_mix_g_2"][0], "n_mix1": a["norm_mix_g_2"][1],
            "n_ffn0": a["norm_ffn_g_2"][0], "n_ffn1": a["norm_ffn_g_2"][1],
            "b_u": a["sgu_b_in_2"][0, :SGU], "mu": a["rwkv_mu_2"], "w0": a["rwkv_w0_2"], "a0": a["rwkv_a0_2"],
            "k_k": a["rwkv_k_k_2"], "k_a": a["rwkv_k_a_2"], "r_k": a["rwkv_r_k_2"]}
    inv_freq = (10000.0 ** (-np.arange(HD // 2) / (HD // 2))).astype(np.float32)
    rows = {"sb_q": a["sb_q_gain"], "sb_k": a["sb_k_gain"], "ret_q": a["ret_q_gain"], "ret_k": a["ret_k_gain"],
            "gn_g": a["ret_gn_gain"], "gn_b": a["ret_gn_bias"], "b_router": a["b_router"], "inv_freq": inv_freq,
            "b_v": a["sgu_b_in_2"][0, SGU:], "ln_g": a["sgu_ln_g_2"], "ln_b": a["sgu_ln_b_2"],
            "b_s": a["sgu_b_s_2"], "final": a["final_norm_g_2"], "rln_g": a["rwkv_ln_g_2"],
            "rln_b": a["rwkv_ln_b_2"]}
    arrays = {
        "x": a["x"][0],
        "pT": a["p"][0, 0].T,
        "positions": a["positions"].reshape(TC, P).T,
        "cols": np.concatenate([col(cols[n]) for n in COLS], 1),
        "rows": np.concatenate([row(rows[n]) for n in ROWS], 1),
        "w_in": a["w_in"][0], "w_out": a["w_out"][0],
        "w_router": a["w_router"][0],
        "w_up": a["w_up_gate"].reshape(EXPERTS * D, 2 * D), "b_up": a["b_up_gate"][0],
        "w_down": a["w_down"].reshape(EXPERTS * D, D), "b_down": a["b_down"][0],
        "w_ple_gate": a["w_ple_gate"][0], "w_ple_proj": a["w_ple_proj"][0],
        "ffn_w1": a["ffn_w1_2"].reshape(2 * D, FF), "ffn_w2": a["ffn_w2_2"].reshape(2 * FF, D),
        "sgu_in": a["sgu_w_in_2"][0], "sgu_out": a["sgu_w_out_2"][0],
        "w_sT": a["sgu_w_s_2"][0].transpose(2, 0, 1).reshape(P, GROUPS * P),
        "w_rkv": a["rwkv_w_rkv_2"][0].reshape(3 * D, D), "w_o": a["rwkv_w_o_2"][0],
        "w_la": a["rwkv_w_lora_a_2"][0], "w_lb": a["rwkv_w_lora_b_2"][0],
        "a_la": a["rwkv_a_lora_a_2"][0], "a_lb": a["rwkv_a_lora_b_2"][0],
        "g_la": a["rwkv_g_lora_a_2"][0], "g_lb": a["rwkv_g_lora_b_2"][0],
    }
    arrays.update(shape_constants())
    arrays = {n: np.ascontiguousarray(v) for n, v in arrays.items()}
    nc = bacc.Bacc("TRN2", target_bir_lowering=False, num_devices=1)
    dram = {n: nc.dram_tensor(f"in_{n}", v.shape, mybir.dt.from_np(v.dtype), kind="ExternalInput").ap()
            for n, v in arrays.items()}
    out = nc.dram_tensor("out_y", (1, T, D), F32, kind="ExternalOutput").ap()
    program(nc, dram, out)
    r = run_bass_kernel_spmd(nc, [{f"in_{n}": v for n, v in arrays.items()}], core_ids=[0])
    return r.results[0]["out_y"]
```
